# Optimizing a Trainium2 kernel written in Bass

```python
import math
import jax, jax.numpy as jnp
from jax import lax
import numpy as np

D_MODEL = 1024
BATCH = 1
SEQ = 2048
DEPTH = 1

N_HEADS_ATTN = 8
HEAD_DIM = 64
ATTN_WIDTH = N_HEADS_ATTN * HEAD_DIM
DILATION_PATTERNS = ((128, 1), (512, 4), (2048, 16))
NUM_BUCKETS = 32
MAX_DISTANCE = 2048
SSM_WIDTH = D_MODEL // 2
SSM_GROUP = 16
SSM_GROUPS = SSM_WIDTH // SSM_GROUP
SSM_STATE = 64
DT_MIN = 1e-3
DT_MAX = 1e-1
IN_WIDTH = 3 * ATTN_WIDTH + SSM_WIDTH + 2 * D_MODEL
N_EXPERT_GROUPS = 4
EXPERTS_PER_GROUP = 8
N_EXPERTS = N_EXPERT_GROUPS * EXPERTS_PER_GROUP
TOP_K = 2
D_EXPERT = D_MODEL // 2
MOE_BLOCK = 128
RMS_EPS = 1e-6
NEG_INF = -1e30

kernel_name = 'hybrid_dilated_attn_s5_hmoe_block'

def rms_norm(x, gain):
    xf = x.astype(jnp.float32)
    y = xf * lax.rsqrt(jnp.mean(xf * xf, axis=-1, keepdims=True) + RMS_EPS)
    return (y * gain.astype(jnp.float32)).astype(x.dtype)

def t5_bucket(dist):
    exact = NUM_BUCKETS // 2
    d_f = jnp.maximum(dist, exact).astype(jnp.float32)
    large = exact + (jnp.log(d_f / exact) / math.log(MAX_DISTANCE / exact)
                     * (NUM_BUCKETS - exact)).astype(jnp.int32)
    return jnp.where(dist < exact, dist, jnp.minimum(large, NUM_BUCKETS - 1))

def dilated_band_attention(q, k, v, rel_bias, window, dil):
    bsz, seq, n_heads, head_dim = q.shape
    span = window // dil
    blk = span
    sub_len = -(-seq // (dil * blk)) * blk
    seq_pad = sub_len * dil
    n_blk = sub_len // blk
    pad = ((0, 0), (0, seq_pad - seq), (0, 0), (0, 0))

    def to_blocks(t):
        return jnp.pad(t, pad).reshape(bsz, n_blk, blk, dil, n_heads, head_dim)

    def with_prev(t):
        prev = jnp.pad(t[:, :-1], ((0, 0), (1, 0), (0, 0), (0, 0), (0, 0), (0, 0)))
        return jnp.concatenate([prev, t], axis=2)

    qb = to_blocks(q)
    kc = with_prev(to_blocks(k))
    vc = with_prev(to_blocks(v))
    qi = jnp.arange(blk)[:, None]
    ki = jnp.arange(2 * blk)[None, :]
    sub_dist = blk + qi - ki
    band = (sub_dist >= 0) & (sub_dist <= span)
    in_range = (jnp.arange(n_blk)[:, None, None] * blk + ki[None] - blk) >= 0
    mask = (band[None] & in_range)[None, :, None, None]
    bias = rel_bias.astype(jnp.float32)[t5_bucket(jnp.maximum(sub_dist, 0) * dil)]
    bias = jnp.transpose(bias, (2, 0, 1))
    s = jnp.einsum('bnqrhd,bnkrhd->bnrhqk', qb, kc) * head_dim ** -0.5 + bias
    s = jnp.where(mask, s, NEG_INF)
    m = jnp.max(s, axis=-1, keepdims=True)
    p = jnp.exp(s - m)
    l = jnp.sum(p, axis=-1)
    o = jnp.einsum('bnrhqk,bnkrhd->bnqrhd', p, vc) / jnp.transpose(l, (0, 1, 4, 2, 3))[..., None]
    lse = jnp.transpose(m[..., 0] + jnp.log(l), (0, 1, 4, 2, 3))
    o = o.reshape(bsz, seq_pad, n_heads, head_dim)[:, :seq]
    lse = lse.reshape(bsz, seq_pad, n_heads)[:, :seq]
    return o, lse

def dilated_mixture_attention(q, k, v, rel_bias):
    q, k, v = (t.astype(jnp.float32) for t in (q, k, v))
    outs, lses = [], []
    for window, dil in DILATION_PATTERNS:
        o, lse = dilated_band_attention(q, k, v, rel_bias, window, dil)
        outs.append(o)
        lses.append(lse)
    w = jax.nn.softmax(jnp.stack(lses), axis=0)
    return jnp.einsum('pbsh,pbshd->bshd', w, jnp.stack(outs))

def s5_mixer(u, a_re, a_im, log_dt, b_re, b_im, c_re, c_im, d_skip, w_glu, b_glu):
    bsz, seq, _ = u.shape
    f32 = jnp.float32
    ug = u.astype(f32).reshape(bsz, seq, SSM_GROUPS, SSM_GROUP)
    lam = lax.complex(a_re.astype(f32), a_im.astype(f32))
    dt = jnp.exp(log_dt.astype(f32))[:, None]
    a_bar = jnp.exp(lam * dt)
    b_bar = ((a_bar - 1.0) / lam)[..., None] * lax.complex(b_re.astype(f32), b_im.astype(f32))
    bu = jnp.einsum('bsgh,gph->bsgp', ug.astype(jnp.complex64), b_bar)
    a_seq = jnp.broadcast_to(a_bar, (1, seq) + a_bar.shape)

    def combine(e1, e2):
        a1, h1 = e1
        a2, h2 = e2
        return a1 * a2, a2 * h1 + h2

    _, states = lax.associative_scan(combine, (a_seq, bu), axis=1)
    c_mat = lax.complex(c_re.astype(f32), c_im.astype(f32))
    y = jnp.real(jnp.einsum('ghp,bsgp->bsgh', c_mat, states)) \
        + d_skip.astype(f32).reshape(SSM_GROUPS, SSM_GROUP) * ug
    y = jax.nn.gelu(y.reshape(bsz, seq, SSM_WIDTH))
    y = y * jax.nn.sigmoid(y @ w_glu.astype(f32) + b_glu.astype(f32))
    return y.astype(u.dtype)

def hierarchical_moe(h, w_rg, b_rg, w_re, b_re, w1, w3, w2):
    bsz, seq, d = h.shape
    n_tok = bsz * seq
    hf = h.reshape(n_tok, d)
    g_logits = (hf @ w_rg + b_rg).astype(jnp.float32)
    g_prob = jax.nn.softmax(g_logits, axis=-1)
    _, g_sel = lax.top_k(g_logits, 1)
    g_gate = jnp.take_along_axis(g_prob, g_sel, axis=-1)
    e_logits = (hf @ w_re + b_re).astype(jnp.float32).reshape(n_tok, N_EXPERT_GROUPS, EXPERTS_PER_GROUP)
    e_in = jnp.take_along_axis(e_logits, g_sel[:, :, None], axis=1)[:, 0]
    top_v, top_i = lax.top_k(e_in, TOP_K)
    weights = g_gate * jax.nn.softmax(top_v, axis=-1)
    expert_ids = g_sel * EXPERTS_PER_GROUP + top_i
    n_assign = n_tok * TOP_K
    e_flat = expert_ids.reshape(n_assign)
    tok_flat = jnp.repeat(jnp.arange(n_tok, dtype=jnp.int32), TOP_K)
    w_flat = weights.reshape(n_assign)
    order = jnp.argsort(e_flat)
    e_sorted = e_flat[order]
    counts = jnp.bincount(e_flat, length=N_EXPERTS)
    starts = jnp.cumsum(counts) - counts
    padded = (counts + MOE_BLOCK - 1) // MOE_BLOCK * MOE_BLOCK
    pad_ends = jnp.cumsum(padded)
    pad_starts = pad_ends - padded
    dest = pad_starts[e_sorted] + jnp.arange(n_assign) - starts[e_sorted]
    n_blocks = (n_assign + N_EXPERTS * (MOE_BLOCK - 1) + MOE_BLOCK - 1) // MOE_BLOCK
    cap = n_blocks * MOE_BLOCK
    row_tok = jnp.zeros((cap,), jnp.int32).at[dest].set(tok_flat[order])
    row_w = jnp.zeros((cap,), jnp.float32).at[dest].set(w_flat[order])
    block_expert = jnp.minimum(
        jnp.searchsorted(pad_ends, jnp.arange(n_blocks) * MOE_BLOCK, side='right'), N_EXPERTS - 1)
    xb = hf[row_tok].reshape(n_blocks, MOE_BLOCK, d)

    def expert_block(args):
        xblk, e = args
        return (jax.nn.silu(xblk @ w1[e]) * (xblk @ w3[e])) @ w2[e]

    yb = lax.map(expert_block, (xb, block_expert)).reshape(cap, d)
    out = jnp.zeros((n_tok, d), jnp.float32).at[row_tok].add(yb.astype(jnp.float32) * row_w[:, None])
    return out.reshape(bsz, seq, d).astype(h.dtype)

def setup_inputs(seed: int = 0) -> dict:
    key = jax.random.key(seed)
    ks = jax.random.split(key, 32)
    f32 = jnp.float32
    L = DEPTH

    def nrm(k, shape, fan_in):
        return jax.random.normal(k, shape, f32) * fan_in ** -0.5

    def gain(k):
        return 1.0 + 0.05 * jax.random.normal(k, (L, D_MODEL), f32)

    return {
        'x': jax.random.normal(ks[0], (BATCH, SEQ, D_MODEL), f32),
        'c': jax.random.normal(ks[1], (BATCH, D_MODEL), f32),
        'w_mod': 0.5 * nrm(ks[2], (L, D_MODEL, 6 * D_MODEL), D_MODEL),
        'b_mod': 0.01 * jax.random.normal(ks[3], (L, 6 * D_MODEL), f32),
        'g_pre_mix': gain(ks[4]),
        'g_post_mix': gain(ks[5]),
        'g_pre_ffn': gain(ks[6]),
        'g_post_ffn': gain(ks[7]),
        'w_in': nrm(ks[8], (L, D_MODEL, IN_WIDTH), D_MODEL),
        'rel_bias': 0.5 * jax.random.normal(ks[9], (NUM_BUCKETS, N_HEADS_ATTN), f32),
        'a_re': -0.5 + 0.01 * jax.random.normal(ks[10], (L, SSM_GROUPS, SSM_STATE), f32),
        'a_im': jnp.pi * jnp.arange(SSM_STATE, dtype=f32) + 0.01 * jax.random.normal(ks[11], (L, SSM_GROUPS, SSM_STATE), f32),
        'log_dt': jax.random.uniform(ks[12], (L, SSM_GROUPS), f32, math.log(DT_MIN), math.log(DT_MAX)),
        'ssm_b_re': nrm(ks[13], (L, SSM_GROUPS, SSM_STATE, SSM_GROUP), 2 * SSM_GROUP),
        'ssm_b_im': nrm(ks[14], (L, SSM_GROUPS, SSM_STATE, SSM_GROUP), 2 * SSM_GROUP),
        'ssm_c_re': nrm(ks[15], (L, SSM_GROUPS, SSM_GROUP, SSM_STATE), SSM_STATE),
        'ssm_c_im': nrm(ks[16], (L, SSM_GROUPS, SSM_GROUP, SSM_STATE), SSM_STATE),
        'd_skip': jax.random.normal(ks[17], (L, SSM_WIDTH), f32),
        'w_glu': nrm(ks[18], (L, SSM_WIDTH, SSM_WIDTH), SSM_WIDTH),
        'b_glu': 0.01 * jax.random.normal(ks[19], (L, SSM_WIDTH), f32),
        'w_branch_attn': nrm(ks[20], (L, ATTN_WIDTH, D_MODEL), ATTN_WIDTH),
        'w_branch_ssm': nrm(ks[21], (L, SSM_WIDTH, D_MODEL), SSM_WIDTH),
        'w_out': nrm(ks[22], (L, D_MODEL, D_MODEL), D_MODEL),
        'w_router_group': nrm(ks[23], (L, D_MODEL, N_EXPERT_GROUPS), D_MODEL),
        'b_router_group': 0.01 * jax.random.normal(ks[24], (L, N_EXPERT_GROUPS), f32),
        'w_router_expert': nrm(ks[25], (L, D_MODEL, N_EXPERTS), D_MODEL),
        'b_router_expert': 0.01 * jax.random.normal(ks[26], (L, N_EXPERTS), f32),
        'w1': nrm(ks[27], (L, N_EXPERTS, D_MODEL, D_EXPERT), D_MODEL),
        'w3': nrm(ks[28], (L, N_EXPERTS, D_MODEL, D_EXPERT), D_MODEL),
        'w2': nrm(ks[29], (L, N_EXPERTS, D_EXPERT, D_MODEL), D_EXPERT),
    }

def reference(x, c, w_mod, b_mod, g_pre_mix, g_post_mix, g_pre_ffn, g_post_ffn, w_in, rel_bias,
              a_re, a_im, log_dt, ssm_b_re, ssm_b_im, ssm_c_re, ssm_c_im, d_skip, w_glu, b_glu,
              w_branch_attn, w_branch_ssm, w_out, w_router_group, b_router_group,
              w_router_expert, b_router_expert, w1, w3, w2):
    bsz, seq, _ = x.shape
    splits = [ATTN_WIDTH, 2 * ATTN_WIDTH, 3 * ATTN_WIDTH, 3 * ATTN_WIDTH + SSM_WIDTH]
    for l in range(DEPTH):
        mod = jax.nn.silu(c) @ w_mod[l] + b_mod[l]
        sh1, sc1, gt1, sh2, sc2, gt2 = [m[:, None, :] for m in jnp.split(mod, 6, axis=-1)]
        h = rms_norm(x, g_pre_mix[l]) * (1.0 + sc1) + sh1
        proj = h @ w_in[l]
        q, k, v, u, gate_logits = jnp.split(proj, splits, axis=-1)
        heads = (bsz, seq, N_HEADS_ATTN, HEAD_DIM)
        attn = dilated_mixture_attention(q.reshape(heads), k.reshape(heads), v.reshape(heads), rel_bias)
        attn = attn.reshape(bsz, seq, ATTN_WIDTH).astype(x.dtype)
        ssm = s5_mixer(u, a_re[l], a_im[l], log_dt[l], ssm_b_re[l], ssm_b_im[l],
                       ssm_c_re[l], ssm_c_im[l], d_skip[l], w_glu[l], b_glu[l])
        g_attn, g_ssm = jnp.split(jax.nn.sigmoid(gate_logits), 2, axis=-1)
        merged = g_attn * (attn @ w_branch_attn[l]) + g_ssm * (ssm @ w_branch_ssm[l])
        y = merged @ w_out[l]
        x = x + gt1 * rms_norm(y, g_post_mix[l])
        h = rms_norm(x, g_pre_ffn[l]) * (1.0 + sc2) + sh2
        y = hierarchical_moe(h, w_router_group[l], b_router_group[l], w_router_expert[l],
                             b_router_expert[l], w1[l], w3[l], w2[l])
        x = x + gt2 * rms_norm(y, g_post_ffn[l])
    return x


_drawn_inputs = setup_inputs


def setup_inputs(seed=0):
    import zlib

    import numpy as np

    out = dict(_drawn_inputs(seed))
    spreads = {}
    factors = {'g_post_ffn': 4.14,
     'a_re': 8.0,
     'b_glu': 4.612,
     'b_router_group': 3.199,
     'b_router_expert': 2.859}
    for name, (base, spread) in spreads.items():
        noise = np.random.default_rng([zlib.crc32(name.encode()), seed]).standard_normal(out[name].shape)
        drawn = base * np.exp(spread * noise) if base else spread * noise
        out[name] = __import__('jax').numpy.asarray(drawn.astype(out[name].dtype))
    for name, factor in factors.items():
        out[name] = (out[name] * factor).astype(out[name].dtype)
    return out
```

```python
from contextlib import ExitStack

import numpy as np

import concourse.bass as bass
from concourse import mybir

ALU = mybir.AluOpType
ACT = mybir.ActivationFunctionType
F32 = mybir.dt.float32
I32 = mybir.dt.int32
AX_X = mybir.AxisListType.X

P = 128
D = 1024
KD = D // P
T = 2048
NT = T // P
NH, HD = 8, 64
AW = NH * HD
DILS = (1, 4, 16)
NEG = -1e30
NUM_B, MAX_DIST = 32, 2048
EPS = 1e-6
NG_S, CH_S, ST_S = 32, 16, 64
SW = NG_S * CH_S
LC = 16
NC = T // LC
QKVU = 3 * AW + SW
IN_W = QKVU + 2 * D
NGR, EPG = 4, 8
NE = NGR * EPG
DE = D // 2
KE = DE // P
NBLK = 64
CAP = NBLK * P


def ds(i, n):
    return bass.ds(i, n)


def bucket_one_hot():
    exact = NUM_B // 2
    hot = np.zeros((NUM_B + 1, len(DILS), 3 * P - 1), np.float32)
    hot[NUM_B] = 1.0
    for p, dil in enumerate(DILS):
        for d in range(P + 1):
            dist = d * dil
            large = exact + int(np.float32(np.log(np.float32(max(dist, exact)) / np.float32(exact)))
                                / np.float32(np.log(MAX_DIST / exact)) * np.float32(NUM_B - exact))
            b = dist if dist < exact else min(large, NUM_B - 1)
            at = P - 1 + P - d
            hot[NUM_B, p, at] = 0.0
            hot[b, p, at] = 1.0
    return hot


class Ctx:

    def __init__(self, nc):
        self.nc, self.stack, self.sems = nc, ExitStack(), []

    def __enter__(self):
        self.stack.__enter__()
        return self

    def __exit__(self, *a):
        if a[0] is None and self.sems:
            self.nc.all_engine_barrier()
            self.nc.clear_and_free_semaphores(self.sems)
            self.nc.all_engine_barrier()
        return self.stack.__exit__(*a)

    def sb(self, name, shape, dt=F32):
        return self.stack.enter_context(self.nc.sbuf_tensor(name, shape, dt))

    def ps(self, name, shape, dt=F32):
        return self.stack.enter_context(self.nc.psum_tensor(name, shape, dt))

    def sem(self, name):
        self.sems.append(self.nc.alloc_semaphore(name))
        return self.sems[-1]


def stage_modulation(nc, g, A):
    with Ctx(nc) as c:
        wm = [c.sb(f"wmod{b}", [P, 6 * D]) for b in range(2)]
        ccol = c.sb("ccol", [P, KD])
        sig = c.sb("csig", [P, KD])
        scol = c.sb("scol", [P, KD])
        bmod = c.sb("bmod", [P, 6 * KD])
        mod = c.sb("mod", [P, 6 * KD])
        gains = c.sb("gains", [P, 4, KD])
        gcol = c.sb("gcol", [P, 2, KD])
        xs = [c.sb(f"xs{b}", [P, D]) for b in range(2)]
        ss = c.sb("ss", [P, NT])
        ms = c.sb("ms", [P, NT])
        psm = c.ps("psm", [P, 512])
        psr = [c.ps(f"psr{b}", [P, 512]) for b in range(4)]
        small_in = c.sem("mod_small_in")
        w_in = [c.sem(f"wmod_in{b}") for b in range(2)]
        w_used = c.sem("wmod_used")
        sig_done = c.sem("csig_done")
        silu_done = c.sem("csilu_done")
        mod_done = c.sem("mod_done")
        vstep = c.sem("mod_vstep")
        ident0 = c.sem("ident0")
        ident1 = c.sem("ident_done")
        rows_done = c.sem("rows_done")
        rows_out = c.sem("rows_out")
        x_in = [c.sem(f"xs_in{b}") for b in range(2)]
        sq = c.sem("x_sq")
        ms_done = c.sem("ms_done")
        rms_done = c.sem("rms_done")
        rstd_done = c.sem("rstd_done")
        xv = A["x"][0].rearrange("(t p) n -> t p n", p=P)
        wv = A["w_mod"][0].rearrange("(k p) n -> k p n", p=P)

        with nc.Block() as block:
            @block.sync
            def _(sp):
                sp.dma_start(ccol[:, :], A["c"].rearrange("a (k p) -> p (a k)", p=P),
                             allow_slow_non_contiguous=True).then_inc(small_in, 16)
                sp.dma_start(bmod[:, :], A["b_mod"].rearrange("a (k p) -> p (a k)", p=P),
                             allow_slow_non_contiguous=True).then_inc(small_in, 16)
                for n, name in enumerate(("g_pre_mix", "g_post_mix", "g_pre_ffn", "g_post_ffn")):
                    sp.dma_start(gains[:, n, :], A[name].rearrange("a (k p) -> p (a k)", p=P),
                                 allow_slow_non_contiguous=True).then_inc(small_in, 16)
                for b in range(2):
                    sp.dma_start(wm[b][:, :], wv[b]).then_inc(w_in[b], 16)
                for b in range(2):
                    sp.dma_start(xs[b][:, :], xv[b]).then_inc(x_in[b], 16)
                with sp.Fori(1, NT // 2) as i:
                    for b in range(2):
                        sp.wait_ge(sq, 2 * i + b - 1)
                        sp.dma_start(xs[b][:, :], xv[ds(2 * i + b, 1)].rearrange("a p n -> (a p) n")).then_inc(x_in[b], 16)
                with sp.Fori(1, KD // 2) as i:
                    for b in range(2):
                        sp.wait_ge(w_used, 2 * i + b - 1)
                        sp.dma_start(wm[b][:, :], wv[ds(2 * i + b, 1)].rearrange("a p n -> (a p) n")).then_inc(w_in[b], 16)

            @block.gpsimd
            def _(pool):
                nc.gpsimd.memset(g["ident"][:, :], 0.0).then_inc(ident0, 1)
                pool.wait_ge(ident0, 1)
                nc.gpsimd.affine_select(out=g["ident"][:, :], in_=g["ident"][:, :], compare_op=ALU.not_equal,
                                        fill=1.0, base=0, pattern=[[-1, P]], channel_multiplier=1).then_inc(ident1, 1)

            @block.scalar
            def _(act):
                act.wait_ge(small_in, 96)
                nc.scalar.activation(sig[:, :], ccol[:, :], ACT.Sigmoid).then_inc(sig_done, 1)
                with act.Fori(0, NT // 2) as i:
                    for b in range(2):
                        act.wait_ge(x_in[b], 16 * i + 16)
                        nc.scalar.activation(xs[b][:, :], xs[b][:, :], ACT.Square,
                                             accum_out=ss[:, ds(2 * i + b, 1)]).then_inc(sq, 1)
                act.wait_ge(ms_done, 1)
                nc.scalar.activation(ms[:, :], ms[:, :], ACT.Sqrt).then_inc(rms_done, 1)

            @block.tensor
            def _(pe):
                pe.wait_ge(silu_done, 1)
                def chunk(b, first, last):
                    for n in range(6 * KD):
                        mm = nc.tensor.matmul(psm[:, n:n + 1], wm[b][:, n * P:(n + 1) * P], scol[:, chunk.k],
                                              start=first and n == 0, stop=last, skip_group_check=True)
                    mm.then_inc(w_used, 1)
                for b in range(2):
                    pe.wait_ge(w_in[b], 16)
                    chunk.k = slice(b, b + 1)
                    chunk(b, b == 0, False)
                with pe.Fori(1, KD // 2) as i:
                    for b in range(2):
                        pe.wait_ge(w_in[b], 16 * i + 16)
                        chunk.k = ds(2 * i + b, 1)
                        chunk(b, False, True)
                pe.wait_ge(ident1, 1)
                pe.wait_ge(vstep, 6)
                for r in range(2):
                    for k in range(KD):
                        o = psr[2 * r + k // 4][:, (k % 4) * P:(k % 4 + 1) * P]
                        mm = nc.tensor.matmul(o, gcol[:, r, k:k + 1].to_broadcast([P, P]), g["ident"][:, :],
                                              start=True, stop=True)
                mm.then_inc(rows_done, 1)

            @block.vector
            def _(v):
                v.wait_ge(sig_done, 1)
                v.tensor_tensor(scol[:, :], ccol[:, :], sig[:, :], ALU.mult).then_inc(silu_done, 1)
                v.wait_ge(sq, NT)
                v.tensor_scalar(ms[:, :], ss[:, :], 1.0 / D, EPS, ALU.mult, ALU.add).then_inc(ms_done, 1)
                v.wait_ge(rms_done, 1)
                v.reciprocal(g["rstd"][:, :], ms[:, :]).then_inc(rstd_done, 1)
                v.wait_ge(w_used, KD)
                v.tensor_tensor(mod[:, :], psm[:, 0:6 * KD], bmod[:, :], ALU.add).then_inc(mod_done, 1)
                v.wait_ge(mod_done, 1)
                for r in range(2):
                    sh, sc, gt = (mod[:, (3 * r + j) * KD:(3 * r + j + 1) * KD] for j in range(3))
                    v.scalar_tensor_tensor(out=g["acol"][:, r, :], in0=sc, scalar=1.0, in1=gains[:, 2 * r, :],
                                           op0=ALU.add, op1=ALU.mult).then_inc(vstep, 1)
                    v.tensor_copy(g["bcol"][:, r, :], sh).then_inc(vstep, 1)
                    v.tensor_tensor(gcol[:, r, :], gt, gains[:, 2 * r + 1, :], ALU.mult).then_inc(vstep, 1)
                v.wait_ge(rows_done, 1)
                for j in range(4):
                    v.tensor_copy(g["grow"][:, j // 2, (j % 2) * 512:(j % 2 + 1) * 512], psr[j][:, :]).then_inc(rows_out, 1)
                v.wait_ge(rows_out, 4)
                v.wait_ge(rstd_done, 1)


def stage_projection(nc, g, A, S):
    with Ctx(nc) as c:
        w = c.sb("w_in_sb", [P, KD, IN_W])
        x = [c.sb(f"xt{b}", [P, D]) for b in range(2)]
        xn = [c.sb(f"xn{b}", [P, D]) for b in range(2)]
        hT = [c.sb(f"hT{b}", [P, KD, P]) for b in range(2)]
        qst = [c.sb(f"qst{b}", [P, QKVU]) for b in range(2)]
        gst = [c.sb("gst", [P, 2 * D])] * 2
        pst = [c.ps(f"pst{b}", [P, 4, P]) for b in range(2)]
        pso = [c.ps(f"pso{b}", [P, 512]) for b in range(4)]
        w_ld = [c.sem(f"win_in{k}") for k in range(KD)]
        x_in = [c.sem(f"x_in{b}") for b in range(2)]
        xnd = c.sem("xn_done")
        tp = c.sem("hT_psum")
        ht = c.sem("hT_done")
        po = c.sem("proj_psum")
        qe = c.sem("qkvu_evac")
        ge = c.sem("gates_evac")
        q_st = [c.sem(f"qkvu_st{b}") for b in range(2)]
        g_st = c.sem("gates_st")
        xv = A["x"][0].rearrange("(t p) n -> t p n", p=P)
        qv = S["qkvu"].rearrange("(t p) n -> t p n", p=P)
        gv = S["gates"].rearrange("(t p) n -> t p n", p=P)

        with nc.Block() as block:
            @block.sync
            def _(sp):
                for b in range(2):
                    sp.dma_start(x[b][:, :], xv[b]).then_inc(x_in[b], 16)
                wv = A["w_in"][0].rearrange("(k p) n -> k p n", p=P)
                for k in range(KD):
                    sp.dma_start(w[:, k, :], wv[k]).then_inc(w_ld[k], 16)

                def stores(t, b):
                    sp.wait_ge(qe, 4 * t + 4)
                    sp.dma_start(qv[ds(t, 1)].rearrange("a p n -> (a p) n"), qst[b][:, :]).then_inc(q_st[b], 16)
                    sp.wait_ge(ge, 4 * t + 4)
                    sp.dma_start(gv[ds(t, 1)].rearrange("a p n -> (a p) n"), gst[b][:, :]).then_inc(g_st, 16)

                with sp.Fori(0, NT // 2 - 1) as i:
                    for b in range(2):
                        t = 2 * i + b
                        sp.wait_ge(xnd, t + 1)
                        sp.dma_start(x[b][:, :], xv[ds(t + 2, 1)].rearrange("a p n -> (a p) n")).then_inc(x_in[b], 16)
                        stores(t, b)
                for b in range(2):
                    stores(NT - 2 + b, b)
                for b in range(2):
                    sp.wait_ge(q_st[b], 16 * NT // 2)
                sp.wait_ge(g_st, 16 * NT)

            @block.scalar
            def _(act):
                def gates(i, b, t, first):
                    for n in range(4):
                        act.wait_ge(po, 8 * t + 4 + n + 1)
                        if n == 0 and not first:
                            act.wait_ge(g_st, 16 * t)
                        nc.scalar.activation(gst[b][:, n * 512:(n + 1) * 512], pso[n][:, :],
                                             ACT.Sigmoid).then_inc(ge, 1)

                gates(0, 0, 0, True)
                gates(0, 1, 1, False)
                with act.Fori(1, NT // 2) as i:
                    for b in range(2):
                        gates(i, b, 2 * i + b, False)

            @block.tensor
            def _(pe):
                def transposes(t, b):
                    pe.wait_ge(xnd, t + 1)
                    for half in range(2):
                        if not (isinstance(t, int) and t == 0):
                            pe.wait_ge(ht, 8 * t - 4 + 4 * half)
                        for k in range(4):
                            mm = nc.tensor.transpose(pst[half][:, k, :], xn[b][:, (4 * half + k) * P:(4 * half + k + 1) * P],
                                                     g["ident"][:, :])
                        mm.then_inc(tp, 1)

                def project(t, b):
                    first = isinstance(t, int) and t == 0
                    pe.wait_ge(ht, 8 * t + 8)
                    for n in range(8):
                        if n < 4 and not first:
                            pe.wait_ge(ge, 4 * t - 3 + n)
                        if n >= 4:
                            pe.wait_ge(qe, 4 * t + n - 3)
                        for k in range(KD):
                            if first and n == 0:
                                pe.wait_ge(w_ld[k], 16)
                            mm = nc.tensor.matmul(pso[n % 4][:, :], hT[b][:, k, :], w[:, k, n * 512:(n + 1) * 512],
                                                  start=k == 0, stop=k == KD - 1)
                        mm.then_inc(po, 1)

                transposes(0, 0)
                project(0, 0)
                transposes(1, 1)
                project(1, 1)
                with pe.Fori(1, NT // 2) as i:
                    for b in range(2):
                        transposes(2 * i + b, b)
                        project(2 * i + b, b)

            @block.vector
            def _(v):
                def norm(i, b):
                    t = 2 * i + b
                    v.wait_ge(x_in[b], 16 * i + 16)
                    if not (isinstance(t, int) and t < 2):
                        v.wait_ge(tp, 2 * t - 2)
                    v.tensor_scalar(xn[b][:, :], x[b][:, :], g["rstd"][:, ds(t, 1)], None, ALU.mult).then_inc(xnd, 1)

                def affine(t, b):
                    for k in range(KD):
                        v.wait_ge(tp, 2 * t + k // 4 + 1)
                        if k == 0 and not (isinstance(t, int) and t < 2):
                            v.wait_ge(po, 8 * t - 8)
                        v.tensor_scalar(hT[b][:, k, :], pst[k // 4][:, k % 4, :], g["acol"][:, 0, k:k + 1],
                                        g["bcol"][:, 0, k:k + 1], ALU.mult, ALU.add).then_inc(ht, 1)

                def evac(t, b):
                    for n in range(4):
                        v.wait_ge(po, 8 * t + n + 1)
                        if n == 0 and not (isinstance(t, int) and t < 2):
                            v.wait_ge(q_st[b], 16 * evac.i)
                        v.tensor_scalar(qst[b][:, n * 512:(n + 1) * 512], pso[n][:, :],
                                        HD ** -0.5 if n == 0 else 1.0, None, ALU.mult).then_inc(qe, 1)

                norm(0, 0)
                affine(0, 0)
                norm(0, 1)
                evac(0, 0)
                affine(1, 1)
                norm(1, 0)
                evac(1, 1)
                with v.Fori(1, NT // 2 - 1) as i:
                    evac.i = i
                    affine(2 * i, 0)
                    norm(i, 1)
                    evac(2 * i, 0)
                    affine(2 * i + 1, 1)
                    norm(i + 1, 0)
                    evac(2 * i + 1, 1)
                evac.i = NT // 2 - 1
                affine(NT - 2, 0)
                norm(NT // 2 - 1, 1)
                evac(NT - 2, 0)
                affine(NT - 1, 1)
                evac(NT - 1, 1)


def stage_bias(nc, g, A, S):
    W = 3 * P - 1
    with Ctx(nc) as c:
        hot = c.sb("bucket_hot", [NUM_B + 1, len(DILS), W])
        rb = c.sb("rel_bias_sb", [NUM_B + 1, NH])
        row = c.sb("bias_row", [NH, len(DILS), W])
        ps = [c.ps(f"ps_bias{p}", [P, 512]) for p in range(len(DILS))]
        hot_in, neg_done, mm_done = c.sem("hot_in"), c.sem("neg_done"), c.sem("bias_mm")
        row_done, row_st, bias_in = c.sem("row_done"), c.sem("row_st"), g["bias_in"]
        with nc.Block() as block:
            @block.sync
            def _(sp):
                sp.dma_start(hot[:, :, :], A["bucket_hot"]).then_inc(hot_in, 16)
                sp.dma_start(rb[0:NUM_B, :], A["rel_bias"]).then_inc(hot_in, 16)
                sp.wait_ge(row_done, len(DILS))
                sp.dma_start(S["bias_rows"], row[:, :, :]).then_inc(row_st, 16)
                sp.wait_ge(row_st, 16)
                pitch = NH * len(DILS) * W
                one = S["bias_rows"]
                sp.dma_start(S["bias_copies"], bass.AP(tensor=one.tensor, offset=one.offset, ap=[[0, P], [1, pitch]])).then_inc(row_st, 16)
                sp.wait_ge(row_st, 32)
                src = S["bias_copies"]
                for p in range(len(DILS)):
                    view = bass.AP(tensor=src.tensor, offset=src.offset + p * W + P - 1,
                                   ap=[[pitch - 1, P], [len(DILS) * W, NH], [1, 2 * P]])
                    sp.dma_start(g["bias"][:, p, :, :], view).then_inc(bias_in, 16)
                sp.wait_ge(bias_in, 16 * len(DILS))

            @block.tensor
            def _(pe):
                pe.wait_ge(hot_in, 32)
                pe.wait_ge(neg_done, 1)
                for p in range(len(DILS)):
                    nc.tensor.matmul(ps[p][0:NH, 0:W], rb[:, :], hot[:, p, :], start=True, stop=True).then_inc(mm_done, 1)

            @block.vector
            def _(v):
                v.memset(rb[NUM_B:NUM_B + 1, :], NEG).then_inc(neg_done, 1)
                for p in range(len(DILS)):
                    v.wait_ge(mm_done, p + 1)
                    v.tensor_copy(row[:, p, :], ps[p][0:NH, 0:W]).then_inc(row_done, 1)


def stage_attention(nc, g, A, S):
    NP_ = NH // 2
    with Ctx(nc) as c:
        qk = [c.sb(f"qk{b}", [P, 2 * AW]) for b in range(2)]
        vv = [c.sb(f"v{b}", [P, AW]) for b in range(4)]
        qT = [c.sb(f"qT{b}", [P, NP_, P]) for b in range(2)]
        kT = c.sb("kT", [P, NP_, 5, P])
        pr = [c.sb(f"probs{b}", [P, 2, 2 * P]) for b in range(4)]
        pT = [c.sb(f"probsT{b}", [P, 2, 2, P]) for b in range(2)]
        nm = [c.sb(f"negmax{b}", [P, 2]) for b in range(4)]
        osb = [c.sb(f"osb{b}", [P, AW + 2 * NH]) for b in range(2)]
        tick = c.sb("tick", [P, 4])
        ps_t = c.ps("ps_qk", [P, NP_, P])
        ps_s = [c.ps(f"ps_s{b}", [P, 2, 2 * P]) for b in range(4)]
        ps_p = [c.ps(f"ps_p{b}", [P, 2, 2, P]) for b in range(2)]
        ps_o = c.ps("ps_o", [P, NH, HD])
        qk_in = [c.sem(f"qk_in{b}") for b in range(2)]
        v_in = [c.sem(f"v_in{b}") for b in range(4)]
        tq, qkT = c.sem("qk_psum"), c.sem("qkT_done")
        k_again = c.sem("k_again")
        mx = c.sem("max_done")
        s_ps, s_sb = c.sem("s_psum"), c.sem("s_biased")
        ex = c.sem("exp_done")
        p_ps, p_sb = c.sem("pT_psum"), c.sem("pT_done")
        pv, oe = c.sem("pv_done"), c.sem("o_evac")
        o_st = [c.sem(f"o_st{b}") for b in range(2)]

        rows = S["qkvu"]

        def head(j, h):
            return 4 * (j // 2) + j % 2 + 2 * h

        def tokens(dram, d, i, r, c0, c1):
            if d == 1:
                return dram.rearrange("(b p) n -> b p n", p=P)[ds(4 * i + r, 1), :, c0:c1].rearrange("a p n -> (a p) n")
            if d == 4:
                v = dram.rearrange("(b p s) n -> b s p n", p=P, s=4)
                return v[r, ds(i, 1), :, c0:c1].rearrange("a p n -> (a p) n")
            v = dram.rearrange("(p s) n -> s p n", s=16)
            return v[ds(4 * i + r, 1), :, c0:c1].rearrange("a p n -> (a p) n")

        def groups(eng, body):
            for p in range(len(DILS)):
                if p == 0:
                    body(p, 0, True)
                with eng.Fori(1 if p == 0 else 0, 4) as i:
                    body(p, i, False)

        def prev(p, r, first):
            return p == 0 and (r > 0 or not first) or p == 1 and r > 0

        with nc.Block() as block:
            @block.sync
            def _(sp):
                def body(p, i, first):
                    for r in range(4):
                        u = 16 * p + 4 * i + r
                        if not (first and r < 2):
                            sp.wait_ge(tq, 2 * u - 2)
                        sp.dma_start(qk[r % 2][:, :], tokens(rows, DILS[p], i, r, 0, 2 * AW)).then_inc(qk_in[r % 2], 16)
                        if not first:
                            sp.wait_ge(pv, NP_ * (u - 2))
                        sp.dma_start(vv[r][:, :], tokens(rows, DILS[p], i, r, 2 * AW, 3 * AW)).then_inc(v_in[r], 16)
                groups(sp, body)

            @block.gpsimd
            def _(pool):
                def body(p, i, first):
                    for r in range(4):
                        u = 16 * p + 4 * i + r
                        pool.wait_ge(oe, u + 1)
                        pool.dma_start(tokens(S["o"][p], DILS[p], i, r, 0, AW + 2 * NH), osb[r % 2][:, :]).then_inc(o_st[r % 2], 16)
                groups(pool, body)
                for b in range(2):
                    pool.wait_ge(o_st[b], 16 * 24)

            @block.tensor
            def _(pe):
                def body(p, i, first):
                    u0 = 16 * p + 4 * i
                    n0 = NP_ * u0

                    def turn_qk(r, h):
                        u = u0 + r
                        pe.wait_ge(qk_in[r % 2], 16 * (8 * p + 2 * i + r // 2 + 1))
                        if not (first and r == 0 and h == 0):
                            pe.wait_ge(qkT, 2 * u + h)
                        for n in range(NP_):
                            mm = nc.tensor.transpose(ps_t[:, n, :], qk[r % 2][:, (NP_ * h + n) * P:(NP_ * h + n + 1) * P],
                                                     g["ident"][:, :])
                        mm.then_inc(tq, 1)

                    def scores(m):
                        r, j = m // NP_, m % NP_
                        has = prev(p, r, first)
                        own = 4 if r == 0 and has else r
                        pe.wait_ge(qkT, 2 * (u0 + r) + 2)
                        if own == 4:
                            pe.wait_ge(k_again, i)
                        if not (first and m < 4):
                            pe.wait_ge(s_sb, n0 + m - 3)
                        for h in range(2):
                            hh = head(j, h)
                            lo, hi = HD * (hh % 2), HD * (hh % 2 + 1)
                            keys = slice(own - 1, own + 1) if has else slice(own, own + 1)
                            mm = nc.tensor.matmul(ps_s[m % 4][:, h, (0 if has else P):], qT[r % 2][lo:hi, hh // 2, :],
                                                  kT[lo:hi, hh // 2, keys, :], start=True, stop=True)
                        mm.then_inc(s_ps, 1)

                    def turn(m):
                        pe.wait_ge(ex, n0 + m + 1)
                        if not (first and m < 2):
                            pe.wait_ge(p_sb, n0 + m - 1)
                        for h in range(2):
                            for w in range(0 if prev(p, m // NP_, first) else 1, 2):
                                mm = nc.tensor.transpose(ps_p[m % 2][:, h, w, :], pr[m % 4][:, h, w * P:(w + 1) * P],
                                                         g["ident"][:, :])
                        mm.then_inc(p_ps, 1)

                    def values(m):
                        r, j = m // NP_, m % NP_
                        if j == 0:
                            pe.wait_ge(v_in[r], 16 * (4 * p + i + 1))
                            if not (first and r == 0):
                                pe.wait_ge(oe, u0 + r)
                        pe.wait_ge(p_sb, n0 + m + 1)
                        has = prev(p, r, first)
                        for h in range(2):
                            hh = head(j, h)
                            for w in range(0 if has else 1, 2):
                                mm = nc.tensor.matmul(ps_o[:, hh, :], pT[m % 2][:, h, w, :],
                                                      vv[(r - 1 + w) % 4][:, hh * HD:(hh + 1) * HD],
                                                      start=not (has and w), stop=w == 1)
                        mm.then_inc(pv, 1)

                    turn_qk(0, 0)
                    turn_qk(0, 1)
                    scores(0)
                    scores(1)
                    for m in range(4 * NP_):
                        r, j = m // NP_, m % NP_
                        if m + 2 < 4 * NP_:
                            scores(m + 2)
                        if j < 2 and r < 3:
                            turn_qk(r + 1, j)
                        turn(m)
                        if m:
                            values(m - 1)
                    values(4 * NP_ - 1)
                groups(pe, body)

            @block.vector
            def _(v):
                def body(p, i, first):
                    u0 = 16 * p + 4 * i
                    n0 = NP_ * u0

                    def evac_qk(r, h):
                        u = u0 + r
                        v.wait_ge(tq, 2 * u + h + 1)
                        if not (first and r < 2):
                            v.wait_ge(s_ps, NP_ * (u - 1))
                        dst = kT[:, :, r, :] if h else qT[r % 2][:, :, :]
                        v.tensor_copy(dst, ps_t[:, :, :]).then_inc(qkT, 1)
                        if h and r == 0 and p == 0 and not first:
                            v.wait_ge(qkT, 2 * u + 2)
                            v.tensor_copy(kT[:, :, 4, :], kT[:, :, 0, :]).then_inc(k_again, 1)

                    def bias_max(m):
                        r, j = m // NP_, m % NP_
                        u, n, b = u0 + r, n0 + m, m % 4
                        k0 = 0 if prev(p, r, first) else P
                        if j == 0 and not (first and r < 2):
                            v.wait_ge(o_st[r % 2], 16 * (8 * p + 2 * i + r // 2))
                        if not (first and m < 4):
                            v.wait_ge(p_ps, n - 3)
                        v.wait_ge(s_ps, n + 1)
                        v.memset(tick[:, b:b + 1], 0.0)
                        for h in range(2):
                            hh = head(j, h)
                            v.tensor_tensor_reduce(pr[b][:, h, k0:], ps_s[b][:, h, k0:], g["bias"][:, p, hh, k0:], 1.0, -3e38,
                                                   ALU.add, ALU.max, osb[r % 2][:, AW + hh:AW + hh + 1]).then_inc(mx, 1)
                        v.wait_ge(mx, 2 * n + 2)
                        v.tensor_scalar(nm[b][:, :], osb[r % 2][:, AW + head(j, 0):AW + head(j, 1) + 1:2], -1.0, None,
                                        ALU.mult).then_inc(s_sb, 1)

                    def evac_o(r):
                        u = u0 + r
                        v.wait_ge(pv, NP_ * u + NP_)
                        v.wait_ge(ex, NP_ * u + NP_)
                        v.tensor_copy(osb[r % 2][:, 0:AW], ps_o[:, :, :].rearrange("p h d -> p (h d)")).then_inc(oe, 1)

                    evac_qk(0, 0)
                    evac_qk(0, 1)
                    for m in range(4 * NP_):
                        r, j = m // NP_, m % NP_
                        bias_max(m)
                        if j == 1 and r:
                            evac_o(r - 1)
                        if j in (1, 2) and r < 3:
                            evac_qk(r + 1, j - 1)
                    evac_o(3)
                v.wait_ge(g["bias_in"], 16 * len(DILS))
                groups(v, body)

            @block.scalar
            def _(act):
                def body(p, i, first):
                    n0 = NP_ * (16 * p + 4 * i)
                    for m in range(4 * NP_ + 1):
                        if m < 4 * NP_:
                            r, j = m // NP_, m % NP_
                            k0 = 0 if prev(p, r, first) else P
                            act.wait_ge(s_sb, n0 + m + 1)
                            for h in range(2):
                                hh = head(j, h)
                                e = nc.scalar.activation(pr[m % 4][:, h, k0:], pr[m % 4][:, h, k0:], ACT.Exp,
                                                         bias=nm[m % 4][:, h:h + 1],
                                                         accum_out=osb[r % 2][:, AW + NH + hh:AW + NH + hh + 1])
                            e.then_inc(ex, 1)
                        if m:
                            q = m - 1
                            act.wait_ge(p_ps, n0 + m)
                            if not (first and q < 2):
                                act.wait_ge(pv, n0 + q - 1)
                            w0 = 0 if prev(p, q // NP_, first) else 1
                            nc.scalar.activation(pT[q % 2][:, :, w0:, :], ps_p[q % 2][:, :, w0:, :], ACT.Copy).then_inc(p_sb, 1)
                groups(act, body)


REC = 2 * 192 + 4 * 256


def stage_ssm_tables(nc, g, A, S):
    H = ST_S
    with Ctx(nc) as c:
        craw = [c.sb(f"craw{n}", [P, 4, 2, H]) for n in range(2)]
        araw = [c.sb(f"araw{n}", [NG_S, 2, H]) for n in range(2)]
        B = [c.sb(f"B{n}", [P, NG_S, CH_S]) for n in range(2)]
        C = [c.sb(f"C{n}", [P, NG_S, CH_S]) for n in range(2)]
        lam = [c.sb(f"lam{n}", [P, NG_S]) for n in range(2)]
        dt = c.sb("dt", [P, NG_S])
        dsk = c.sb("dskip", [CH_S, NG_S])
        sm = {n: c.sb(f"sm_{n}", [P, NG_S]) for n in
              ("zr", "zi", "n", "r", "ab", "cs", "sn", "ea", "nr", "ni", "den", "inv", "t0", "t1", "fr", "fi", "z16")}
        pw = [c.sb(f"pw{n}", [P, LC + 1, NG_S]) for n in range(2)]
        pt = [c.sb(f"pt{n}", [P, NC // 2 * NG_S]) for n in range(2)]
        un = [c.sb(f"un{n}", [P, NG_S]) for n in range(2)]
        q1, q2, s2 = (c.sb(n, [P, LC + 1, NG_S]) for n in ("q1", "q2", "s2"))
        s1 = c.sb("s1", [P, LC + 1, NG_S])
        Bb = [c.sb(f"Bb{n}", [P, NG_S, CH_S]) for n in range(2)]
        tmp = [c.sb(f"tmp{n}", [P, NG_S, CH_S]) for n in range(2)]
        G = c.sb("G", [P, NG_S, LC + 1, CH_S])
        E = c.sb("E", [P, NG_S, LC, CH_S])
        dm = c.sb("dm", [CH_S, NG_S, CH_S])
        K = c.sb("K", [CH_S, 4, 256])
        zer = c.sb("zer", [CH_S, 256])
        Est = [c.sb(f"Est{b}", [P, 2, 3, H]) for b in range(2)]
        psA = c.ps("psA", [P, 4, P])
        psC = c.ps("psC", [P, 4, P])
        psK = [c.ps(f"psK{b}", [P, 2, 256]) for b in range(2)]
        psE = [c.ps(f"psE{b}", [P, 2, 2, H]) for b in range(2)]
        in_ = c.sem("ssm_in")
        tr, tr_out, dt_done = c.sem("ssm_tr"), c.sem("ssm_tr_out"), c.sem("dt_done")
        act_r, trig, step_n = c.sem("angle_ready"), c.sem("trig_done"), c.sem("ssm_step")
        k_ps, k_out, k_st = c.sem("k_psum"), c.sem("k_out"), c.sem("k_st")
        e_ps, e_out, e_st = c.sem("e_psum"), c.sem("e_out"), [c.sem(f"e_st{b}") for b in range(2)]
        g_done, e_done, zer_done, t_st = c.sem("G_done"), c.sem("E_done"), c.sem("zer_done"), c.sem("T_st")
        rot, rho = g["rot"], g["rho"]
        rec = S["rec"]
        t2 = c.sb("t2big", [P, NG_S, LC, CH_S])

        with nc.Block() as block:
            @block.sync
            def _(sp):
                for n, name in enumerate(("ssm_c_re", "ssm_c_im")):
                    for d in range(2):
                        sp.dma_start(craw[n][:, :, d, :], A[name][0].rearrange("(k g) c p -> (g c) k p", g=8)).then_inc(in_, 16)
                for n, name in enumerate(("a_re", "a_im")):
                    for d in range(2):
                        sp.dma_start(araw[n][:, d, :], A[name][0]).then_inc(in_, 16)
                for n, name in enumerate(("ssm_b_re", "ssm_b_im")):
                    for d in range(2):
                        sp.dma_start(B[n][H * d:H * d + H, :, :], A[name][0].rearrange("g p c -> p g c")).then_inc(in_, 16)
                sp.dma_start(dt[:, :], A["log_dt"].to_broadcast([P, NG_S])).then_inc(in_, 16)
                sp.dma_start(dsk[:, :], A["d_skip"].rearrange("a (g c) -> c (a g)", c=CH_S),
                             allow_slow_non_contiguous=True).then_inc(in_, 16)
                sp.wait_ge(g_done, 1)
                gr = rec.rearrange("g p n -> p g n")
                sp.dma_start(gr[:, :, 384:640], G[:, :, 1:, :].rearrange("p g s c -> p g (s c)")).then_inc(t_st, 16)
                for d in range(2):
                    sp.dma_start(gr[H * d:H * d + H, :, 640:896],
                                 G[H * (1 - d):H * (1 - d) + H, :, 1:, :].rearrange("p g s c -> p g (s c)")).then_inc(t_st, 16)
                sp.wait_ge(zer_done, 1)
                kp = S["kpad"]
                for q in range(NG_S // 4):
                    sp.wait_ge(k_out, 3 * q + 3)
                    sp.dma_start(kp[4 * q:4 * q + 4, :, 256:512].rearrange("g c n -> c g n"), K[:, :, :]).then_inc(k_st, 16)
                for gi in range(NG_S):
                    sp.dma_start(kp[gi, :, 0:256], zer[:, :]).then_inc(k_st, 16)
                sp.wait_ge(k_st, 16 * (NG_S // 4 + NG_S))
                for s in range(LC):
                    k, r = s // 8, s % 8
                    sp.dma_start(rec[:, CH_S * r:CH_S * r + CH_S, 896 + 256 * k:1152 + 256 * k],
                                 kp[:, :, 256 - CH_S * s:512 - CH_S * s]).then_inc(t_st, 16)
                sp.wait_ge(t_st, 16 * (3 + LC))

            @block.gpsimd
            def _(pool):
                for gi in range(NG_S):
                    b = gi % 2
                    pool.wait_ge(e_out, 2 * gi + 2)
                    pool.dma_start(rec[gi, :, 0:384], Est[b][:, :, :, :].rearrange("p k r h -> p (k r h)")).then_inc(e_st[b], 16)
                for b in range(2):
                    pool.wait_ge(e_st[b], 16 * NG_S // 2)

            @block.tensor
            def _(pe):
                pe.wait_ge(in_, 16 * 14)
                for n in range(2):
                    mm = nc.tensor.transpose(psA[:, n, 0:NG_S], araw[n][:, :, :].rearrange("g d p -> g (d p)"),
                                             g["ident"][0:NG_S, 0:NG_S])
                mm.then_inc(tr, 1)
                for n in range(2):
                    if n:
                        pe.wait_ge(tr_out, 2)
                    for k in range(4):
                        mm = nc.tensor.transpose(psC[:, k, :], craw[n][:, k, :, :].rearrange("q d p -> q (d p)"), g["ident"][:, :])
                    mm.then_inc(tr, 1)
                pe.wait_ge(g_done, 1)
                pe.wait_ge(e_done, 1)
                for gi in range(NG_S):
                    q = gi // 2
                    if gi % 2 == 0 and q >= 2:
                        pe.wait_ge(k_out, 3 * (q // 2) - 1 if q % 2 == 1 else 3 * (q // 2) - 2)
                    mm = nc.tensor.matmul(psK[q % 2][0:CH_S, gi % 2, :], E[:, gi, LC - 1, :],
                                          G[:, gi, 0:LC, :].rearrange("p s c -> p (s c)"), start=True, stop=True)
                    if gi % 2:
                        mm.then_inc(k_ps, 1)
                for gi in range(NG_S):
                    b = gi % 2
                    if gi >= 2:
                        pe.wait_ge(e_out, 2 * gi - 2)
                    for k in range(2):
                        mm = nc.tensor.transpose(psE[b][:, k, :, :].rearrange("p r h -> p (r h)"),
                                                 E[:, gi, 8 * k:8 * k + 8, :].rearrange("p s c -> p (s c)"), g["ident"][:, :])
                    mm.then_inc(e_ps, 1)

            @block.scalar
            def _(act):
                act.wait_ge(in_, 16 * 14)
                nc.scalar.activation(dt[:, :], dt[:, :], ACT.Exp).then_inc(dt_done, 1)
                act.wait_ge(act_r, 1)
                nc.scalar.activation(sm["ea"][:, :], sm["zr"][:, :], ACT.Exp).then_inc(trig, 1)
                nc.scalar.activation(rho[:, :], sm["z16"][:, :], ACT.Exp).then_inc(trig, 1)
                nc.scalar.activation(sm["sn"][:, :], sm["r"][:, :], ACT.Sin).then_inc(trig, 1)
                nc.scalar.activation(sm["cs"][:, :], sm["ab"][:, :], ACT.Sin).then_inc(trig, 1)
                for gi in range(NG_S):
                    b = gi % 2
                    act.wait_ge(e_ps, gi + 1)
                    if gi >= 2:
                        act.wait_ge(e_st[b], 16 * (gi // 2))
                    nc.scalar.activation(Est[b][:, :, 0:2, :], psE[b][:, :, :, :], ACT.Copy).then_inc(e_out, 1)
                    nc.scalar.activation(Est[b][:, :, 2, :], psE[b][:, :, 0, :], ACT.Copy).then_inc(e_out, 1)

            @block.vector
            def _(v):
                n_steps = [0]

                def did(ins):
                    n_steps[0] += 1
                    ins.then_inc(step_n, 1)
                    v.wait_ge(step_n, n_steps[0])

                def tt(o, a, b, op):
                    did(v.tensor_tensor(o, a, b, op))

                def cmul(o, a, b, shape):
                    x, y = (pt[n][:, 0:shape[0] * shape[1]].rearrange("p (m g) -> p m g", g=shape[1]) for n in range(2))
                    tt(x, a[0], b[0], ALU.mult)
                    tt(y, a[1], b[1], ALU.mult)
                    tt(o[0], x, y, ALU.subtract)
                    tt(x, a[0], b[1], ALU.mult)
                    tt(y, a[1], b[0], ALU.mult)
                    tt(o[1], x, y, ALU.add)

                v.memset(zer[:, :], 0.0).then_inc(zer_done, 1)
                v.wait_ge(tr, 1)
                did(v.tensor_copy(lam[0][:, :], psA[:, 0, 0:NG_S]))
                did(v.tensor_copy(lam[1][:, :], psA[:, 1, 0:NG_S]))
                for n in range(2):
                    v.wait_ge(tr, n + 2)
                    v.tensor_copy(C[n][:, :, :].rearrange("p g c -> p (g c)"), psC[:, :, :].rearrange("p k n -> p (k n)")).then_inc(tr_out, 2)
                v.wait_ge(tr_out, 4)
                v.wait_ge(dt_done, 1)
                t = {k: x[:, :] for k, x in sm.items()}
                tt(t["zr"], lam[0][:, :], dt[:, :], ALU.mult)
                tt(t["zi"], lam[1][:, :], dt[:, :], ALU.mult)
                did(v.tensor_scalar(t["z16"], t["zr"], float(LC), None, ALU.mult))
                big = 1.5 * 2 ** 23
                did(v.tensor_scalar(t["n"], t["zi"], 1 / (2 * np.pi), big, ALU.mult, ALU.add))
                did(v.tensor_scalar(t["n"], t["n"], big, None, ALU.subtract))
                c1 = 6.28125
                c2 = float(np.float32(np.round((2 * np.pi - c1) * 2 ** 20) / 2 ** 20))
                c3 = 2 * np.pi - c1 - c2
                did(v.scalar_tensor_tensor(out=t["r"], in0=t["n"], scalar=-c1, in1=t["zi"], op0=ALU.mult, op1=ALU.add))
                did(v.scalar_tensor_tensor(out=t["t0"], in0=t["n"], scalar=-c2, in1=t["r"], op0=ALU.mult, op1=ALU.add))
                did(v.scalar_tensor_tensor(out=t["r"], in0=t["n"], scalar=-c3, in1=t["t0"], op0=ALU.mult, op1=ALU.add))
                pi = float(np.float32(np.pi)) * (1 - 2 ** -23)
                did(v.tensor_scalar(t["r"], t["r"], pi, -pi, ALU.min, ALU.max))
                did(v.scalar_tensor_tensor(out=t["t0"], in0=t["r"], scalar=-1.0, in1=t["r"], op0=ALU.mult, op1=ALU.max))
                v.tensor_scalar(t["ab"], t["t0"], -1.0, np.pi / 2, ALU.mult, ALU.add).then_inc(act_r, 1)
                v.wait_ge(trig, 4)
                tt(pw[0][:, 1, :], t["ea"], t["cs"], ALU.mult)
                tt(pw[1][:, 1, :], t["ea"], t["sn"], ALU.mult)
                did(v.memset(pw[0][:, 0, :], 1.0))
                did(v.memset(pw[1][:, 0, :], 0.0))
                did(v.tensor_scalar(t["nr"], pw[0][:, 1, :], -1.0, None, ALU.add))
                ni = pw[1][:, 1, :]
                tt(t["t0"], lam[0][:, :], lam[0][:, :], ALU.mult)
                tt(t["t1"], lam[1][:, :], lam[1][:, :], ALU.mult)
                tt(t["den"], t["t0"], t["t1"], ALU.add)
                did(v.reciprocal(t["inv"], t["den"]))
                tt(t["t0"], t["nr"], lam[0][:, :], ALU.mult)
                tt(t["t1"], ni, lam[1][:, :], ALU.mult)
                tt(t["fr"], t["t0"], t["t1"], ALU.add)
                tt(t["fr"], t["fr"], t["inv"], ALU.mult)
                tt(t["t0"], ni, lam[0][:, :], ALU.mult)
                tt(t["t1"], t["nr"], lam[1][:, :], ALU.mult)
                tt(t["fi"], t["t0"], t["t1"], ALU.subtract)
                tt(t["fi"], t["fi"], t["inv"], ALU.mult)
                fr, fi = (sm[n][:, :].unsqueeze(2).to_broadcast([P, NG_S, CH_S]) for n in ("fr", "fi"))
                for o, (x, y, op) in enumerate(((0, 1, ALU.subtract), (1, 0, ALU.add))):
                    tt(tmp[0][:, :, :], B[x][:, :, :], fr, ALU.mult)
                    tt(tmp[1][:, :, :], B[y][:, :, :], fi, ALU.mult)
                    tt(Bb[o][:, :, :], tmp[0][:, :, :], tmp[1][:, :, :], op)
                m = 1
                while m < LC:
                    a_m = [x[:, m:m + 1, :].to_broadcast([P, m, NG_S]) for x in pw]
                    cmul([x[:, m + 1:2 * m + 1, :] for x in pw], [x[:, 1:m + 1, :] for x in pw], a_m, (m, NG_S))
                    m *= 2
                top, bot = slice(0, H), slice(H, P)
                for dst, half, src, sign in ((q1, top, 0, 1.0), (q1, bot, 1, -1.0), (q2, top, 1, -1.0), (q2, bot, 0, -1.0),
                                             (s1, top, 0, 1.0), (s1, bot, 1, 1.0), (s2, top, 1, -1.0), (s2, bot, 0, 1.0)):
                    did(v.tensor_scalar(dst[half, :, :], pw[src][half, :, :], sign, None, ALU.mult))
                for s in range(LC + 1):
                    pq = [x[:, s, :].unsqueeze(2).to_broadcast([P, NG_S, CH_S]) for x in (q1, q2)]
                    tt(tmp[0][:, :, :], C[0][:, :, :], pq[0], ALU.mult)
                    tt(tmp[1][:, :, :], C[1][:, :, :], pq[1], ALU.mult)
                    tt(G[:, :, s, :], tmp[0][:, :, :], tmp[1][:, :, :], ALU.add)
                v.engine_nop().then_inc(g_done, 1)
                for s in range(LC):
                    pq = [x[:, LC - 1 - s, :].unsqueeze(2).to_broadcast([P, NG_S, CH_S]) for x in (s1, s2)]
                    tt(tmp[0][:, :, :], Bb[0][:, :, :], pq[0], ALU.mult)
                    tt(tmp[1][:, :, :], Bb[1][:, :, :], pq[1], ALU.mult)
                    tt(E[:, :, s, :], tmp[0][:, :, :], tmp[1][:, :, :], ALU.add)
                v.engine_nop().then_inc(e_done, 1)
                tt(dm[:, :, :], g["ident"][0:CH_S, 0:CH_S].unsqueeze(1).to_broadcast([CH_S, NG_S, CH_S]),
                   dsk[:, :].unsqueeze(2).to_broadcast([CH_S, NG_S, CH_S]), ALU.mult)
                for q in range(NG_S // 4):
                    if q:
                        v.wait_ge(k_st, 16 * q)
                    for b in range(2):
                        v.wait_ge(k_ps, 2 * q + b + 1)
                        v.tensor_copy(K[:, 2 * b:2 * b + 2, :], psK[b][0:CH_S, :, :]).then_inc(k_out, 1)
                    v.wait_ge(k_out, 3 * q + 2)
                    v.tensor_tensor(K[:, :, 0:CH_S], K[:, :, 0:CH_S], dm[:, 4 * q:4 * q + 4, :], ALU.add).then_inc(k_out, 1)
                x, y = (sm[n][:, :] for n in ("cs", "sn"))
                did(v.tensor_copy(un[0][:, :], x))
                did(v.tensor_copy(un[1][:, :], y))
                for _ in range(4):
                    tt(t["t0"], un[0][:, :], un[0][:, :], ALU.mult)
                    tt(t["t1"], un[1][:, :], un[1][:, :], ALU.mult)
                    tt(t["nr"], un[0][:, :], un[1][:, :], ALU.mult)
                    tt(un[0][:, :], t["t0"], t["t1"], ALU.subtract)
                    did(v.tensor_scalar(un[1][:, :], t["nr"], 2.0, None, ALU.mult))
                for n in range(2):
                    did(v.memset(rot[n][:, :, 0:1], 1.0 - n))
                    did(v.tensor_copy(rot[n][:, :, 1:2], un[n][:, :].unsqueeze(2)))
                m = 1
                while m < NC:
                    k = min(m, NC - 1 - m)
                    if k <= 0:
                        break
                    a = [x[:, :, 1:k + 1] for x in rot]
                    b = [x[:, :, m:m + 1].to_broadcast([P, NG_S, k]) for x in rot]
                    o = [x[:, :, m + 1:m + k + 1] for x in rot]
                    x, y = (pt[n][:, 0:NG_S * k].rearrange("p (g m) -> p g m", m=k) for n in range(2))
                    tt(x, a[0], b[0], ALU.mult)
                    tt(y, a[1], b[1], ALU.mult)
                    tt(o[0], x, y, ALU.subtract)
                    tt(x, a[0], b[1], ALU.mult)
                    tt(y, a[1], b[0], ALU.mult)
                    tt(o[1], x, y, ALU.add)
                    m *= 2
                did(v.tensor_scalar(rot[1][bot, :, :], rot[1][bot, :, :], -1.0, None, ALU.mult))


def stage_ssm(nc, g, A, S):
    with Ctx(nc) as c:
        u = c.sb("u_chunks", [P, LC, SW])
        y = c.sb("y_chunks", [P, LC, SW])
        rec = [c.sb(f"rec{b}", [P, REC]) for b in range(2)]
        ug = [c.sb(f"ug{b}", [P, LC, CH_S]) for b in range(2)]
        uT = [c.sb(f"uT{b}", [P, 2, P]) for b in range(2)]
        t = [[c.sb(f"rt{b}{n}", [P, NC]) for n in range(4)] for b in range(2)]
        hin = [c.sb(f"hin{b}", [P, 2, NC + 1]) for b in range(2)]
        psU = [c.ps(f"psU{b}", [P, 2, P]) for b in range(2)]
        psB = [c.ps(f"psB{b}", [P, 2, NC]) for b in range(2)]
        psY = [c.ps(f"psY{b}", [P, LC, CH_S]) for b in range(2)]
        u_in, rec_in = c.sem("u_in"), [c.sem(f"rec_in{b}") for b in range(2)]
        ugd, utp, utd = c.sem("ug_done"), c.sem("uT_psum"), c.sem("uT_done")
        b_ps, h_done, y_ps, y_done = c.sem("b_psum"), c.sem("h_done"), c.sem("y_psum"), c.sem("y_done")
        z0, rs, y_st = c.sem("hin_zero"), c.sem("rec_step"), c.sem("y_st")
        rot, rho = g["rot"], g["rho"]
        with nc.Block() as block:
            @block.sync
            def _(sp):
                uv = S["qkvu"].rearrange("(j s) n -> j s n", s=LC)
                sp.dma_start(u[:, :, :], uv[:, :, 3 * AW:]).then_inc(u_in, 16)
                for b in range(2):
                    sp.dma_start(rec[b][:, :], S["rec"][b]).then_inc(rec_in[b], 16)
                with sp.Fori(1, NG_S // 2) as i:
                    for b in range(2):
                        sp.wait_ge(y_ps, 2 * i + b - 1)
                        sp.dma_start(rec[b][:, :], S["rec"][ds(2 * i + b, 1)].rearrange("a p n -> (a p) n")).then_inc(rec_in[b], 16)
                sp.wait_ge(y_done, NG_S)
                sp.dma_start(S["y"].rearrange("(j s) n -> j s n", s=LC), y[:, :, :]).then_inc(y_st, 16)
                sp.wait_ge(y_st, 16)

            def pairs(eng, body):
                for b in range(2):
                    body(b, b, True, 0)
                with eng.Fori(1, NG_S // 2) as i:
                    for b in range(2):
                        body(2 * i + b, b, False, i)

            @block.gpsimd
            def _(pool):
                pool.wait_ge(u_in, 16)

                def body(n, b, first, i):
                    if not first:
                        pool.wait_ge(utp, n - 1)
                    nc.gpsimd.tensor_copy(ug[b][:, :, :], u[:, :, ds(CH_S * n, CH_S)]).then_inc(ugd, 1)
                pairs(pool, body)

            @block.tensor
            def _(pe):
                def front(n, b, first, i):
                    pe.wait_ge(ugd, n + 1)
                    if not first:
                        pe.wait_ge(utd, n - 1)
                    for k in range(2):
                        mm = nc.tensor.transpose(psU[b][:, k, :], ug[b][:, 8 * k:8 * k + 8, :].rearrange("p s c -> p (s c)"),
                                                 g["ident"][:, :])
                    mm.then_inc(utp, 1)
                    pe.wait_ge(utd, n + 1)
                    pe.wait_ge(rec_in[b], 16 * i + 16)
                    if not first:
                        pe.wait_ge(h_done, n - 1)
                    for r in range(2):
                        for k in range(2):
                            mm = nc.tensor.matmul(psB[b][:, r, :], rec[b][:, 192 * k + 64 * r:192 * k + 64 * r + P],
                                                  uT[b][:, k, :], start=k == 0, stop=k == 1)
                    mm.then_inc(b_ps, 1)

                def back(n, b, first, i):
                    if not first:
                        pe.wait_ge(y_done, n - 1)
                    o = psY[b][:, :, :].rearrange("p s c -> p (s c)")
                    nc.tensor.matmul(o, uT[b][:, 0, :], rec[b][:, 896:1152], start=True, stop=False, skip_group_check=True)
                    nc.tensor.matmul(o[:, P:], uT[b][:, 1, :], rec[b][:, 1152 + P:1408], start=False, stop=False,
                                     skip_group_check=True)
                    pe.wait_ge(h_done, n + 1)
                    for r in range(2):
                        mm = nc.tensor.matmul(o, hin[b][:, r, 0:NC], rec[b][:, 384 + 256 * r:640 + 256 * r],
                                              start=False, stop=r == 1, skip_group_check=True)
                    mm.then_inc(y_ps, 1)

                front(0, 0, True, 0)
                front(1, 1, True, 0)
                back(0, 0, True, 0)
                with pe.Fori(1, NG_S // 2) as i:
                    front(2 * i, 0, False, i)
                    back(2 * i - 1, 1, False, i)
                    front(2 * i + 1, 1, False, i)
                    back(2 * i, 0, False, i)
                back(NG_S - 1, 1, False, 0)

            @block.scalar
            def _(act):
                def evac(n, b, first, i):
                    act.wait_ge(utp, n + 1)
                    if not first:
                        act.wait_ge(y_ps, n - 1)
                    nc.scalar.activation(uT[b][:, :, :], psU[b][:, :, :], ACT.Copy).then_inc(utd, 1)

                def gelu(n, b, first, i):
                    act.wait_ge(y_ps, n + 1)
                    nc.scalar.activation(y[:, :, ds(CH_S * n, CH_S)], psY[b][:, :, :], ACT.Gelu_apprx_tanh).then_inc(y_done, 1)

                evac(0, 0, True, 0)
                evac(1, 1, True, 0)
                gelu(0, 0, True, 0)
                with act.Fori(1, NG_S // 2) as i:
                    evac(2 * i, 0, False, i)
                    gelu(2 * i - 1, 1, False, i)
                    evac(2 * i + 1, 1, False, i)
                    gelu(2 * i, 0, False, i)
                gelu(NG_S - 1, 1, False, 0)

            @block.vector
            def _(v):
                for b in range(2):
                    v.memset(hin[b][:, :, 0:1], 0.0).then_inc(z0, 1)

                def body(n, b, first, i):
                    v.wait_ge(b_ps, n + 1)
                    x = [a[:, :] for a in t[b]]
                    rr, ri = (r[:, ds(n, 1), :].rearrange("p a j -> p (a j)") for r in rot)
                    v.tensor_tensor(x[0], psB[b][:, 0, :], rr, ALU.mult).then_inc(rs, 1)
                    v.tensor_tensor(x[1], psB[b][:, 1, :], ri, ALU.mult).then_inc(rs, 1)
                    v.wait_ge(rs, 4 * n + 2)
                    v.tensor_tensor(x[2], x[0], x[1], ALU.add).then_inc(rs, 1)
                    v.wait_ge(rs, 4 * n + 3)
                    v.tensor_tensor_scan(x[3], rho[:, ds(n, 1)].to_broadcast([P, NC]), x[2], 0.0, ALU.mult, ALU.add).then_inc(rs, 1)
                    v.wait_ge(rs, 4 * n + 4)
                    if not first:
                        v.wait_ge(y_ps, n - 1)
                    v.tensor_tensor(hin[b][:, 0, 1:], x[3], rr, ALU.mult)
                    v.tensor_tensor(hin[b][:, 1, 1:], x[3], ri, ALU.mult).then_inc(h_done, 1)
                pairs(v, body)


NR = NGR + NE


def stage_merge(nc, g, A, S):
    KA = AW // P
    with Ctx(nc) as c:
        wA = c.sb("w_branch_a", [P, KA, D])
        wS = c.sb("w_branch_s", [P, KA, D])
        wO = c.sb("w_out_sb", [P, KD, D])
        wG = c.sb("w_glu_sb", [P, KA, SW])
        wR = c.sb("w_router", [P, KD, NR])
        bG = c.sb("b_glu_row", [P, SW])
        bR = c.sb("b_router", [P, NR])
        o = [c.sb(f"o_in{b}", [P, 3, AW + 2 * NH]) for b in range(2)]
        y = [c.sb(f"y_in{b}", [P, SW]) for b in range(2)]
        gt = [c.sb(f"gt_in{b}", [P, 2, D]) for b in range(2)]
        x = [c.sb(f"x_in{b}", [P, D]) for b in range(2)]
        acc = [c.sb(f"acc{n}", [P, NH, HD]) for n in range(3)]
        at = c.sb("attn", [P, NH, HD])
        sm = c.sb("ssm_out", [P, SW])
        z = c.sb("glu_z", [P, SW])
        ez = c.sb("glu_e", [P, SW])
        mg = [c.sb(f"mg{n}", [P, D]) for n in range(2)]
        x1 = [c.sb(f"x1_{b}", [P, D]) for b in range(2)]
        xn = [c.sb(f"xn2_{b}", [P, D]) for b in range(2)]
        junk = c.sb("junk_m", [P, D])
        yT, aT, sT = (c.sb(n, [P, KA, P]) for n in ("yT", "aT", "sT"))
        mT = c.sb("mT", [P, KD, P])
        xT = c.sb("x2T", [P, KD, P])
        mx = c.sb("mx_all", [P, NH])
        df = c.sb("m_less", [P, 3, NH])
        wt = c.sb("pat_w", [P, 3, NH])
        wl = c.sb("pat_wl", [P, 3, NH])
        ll = c.sb("pat_l", [P, NH])
        li = c.sb("pat_li", [P, NH])
        wn = c.sb("pat_wn", [P, 3, NH])
        ssq = c.sb("ssq", [P, 3])
        st = {n: c.sb(f"st_{n}", [P, 1]) for n in ("s", "ms", "rt", "rstd", "ms2", "rt2", "rstd2")}
        psT = [c.ps(f"psT{b}", [P, 4, P]) for b in range(2)]
        psA = c.ps("psBA", [P, 2, 512])
        psS = c.ps("psBS", [P, 2, 512])
        psW = c.ps("psW", [P, 2, 512])
        w_in = c.sem("mw_in")
        o_in, y_in, g_in, x_in = ([c.sem(f"{n}{b}") for b in range(2)] for n in ("mo_in", "my_in", "mg_in", "mx_in"))
        y_tp, a_tp, s_tp, m_tp, x_tp = (c.sem(n) for n in ("y_tp", "a_tp", "s_tp", "m_tp", "x_tp"))
        y_T, a_T, s_T, m_T, x_T = (c.sem(n) for n in ("y_T", "a_T", "s_T", "m_T", "x_T"))
        glu_mm, a_mm, s_mm, w_mm, r_mm = (c.sem(n) for n in ("glu_mm", "a_mm", "s_mm", "w_mm", "r_mm"))
        cmb, cw, at_d = c.sem("comb_step"), c.sem("comb_exp"), c.sem("attn_done")
        z_d, ez_d, gl, s_d = c.sem("z_done"), c.sem("ez_done"), c.sem("glu_step"), c.sem("ssm_gated")
        mgs, m_d = c.sem("merge_step"), c.sem("merged")
        sq, ms_d, rt_d, x1s, x1_d, xn_d = (c.sem(n) for n in ("msq", "mms", "mrt", "x1_step", "x1_done", "xn2_done"))
        lg_d = c.sem("logits_done")
        x1_st, xn_st = ([c.sem(f"{n}{b}") for b in range(2)] for n in ("x1_st", "xn2_st"))
        NSTEP = NT + 2

        def real(t):
            return not isinstance(t, int) or 0 <= t < NT

        def past(t, n):
            return not isinstance(t, int) or t >= n

        def steps(eng, body):
            for s in range(2):
                body(s, 0, s)
            with eng.Fori(1, NT // 2 - 1) as i:
                for b in range(2):
                    body(2 * i + b, i, b)
            for s in range(NT - 2, NSTEP):
                body(s, s // 2, s % 2)

        def tile(dram, t):
            return dram.rearrange("(t p) n -> t p n", p=P)[ds(t, 1)].rearrange("a p n -> (a p) n")

        with nc.Block() as block:
            @block.sync
            def _(sp):
                def load_oyg(t, b):
                    for n in range(3):
                        sp.dma_start(o[b][:, n, :], tile(S["o"][n], t)).then_inc(o_in[b], 16)
                    sp.dma_start(y[b][:, :], tile(S["y"], t)).then_inc(y_in[b], 16)
                    sp.dma_start(gt[b][:, :, :].rearrange("p a n -> p (a n)"), tile(S["gates"], t)).then_inc(g_in[b], 16)

                def load_x(t, b):
                    sp.dma_start(x[b][:, :], tile(A["x"][0], t)).then_inc(x_in[b], 16)

                sp.dma_start(wG[:, :, :], A["w_glu"][0].rearrange("(k p) n -> p k n", p=P)).then_inc(w_in, 16)
                sp.dma_start(bG[:, :], A["b_glu"].to_broadcast([P, SW])).then_inc(w_in, 16)
                load_oyg(0, 0)
                for dst, name in ((wA, "w_branch_attn"), (wS, "w_branch_ssm")):
                    sp.dma_start(dst[:, :, :], A[name][0].rearrange("(k p) n -> p k n", p=P)).then_inc(w_in, 16)
                load_oyg(1, 1)
                load_x(0, 0)
                sp.dma_start(wO[:, :, :], A["w_out"][0].rearrange("(k p) n -> p k n", p=P)).then_inc(w_in, 16)
                sp.dma_start(wR[:, :, 0:NGR], A["w_router_group"][0].rearrange("(k p) n -> p k n", p=P)).then_inc(w_in, 16)
                sp.dma_start(wR[:, :, NGR:], A["w_router_expert"][0].rearrange("(k p) n -> p k n", p=P)).then_inc(w_in, 16)
                sp.dma_start(bR[:, 0:NGR], A["b_router_group"].to_broadcast([P, NGR])).then_inc(w_in, 16)
                sp.dma_start(bR[:, NGR:], A["b_router_expert"].to_broadcast([P, NE])).then_inc(w_in, 16)

                def body(s, i, b):
                    if real(s - 1):
                        sp.wait_ge(x1_d, s)
                        sp.dma_start(tile(S["x1"], s - 1), x1[1 - b][:, :]).then_inc(x1_st[1 - b], 16)
                    if real(s + 1):
                        load_x(s + 1, 1 - b)
                    if real(s - 1):
                        sp.wait_ge(xn_d, s)
                        sp.dma_start(tile(S["xn2"], s - 1), xn[1 - b][:, :]).then_inc(xn_st[1 - b], 16)
                    if real(s) and real(s + 2):
                        sp.wait_ge(at_d, s + 1)
                        sp.wait_ge(s_d, s + 1)
                        sp.wait_ge(m_d, s + 1)
                        load_oyg(s + 2, b)
                steps(sp, body)
                for b in range(2):
                    sp.wait_ge(x1_st[b], 16 * NT // 2)
                    sp.wait_ge(xn_st[b], 16 * NT // 2)

            @block.tensor
            def _(pe):
                def turn(bank, src, sem):
                    n = src.shape[1] // P
                    for k in range(n):
                        mm = nc.tensor.transpose(psT[bank][:, k, :], src[:, k * P:(k + 1) * P], g["ident"][:, :])
                    mm.then_inc(sem, 1)

                def product(o_, xT_, w_, width):
                    for h in range((width + 511) // 512):
                        n = min(512, width - 512 * h)
                        for k in range(w_.shape[1]):
                            mm = nc.tensor.matmul(o_[:, h, 0:n], xT_[:, k, :], w_[:, k, 512 * h:512 * h + n],
                                                  start=k == 0, stop=k == w_.shape[1] - 1)
                    return mm

                def body(s, i, b):
                    if real(s):
                        pe.wait_ge(y_in[b], 16 * i + 16)
                        if past(s, 1):
                            pe.wait_ge(s_T, s)
                        turn(0, y[b], y_tp)
                        pe.wait_ge(at_d, s + 1)
                        if past(s, 2):
                            pe.wait_ge(m_T, 2 * s - 2)
                        turn(1, at[:, :, :].rearrange("p h d -> p (h d)"), a_tp)
                        pe.wait_ge(y_T, s + 1)
                        if past(s, 1):
                            pe.wait_ge(m_d, s)
                        product(psS, yT, wG, SW).then_inc(glu_mm, 1)
                        pe.wait_ge(a_T, s + 1)
                        product(psA, aT, wA, D).then_inc(a_mm, 1)
                    if real(s - 2):
                        pe.wait_ge(xn_d, s - 1)
                        if real(s):
                            pe.wait_ge(y_T, s + 1)
                        else:
                            pe.wait_ge(s_T, NT)
                            pe.wait_ge(m_T, 2 * (s - 1))
                            pe.wait_ge(m_d, NT)
                        turn(0, xn[b][:, 0:512], x_tp)
                        if real(s):
                            pe.wait_ge(a_T, s + 1)
                        turn(1, xn[b][:, 512:1024], x_tp)
                        pe.wait_ge(x_T, 2 * (s - 1))
                        for k in range(KD):
                            mm = nc.tensor.matmul(psS[:, 1, 0:NR], xT[:, k, :], wR[:, k, :], start=k == 0, stop=k == KD - 1)
                        mm.then_inc(r_mm, 1)
                    if real(s - 1):
                        pe.wait_ge(m_d, s)
                        if past(s, 2):
                            pe.wait_ge(x_T, 2 * (s - 1))
                        else:
                            pe.wait_ge(y_T, s + 1)
                            pe.wait_ge(a_T, s + 1)
                        turn(0, mg[0][:, 0:512], m_tp)
                        turn(1, mg[0][:, 512:1024], m_tp)
                        pe.wait_ge(m_T, 2 * s)
                        if past(s, 2):
                            pe.wait_ge(x1_d, s - 1)
                        product(psW, mT, wO, D).then_inc(w_mm, 1)
                    if real(s):
                        pe.wait_ge(s_d, s + 1)
                        if past(s, 1):
                            pe.wait_ge(m_T, 2 * s)
                        else:
                            pe.wait_ge(y_T, s + 1)
                        turn(0, sm, s_tp)
                        pe.wait_ge(s_T, s + 1)
                        if past(s, 2):
                            pe.wait_ge(lg_d, s - 1)
                        product(psS, sT, wS, D).then_inc(s_mm, 1)

                pe.wait_ge(w_in, 16 * 9)
                steps(pe, body)

            @block.scalar
            def _(act):
                def leave(bank, dst, tp, n_tp, used, n_used, done):
                    act.wait_ge(tp, n_tp)
                    if n_used is not None:
                        act.wait_ge(used, n_used)
                    nc.scalar.activation(dst, psT[bank][:, :, :], ACT.Copy).then_inc(done, 1)

                def weights(t):
                    act.wait_ge(cmb, 12 * t + 3)
                    nc.scalar.activation(wt[:, :, :], df[:, :, :], ACT.Exp).then_inc(cw, 1)

                def root(dst, src):
                    nc.scalar.activation(dst[:, :], src[:, :], ACT.Sqrt).then_inc(rt_d, 1)

                def body(s, i, b):
                    if real(s):
                        leave(0, yT[:, :, :], y_tp, s + 1, glu_mm, s if past(s, 1) else None, y_T)
                        leave(1, aT[:, :, :], a_tp, s + 1, a_mm, s if past(s, 1) else None, a_T)
                        act.wait_ge(z_d, s + 1)
                        nc.scalar.activation(ez[:, :], z[:, :], ACT.Exp, scale=-1.0).then_inc(ez_d, 1)
                    if real(s - 2):
                        for h in range(2):
                            act.wait_ge(x_tp, 2 * (s - 2) + h + 1)
                            if past(s, 3) and h == 0:
                                act.wait_ge(r_mm, s - 2)
                            for k in range(4):
                                kk = 4 * h + k
                                e = nc.scalar.activation(xT[:, kk, :], psT[h][:, k, :], ACT.Identity,
                                                         bias=g["bcol"][:, 1, kk:kk + 1], scale=g["acol"][:, 1, kk:kk + 1])
                            e.then_inc(x_T, 1)
                    if real(s + 1) and real(s):
                        weights(s + 1)
                    if real(s - 1):
                        for h in range(2):
                            leave(h, mT[:, 4 * h:4 * h + 4, :], m_tp, 2 * (s - 1) + h + 1, w_mm, s - 1 if past(s, 2) else None, m_T)
                    if real(s):
                        leave(0, sT[:, :, :], s_tp, s + 1, s_mm, s if past(s, 1) else None, s_T)
                    if real(s - 1):
                        act.wait_ge(w_mm, s)
                        if past(s, 2):
                            act.wait_ge(sq, 2 * (s - 1))
                            act.wait_ge(ms_d, 2 * (s - 1))
                        nc.scalar.activation(junk[:, :], psW[:, :, :].rearrange("p a n -> p (a n)"), ACT.Square,
                                             accum_out=ssq[:, 0:1]).then_inc(sq, 1)
                        act.wait_ge(ms_d, 2 * s - 1)
                        root(st["rt"], st["ms"])
                        act.wait_ge(x1_d, s)
                        act.wait_ge(sq, 2 * s - 1)
                        nc.scalar.activation(junk[:, :], x1[1 - b][:, :], ACT.Square, accum_out=ssq[:, 1:2]).then_inc(sq, 1)
                        act.wait_ge(ms_d, 2 * s)
                        root(st["rt2"], st["ms2"])

                weights(0)
                steps(act, body)

            @block.vector
            def _(v):
                def did(ins, sem, n):
                    ins.then_inc(sem, 1)
                    v.wait_ge(sem, n)

                def combine(t, i, b):
                    n = 12 * t
                    v.wait_ge(o_in[b], 48 * i + 48)
                    m, l = o[b][:, :, AW:AW + NH], o[b][:, :, AW + NH:]
                    did(v.tensor_tensor(mx[:, :], m[:, 0, :], m[:, 1, :], ALU.max), cmb, n + 1)
                    did(v.tensor_tensor(mx[:, :], mx[:, :], m[:, 2, :], ALU.max), cmb, n + 2)
                    did(v.tensor_tensor(df[:, :, :], m, mx[:, :].unsqueeze(1).to_broadcast([P, 3, NH]), ALU.subtract), cmb, n + 3)
                    v.wait_ge(cw, t + 1)
                    did(v.tensor_tensor(wl[:, :, :], wt[:, :, :], l, ALU.mult), cmb, n + 4)
                    did(v.tensor_tensor(ll[:, :], wl[:, 0, :], wl[:, 1, :], ALU.add), cmb, n + 5)
                    did(v.tensor_tensor(ll[:, :], ll[:, :], wl[:, 2, :], ALU.add), cmb, n + 6)
                    did(v.reciprocal(li[:, :], ll[:, :]), cmb, n + 7)
                    did(v.tensor_tensor(wn[:, :, :], wt[:, :, :], li[:, :].unsqueeze(1).to_broadcast([P, 3, NH]), ALU.mult), cmb, n + 8)
                    for p in range(3):
                        v.tensor_tensor(acc[p][:, :, :], o[b][:, p, 0:AW].rearrange("p (h d) -> p h d", d=HD),
                                        wn[:, p, :].unsqueeze(2).to_broadcast([P, NH, HD]), ALU.mult).then_inc(cmb, 1)
                    v.wait_ge(cmb, n + 11)
                    did(v.tensor_tensor(acc[0][:, :, :], acc[0][:, :, :], acc[1][:, :, :], ALU.add), cmb, n + 12)
                    if past(t, 1):
                        v.wait_ge(a_tp, t)
                    v.tensor_tensor(at[:, :, :], acc[0][:, :, :], acc[2][:, :, :], ALU.add).then_inc(at_d, 1)

                def gated(t, b):
                    v.wait_ge(glu_mm, t + 1)
                    if past(t, 1):
                        v.wait_ge(ez_d, t)
                    v.tensor_tensor(z[:, :], psS[:, 0, :], bG[:, :], ALU.add).then_inc(z_d, 1)
                    v.wait_ge(ez_d, t + 1)
                    did(v.tensor_scalar(ez[:, :], ez[:, :], 1.0, None, ALU.add), gl, 2 * t + 1)
                    did(v.reciprocal(ez[:, :], ez[:, :]), gl, 2 * t + 2)
                    if past(t, 1):
                        v.wait_ge(s_tp, t)
                    v.tensor_tensor(sm[:, :], ez[:, :], y[b][:, :], ALU.mult).then_inc(s_d, 1)

                def logits(t):
                    v.wait_ge(r_mm, t + 1)
                    v.tensor_tensor(g["logits"][:, ds(t, 1), :].rearrange("p a n -> p (a n)"), psS[:, 1, 0:NR], bR[:, :],
                                    ALU.add).then_inc(lg_d, 1)

                def residual(t, i, b):
                    v.wait_ge(sq, 2 * t + 1)
                    if past(t, 1):
                        v.wait_ge(rt_d, 2 * t)
                    v.tensor_scalar(st["ms"][:, :], ssq[:, 0:1], 1.0 / D, EPS, ALU.mult, ALU.add).then_inc(ms_d, 1)
                    v.wait_ge(rt_d, 2 * t + 1)
                    did(v.reciprocal(st["rstd"][:, :], st["rt"][:, :]), x1s, 3 * t + 1)
                    if past(t, 2):
                        v.wait_ge(x1_st[b], 16 * i)
                    v.wait_ge(x_in[b], 16 * i + 16)
                    did(v.scalar_tensor_tensor(out=x1[b][:, :], in0=psW[:, :, :].rearrange("p a n -> p (a n)"),
                                               scalar=st["rstd"][:, 0:1], in1=g["grow"][:, 0, :], op0=ALU.mult, op1=ALU.mult),
                        x1s, 3 * t + 2)
                    v.tensor_tensor(x1[b][:, :], x1[b][:, :], x[b][:, :], ALU.add).then_inc(x1_d, 1)
                    v.wait_ge(sq, 2 * t + 2)
                    v.tensor_scalar(st["ms2"][:, :], ssq[:, 1:2], 1.0 / D, EPS, ALU.mult, ALU.add).then_inc(ms_d, 1)
                    v.wait_ge(rt_d, 2 * t + 2)
                    did(v.reciprocal(st["rstd2"][:, :], st["rt2"][:, :]), x1s, 3 * t + 3)
                    if past(t, 2):
                        v.wait_ge(xn_st[b], 16 * i)
                        v.wait_ge(x_tp, 2 * t - 2)
                    v.tensor_scalar(xn[b][:, :], x1[b][:, :], st["rstd2"][:, 0:1], None, ALU.mult).then_inc(xn_d, 1)

                def merge(t, i, b):
                    v.wait_ge(s_mm, t + 1)
                    v.wait_ge(a_mm, t + 1)
                    v.wait_ge(g_in[b], 16 * i + 16)
                    if past(t, 1):
                        v.wait_ge(m_tp, 2 * t)
                    flat = [p_[:, :, :].rearrange("p a n -> p (a n)") for p_ in (psA, psS)]
                    v.tensor_tensor(mg[0][:, :], flat[0], gt[b][:, 0, :], ALU.mult).then_inc(mgs, 1)
                    v.tensor_tensor(mg[1][:, :], flat[1], gt[b][:, 1, :], ALU.mult).then_inc(mgs, 1)
                    v.wait_ge(mgs, 2 * t + 2)
                    v.tensor_tensor(mg[0][:, :], mg[0][:, :], mg[1][:, :], ALU.add).then_inc(m_d, 1)

                def body(s, i, b):
                    if real(s):
                        gated(s, b)
                    if real(s - 2):
                        logits(s - 2)
                    if real(s + 1) and real(s):
                        combine(s + 1, i + b, 1 - b)
                    if real(s - 1):
                        residual(s - 1, i - 1 + b, 1 - b)
                    if real(s):
                        merge(s, i, b)

                v.wait_ge(w_in, 16 * 9)
                combine(0, 0, 0)
                steps(v, body)


def stage_route(nc, g, A, S):
    with Ctx(nc) as c:
        def sb(name, shape, dt=F32):
            return c.sb("r_" + name, shape, dt)

        lg = g["logits"]
        w8, w8i = sb("w8", [P, EPG]), sb("w8i", [P, EPG], I32)
        bi, bf = sb("bi", [P, NBLK], I32), sb("bf", [P, NBLK])
        tok = sb("tok", [P, NT], I32)
        tri, one = sb("tri", [P, P]), sb("one", [P, P])
        gm, gs, gate = (sb(n, [P, NT]) for n in ("gm", "gs", "gate"))
        gd, ohg, gt = (sb(n, [P, NT, NGR]) for n in ("gd", "ohg", "gt"))
        fm = sb("fm", [P, NT])
        full = sb("full", [P, NT, NGR, EPG])
        ein, e2, ohk, et = sb("ein", [P, NT, EPG]), sb("e2", [P, NT, EPG]), [sb(f"ohk{k}", [P, NT, EPG]) for k in range(2)], sb("et", [P, NT, EPG])
        v12 = [sb(f"v{k}", [P, NT]) for k in range(2)]
        dv, p1 = sb("dv", [P, NT]), sb("p1", [P, NT])
        OH = [sb(f"OH{k}", [P, NT, NGR, EPG]) for k in range(2)]
        oh = sb("OHs", [P, NT, NE])
        tot = sb("tot", [P, NT, NE])
        pre = sb("pre", [P, NT + 1, NE])
        rank = sb("rank", [P, NT, NE])
        nb, cum, st0 = (sb(n, [P, NE]) for n in ("nb", "cum", "st0"))
        cmp_ = sb("cmp", [P, NBLK, NE])
        be, nr, rn, par = (sb(n, [P, NBLK]) for n in ("be", "nr", "rn", "par"))
        npf = sb("npf", [P, 1])
        dest_f = sb("dest_f", [P, NT])
        zi = sb("zi", [P, NBLK + 1], I32)
        ps = [c.ps(f"ps_rank{n}", [P, 512]) for n in range(2)]
        io, tri0 = c.sem("r_iota"), c.sem("r_tri0")
        st_, ex, exd, mm = c.sem("r_step"), c.sem("r_exp_in"), c.sem("r_exp"), c.sem("rank_mm")
        ohd, z_st, sc, ready, tb = c.sem("r_oh"), c.sem("r_zero_st"), c.sem("r_scatter"), c.sem("r_dest"), c.sem("r_table")
        zd = c.sem("r_zero")
        rows = S["row_tok"]

        with nc.Block() as block:
            @block.gpsimd
            def _(pool):
                nc.gpsimd.iota(w8i[:, :], [[-1, EPG]], base=EPG, channel_multiplier=0).then_inc(io, 1)
                nc.gpsimd.iota(bi[:, :], [[1, NBLK]], base=0, channel_multiplier=0).then_inc(io, 1)
                nc.gpsimd.iota(tok[:, :], [[P, NT]], base=0, channel_multiplier=1).then_inc(io, 1)
                nc.gpsimd.memset(one[:, :], 1.0).then_inc(io, 1)
                nc.gpsimd.memset(tri[:, :], 1.0).then_inc(tri0, 1)
                pool.wait_ge(tri0, 1)
                nc.gpsimd.affine_select(out=tri[:, :], in_=tri[:, :], compare_op=ALU.is_gt, fill=0.0, base=0,
                                        pattern=[[1, P]], channel_multiplier=-1).then_inc(io, 1)
                pool.wait_ge(io, 5)
                pool.wait_ge(z_st, 16)
                pool.wait_ge(ready, 2)
                for k in range(2):
                    for t in range(NT):
                        pool.indirect_dma_start(rows, bass.IndirectOffsetOnAxis(g["dest"][:, k, t:t + 1], 0),
                                                tok[:, t:t + 1], None).then_inc(sc, 16)
                pool.wait_ge(sc, 16 * 2 * NT)

            @block.sync
            def _(sp):
                sp.wait_ge(zd, 1)
                sp.dma_start(rows.rearrange("(b p) a -> p (b a)", p=P), zi[:, :],
                             allow_slow_non_contiguous=True).then_inc(z_st, 16)
                sp.wait_ge(sc, 16 * 2 * NT)
                sp.dma_start(g["rowtok"][:, :], rows.rearrange("(b p) a -> p (b a)", p=P),
                             allow_slow_non_contiguous=True).then_inc(tb, 16)
                sp.wait_ge(tb, 16)

            @block.scalar
            def _(act):
                act.wait_ge(ex, 1)
                nc.scalar.activation(gd[:, :, :], gd[:, :, :], ACT.Exp).then_inc(exd, 1)
                act.wait_ge(ex, 2)
                nc.scalar.activation(dv[:, :], dv[:, :], ACT.Exp).then_inc(exd, 1)

            @block.tensor
            def _(pe):
                pe.wait_ge(io, 5)
                pe.wait_ge(ohd, 1)
                f = oh[:, :, :].rearrange("p t e -> p (t e)")
                nc.tensor.matmul(ps[0][:, :], tri[:, :], f, start=True, stop=True).then_inc(mm, 1)
                nc.tensor.matmul(ps[1][:, :], one[:, :], f, start=True, stop=True).then_inc(mm, 1)

            @block.vector
            def _(v):
                n_ = [0]

                def did(ins):
                    n_[0] += 1
                    ins.then_inc(st_, 1)
                    v.wait_ge(st_, n_[0])

                def tt(o, a, b, op):
                    did(v.tensor_tensor(o, a, b, op))

                def ts(o, a, s1, s2, op0, op1=None):
                    did(v.tensor_scalar(o, a, s1, s2, op0, op1) if op1 is not None else v.tensor_scalar(o, a, s1, None, op0))

                def floor(o, a, scale, off):
                    big = 1.5 * 2 ** 23
                    ts(o, a, scale, off, ALU.mult, ALU.add)
                    ts(o, o, big, None, ALU.add)
                    ts(o, o, big, None, ALU.subtract)

                def first_max(o, vals, top, tmp, k):
                    w = w8[:, EPG - k:].unsqueeze(1).to_broadcast([P, NT, k])
                    did(v.tensor_reduce(top, vals, AX_X, ALU.max))
                    tt(tmp, vals, top.unsqueeze(2).to_broadcast([P, NT, k]), ALU.is_equal)
                    tt(tmp, tmp, w, ALU.mult)
                    did(v.tensor_reduce(fm[:, :], tmp, AX_X, ALU.max))
                    tt(o, w, fm[:, :].unsqueeze(2).to_broadcast([P, NT, k]), ALU.is_equal)

                v.memset(zi[:, :], 0).then_inc(zd, 1)
                v.wait_ge(io, 5)
                did(v.tensor_copy(w8[:, :], w8i[:, :]))
                did(v.tensor_copy(bf[:, :], bi[:, :]))
                gl, el = lg[:, :, 0:NGR], lg[:, :, NGR:].rearrange("p t (a b) -> p t a b", b=EPG)
                first_max(ohg[:, :, :], gl, gm[:, :], gt[:, :, :], NGR)
                v.tensor_tensor(gd[:, :, :], gl, gm[:, :].unsqueeze(2).to_broadcast([P, NT, NGR]), ALU.subtract).then_inc(ex, 1)
                tt(full[:, :, :, :], el, ohg[:, :, :].unsqueeze(3).to_broadcast([P, NT, NGR, EPG]), ALU.mult)
                tt(ein[:, :, :], full[:, :, 0, :], full[:, :, 1, :], ALU.add)
                tt(et[:, :, :], full[:, :, 2, :], full[:, :, 3, :], ALU.add)
                tt(ein[:, :, :], ein[:, :, :], et[:, :, :], ALU.add)
                first_max(ohk[0][:, :, :], ein[:, :, :], v12[0][:, :], et[:, :, :], EPG)
                did(v.scalar_tensor_tensor(out=e2[:, :, :], in0=ohk[0][:, :, :], scalar=-3e38, in1=ein[:, :, :],
                                           op0=ALU.mult, op1=ALU.add))
                first_max(ohk[1][:, :, :], e2[:, :, :], v12[1][:, :], et[:, :, :], EPG)
                for k in range(2):
                    tt(OH[k][:, :, :, :], ohg[:, :, :].unsqueeze(3).to_broadcast([P, NT, NGR, EPG]),
                       ohk[k][:, :, :].unsqueeze(2).to_broadcast([P, NT, NGR, EPG]), ALU.mult)
                flat = [x[:, :, :, :].rearrange("p t a b -> p t (a b)") for x in OH]
                tt(oh[:, :, :], flat[0], flat[1], ALU.add)
                v.engine_nop().then_inc(ohd, 1)
                tt(dv[:, :], v12[1][:, :], v12[0][:, :], ALU.subtract)
                v.engine_nop().then_inc(ex, 1)
                v.wait_ge(exd, 1)
                did(v.tensor_reduce(gs[:, :], gd[:, :, :], AX_X, ALU.add))
                did(v.reciprocal(gate[:, :], gs[:, :]))
                v.wait_ge(exd, 2)
                ts(p1[:, :], dv[:, :], 1.0, None, ALU.add)
                did(v.reciprocal(p1[:, :], p1[:, :]))
                tt(g["wgt"][:, 0, :], p1[:, :], gate[:, :], ALU.mult)
                tt(g["wgt"][:, 1, :], g["wgt"][:, 0, :], dv[:, :], ALU.mult)
                v.wait_ge(mm, 2)
                did(v.tensor_copy(tot[:, :, :].rearrange("p t e -> p (t e)"), ps[1][:, :]))
                did(v.memset(pre[:, 0, :], 0.0))
                for t in range(NT):
                    tt(pre[:, t + 1, :], pre[:, t, :], tot[:, t, :], ALU.add)
                tt(rank[:, :, :].rearrange("p t e -> p (t e)"), ps[0][:, :], pre[:, 0:NT, :].rearrange("p t e -> p (t e)"), ALU.add)
                floor(nb[:, :], pre[:, NT, :], 1.0 / P, (P - 1) / P - 0.5 + 0.5 / P)
                did(v.tensor_tensor_scan(cum[:, :], one[:, 0:NE], nb[:, :], 0.0, ALU.mult, ALU.add))
                tt(st0[:, :], cum[:, :], nb[:, :], ALU.subtract)
                ts(st0[:, :], st0[:, :], float(P), None, ALU.mult)
                tt(rank[:, :, :], rank[:, :, :], st0[:, :].unsqueeze(1).to_broadcast([P, NT, NE]), ALU.add)
                for k in range(2):
                    tt(tot[:, :, :], flat[k], rank[:, :, :], ALU.mult)
                    did(v.tensor_reduce(dest_f[:, :], tot[:, :, :], AX_X, ALU.add))
                    v.tensor_copy(g["dest"][:, k, :], dest_f[:, :]).then_inc(ready, 1)
                    v.wait_ge(ready, k + 1)
                tt(cmp_[:, :, :], cum[:, :].unsqueeze(1).to_broadcast([P, NBLK, NE]),
                   bf[:, :].unsqueeze(2).to_broadcast([P, NBLK, NE]), ALU.is_le)
                did(v.tensor_reduce(be[:, :], cmp_[:, :, :], AX_X, ALU.add))
                ts(be[:, :], be[:, :], float(NE - 1), None, ALU.min)
                did(v.memset(nr[:, 0:1], 1.0))
                tt(nr[:, 1:], be[:, 1:], be[:, 0:NBLK - 1], ALU.not_equal)
                did(v.tensor_tensor_scan(rn[:, :], one[:, 0:NBLK], nr[:, :], 0.0, ALU.mult, ALU.add))
                floor(par[:, :], rn[:, :], 0.5, -0.25)
                did(v.scalar_tensor_tensor(out=par[:, :], in0=par[:, :], scalar=-2.0, in1=rn[:, :], op0=ALU.mult, op1=ALU.add))
                floor(npf[:, :], cum[:, NE - 1:NE], 0.5, 0.25)
                did(v.tensor_copy(g["blk"][0:1, 0, 0:NBLK], be[0:1, :]))
                did(v.tensor_copy(g["blk"][0:1, 1, 0:NBLK], nr[0:1, :]))
                did(v.tensor_copy(g["blk"][0:1, 2, 0:NBLK], par[0:1, :]))
                did(v.tensor_copy(g["blk"][0:1, 3, 0:1], npf[0:1, :]))
                ts(npf[:, :], npf[:, :], -1.0, NBLK / 2, ALU.mult, ALU.add)
                did(v.tensor_copy(g["blk"][0:1, 3, 1:2], npf[0:1, :]))
                did(v.memset(g["blk"][0:1, 0:3, NBLK:NBLK + 1], 0))


def stage_experts(nc, g, A, S):
    with Ctx(nc) as c:
        w13 = c.sb("w13", [P, 2, 2, KD, DE])
        w2 = c.sb("w2_sb", [P, 2, KE, D])
        idx = [c.sb(f"idx{b}", [P, 1], I32) for b in range(2)]
        tick, tick0 = c.sb("tick_x", [P, 1]), c.sem("tick_x0")
        xg = [c.sb(f"xg{b}", [P, D]) for b in range(2)]
        xT = [c.sb(f"xgT{b}", [P, KD, P]) for b in range(2)]
        si = c.sb("silu", [P, DE])
        ac = c.sb("act", [P, DE])
        aT = c.sb("actT", [P, KE, P])
        yo = [c.sb(f"yo{b}", [P, D]) for b in range(2)]
        psT = [c.ps(f"ps_xT{h}", [P, 4, P]) for h in range(2)]
        psA = c.ps("ps_aT", [P, KE, P])
        psG, psU = c.ps("ps_g", [P, 512]), c.ps("ps_u", [P, 512])
        psY = c.ps("ps_y", [P, 2, 512])
        w_in = [c.sem(f"we_in{b}") for b in range(2)]
        x_in = [c.sem(f"xg_in{b}") for b in range(2)]
        ix, x_tp, x_T = c.sem("idx_done"), c.sem("xg_tp"), [c.sem(f"xgT_done{h}") for h in range(2)]
        g_mm, u_mm, si_d, ac_d = c.sem("g_mm"), c.sem("u_mm"), c.sem("silu_done"), c.sem("act_done")
        a_tp, a_T, y_mm, y_d = c.sem("a_tp2"), c.sem("a_T2"), c.sem("y_mm"), c.sem("yo_done")
        y_st = [c.sem(f"yo_st{b}") for b in range(2)]
        zero, zero_d, pad_st = c.sb("zero_rows", [P, D]), c.sem("zero_done"), c.sem("pad_st")
        blk = g["blk"]

        def pairs(eng):
            return eng.value_load(blk[0:1, 3, 0:1], min_val=1, max_val=NBLK // 2)

        with nc.Block() as block:
            @block.sync
            def _(sp):
                n_pairs = pairs(sp)

                def weights(n, b):
                    e = sp.value_load(blk[0:1, 0, ds(n, 1)], min_val=0, max_val=NE - 1)
                    new = sp.value_load(blk[0:1, 1, ds(n, 1)], min_val=0, max_val=1)
                    side = sp.value_load(blk[0:1, 2, ds(n, 1)], min_val=0, max_val=1)
                    for m, name in enumerate(("w1", "w3")):
                        src = A[name][0].rearrange("e (k p) n -> e p k n", p=P)[ds(e, 1)].rearrange("a p k n -> (a p) k n")
                        dst = w13[:, ds(side, 1), m, :, :].rearrange("p a k n -> p (a k) n")
                        sp.dma_start(dst, src, cond=new > 0).then_inc(w_in[b], 16)
                    src = A["w2"][0].rearrange("e (k p) n -> e p k n", p=P)[ds(e, 1)].rearrange("a p k n -> (a p) k n")
                    sp.dma_start(w2[:, ds(side, 1), :, :].rearrange("p a k n -> p (a k) n"), src, cond=new > 0).then_inc(w_in[b], 16)

                weights(0, 0)
                sp.wait_ge(zero_d, 1)
                with sp.Fori(n_pairs, NBLK // 2) as i:
                    for b in range(2):
                        sp.dma_start(S["yb"].rearrange("(t p) n -> t p n", p=P)[ds(2 * i + b, 1)].rearrange("a p n -> (a p) n"),
                                     zero[:, :]).then_inc(pad_st, 16)
                with sp.Fori(0, n_pairs) as i:
                    for b in range(2):
                        n = 2 * i + b
                        sp.wait_ge(y_mm, n)
                        weights(n + 1, 1 - b)
                        sp.wait_ge(y_d, n + 1)
                        sp.dma_start(S["yb"].rearrange("(t p) n -> t p n", p=P)[ds(n, 1)].rearrange("a p n -> (a p) n"),
                                     yo[b][:, :]).then_inc(y_st[b], 16)

            @block.gpsimd
            def _(pool):
                n_pairs = pairs(pool)
                nc.gpsimd.memset(tick[:, :], 0.0).then_inc(tick0, 1)
                pool.wait_ge(tick0, 1)

                def gather(n, b):
                    nc.gpsimd.tensor_copy(idx[b][:, :], g["rowtok"][:, ds(n, 1)]).then_inc(ix, 1)
                    pool.wait_ge(ix, n + 1)
                    nc.gpsimd.tensor_tensor(tick[:, :], tick[:, :], tick[:, :], ALU.add)
                    pool.indirect_dma_start(xg[b][:, :], None, S["xn2"],
                                            bass.IndirectOffsetOnAxis(idx[b][:, 0:1], 0)).then_inc(x_in[b], 16)

                gather(0, 0)
                with pool.Fori(0, n_pairs) as i:
                    for b in range(2):
                        n = 2 * i + b
                        pool.wait_ge(x_tp, 2 * n)
                        gather(n + 1, 1 - b)

            @block.tensor
            def _(pe):
                n_pairs = pairs(pe)
                n_empty = pe.value_load(blk[0:1, 3, 1:2], min_val=0, max_val=NBLK // 2)

                def turn(n, b, i):
                    pe.wait_ge(x_in[b], 16 * i + 16)
                    for h in range(2):
                        pe.wait_ge(x_T[h], n)
                        for k in range(4):
                            mm = nc.tensor.transpose(psT[h][:, k, :], xg[b][:, (4 * h + k) * P:(4 * h + k + 1) * P], g["ident"][:, :])
                        mm.then_inc(x_tp, 1)

                turn(0, 0, 0)
                with pe.Fori(0, n_pairs) as i:
                    for b in range(2):
                        n = 2 * i + b
                        side = pe.value_load(blk[0:1, 2, ds(n, 1)], min_val=0, max_val=1)
                        pe.wait_ge(w_in[b], 48 * i + 48)
                        for h in range(2):
                            pe.wait_ge(x_T[h], n + 1)
                        for m, (o, s, free) in enumerate(((psG, g_mm, ac_d), (psU, u_mm, ac_d))):
                            pe.wait_ge(free, n)
                            for k in range(KD):
                                mm = nc.tensor.matmul(o[:, :], xT[b][:, k, :],
                                                      w13[:, ds(side, 1), m, k, :].rearrange("p a n -> p (a n)"),
                                                      start=k == 0, stop=k == KD - 1)
                            mm.then_inc(s, 1)
                        turn(n + 1, 1 - b, i + b)
                        pe.wait_ge(ac_d, n + 1)
                        pe.wait_ge(a_T, n)
                        for k in range(KE):
                            mm = nc.tensor.transpose(psA[:, k, :], ac[:, k * P:(k + 1) * P], g["ident"][:, :])
                        mm.then_inc(a_tp, 1)
                        pe.wait_ge(a_T, n + 1)
                        pe.wait_ge(y_d, n)
                        for h in range(2):
                            for k in range(KE):
                                mm = nc.tensor.matmul(psY[:, h, :], aT[:, k, :],
                                                      w2[:, ds(side, 1), k, 512 * h:512 * h + 512].rearrange("p a n -> p (a n)"),
                                                      start=k == 0, stop=k == KE - 1)
                        mm.then_inc(y_mm, 1)
                for b in range(2):
                    pe.wait_ge(x_in[b], 16 * n_pairs + 16 * (1 - b))
                    pe.wait_ge(w_in[b], 48 * n_pairs + 48 * (1 - b))
                    pe.wait_ge(y_st[b], 16 * n_pairs)
                pe.wait_ge(pad_st, 32 * n_empty)

            def leave(eng, op, h, n, b):
                eng.wait_ge(x_tp, 2 * n + h + 1)
                for k in range(4 * h, 4 * h + 4):
                    e = op(xT[b][:, k, :], psT[h][:, k % 4, :], g["acol"][:, 1, k:k + 1], g["bcol"][:, 1, k:k + 1])
                e.then_inc(x_T[h], 1)

            @block.scalar
            def _(act):
                n_pairs = pairs(act)

                def op(o, a, s, t):
                    return nc.scalar.activation(o, a, ACT.Identity, bias=t, scale=s)

                leave(act, op, 0, 0, 0)
                with act.Fori(0, n_pairs) as i:
                    for b in range(2):
                        n = 2 * i + b
                        act.wait_ge(g_mm, n + 1)
                        act.wait_ge(ac_d, n)
                        nc.scalar.activation(si[:, :], psG[:, :], ACT.Silu).then_inc(si_d, 1)
                        act.wait_ge(u_mm, n)
                        leave(act, op, 0, n + 1, 1 - b)
                        act.wait_ge(y_mm, n + 1)
                        act.wait_ge(y_st[b], 16 * i)
                        nc.scalar.activation(yo[b][:, :], psY[:, :, :].rearrange("p a n -> p (a n)"), ACT.Copy).then_inc(y_d, 1)

            @block.vector
            def _(v):
                n_pairs = pairs(v)
                v.memset(zero[:, :], 0.0).then_inc(zero_d, 1)

                def op(o, a, s, t):
                    return v.tensor_scalar(o, a, s, t, ALU.mult, ALU.add)

                leave(v, op, 1, 0, 0)
                with v.Fori(0, n_pairs) as i:
                    for b in range(2):
                        n = 2 * i + b
                        v.wait_ge(si_d, n + 1)
                        v.wait_ge(u_mm, n + 1)
                        v.wait_ge(a_tp, n)
                        v.tensor_tensor(ac[:, :], si[:, :], psU[:, :], ALU.mult).then_inc(ac_d, 1)
                        leave(v, op, 1, n + 1, 1 - b)
                        v.wait_ge(a_tp, n + 1)
                        v.wait_ge(y_mm, n)
                        v.tensor_copy(aT[:, :, :], psA[:, :, :]).then_inc(a_T, 1)


def stage_output(nc, g, A, S, out):
    with Ctx(nc) as c:
        idx = [[c.sb(f"di{b}{k}", [P, 1], I32) for k in range(2)] for b in range(2)]
        yr = [[c.sb(f"yr{b}{k}", [P, D]) for k in range(2)] for b in range(2)]
        x1 = [c.sb(f"x1o{b}", [P, D]) for b in range(2)]
        y = [c.sb(f"ysum{b}", [P, D]) for b in range(2)]
        ob = [c.sb(f"ob{b}", [P, D]) for b in range(2)]
        junk = [c.sb(f"junk_o{b}", [P, D]) for b in range(2)]
        ssq, ms, rt, rstd = ([c.sb(f"{n}{b}", [P, 1]) for b in range(2)] for n in ("o_ss", "o_ms", "o_rt", "o_rstd"))
        ix = c.sem("di_done")
        tick, tick0 = c.sb("tick_o", [P, 1]), c.sem("tick_o0")
        y_in = [c.sem(f"yr_in{b}") for b in range(2)]
        x_in = [c.sem(f"x1o_in{b}") for b in range(2)]
        ys, y_d, sq, ms_d, rt_d, os_, o_d = (c.sem(n) for n in ("y_scaled", "y_sum", "o_sq", "o_ms_d", "o_rt_d", "o_step", "o_done"))
        o_st = [c.sem(f"out_st{b}") for b in range(2)]

        def tile(dram, t):
            return dram.rearrange("(t p) n -> t p n", p=P)[ds(t, 1)].rearrange("a p n -> (a p) n")

        with nc.Block() as block:
            @block.gpsimd
            def _(pool):
                nc.gpsimd.memset(tick[:, :], 0.0).then_inc(tick0, 1)
                pool.wait_ge(tick0, 1)
                with pool.Fori(0, NT // 2) as i:
                    for b in range(2):
                        t = 2 * i + b
                        for k in range(2):
                            if b == 0 and k == 0:
                                pool.wait_ge(y_d, 2 * i)
                            nc.gpsimd.tensor_copy(idx[b][k][:, :], g["dest"][:, k, ds(t, 1)]).then_inc(ix, 1)
                            pool.wait_ge(ix, 2 * t + k + 1)
                            nc.gpsimd.tensor_tensor(tick[:, :], tick[:, :], tick[:, :], ALU.add)
                            pool.indirect_dma_start(yr[b][k][:, :], None, S["yb"],
                                                    bass.IndirectOffsetOnAxis(idx[b][k][:, 0:1], 0)).then_inc(y_in[b], 16)

            @block.sync
            def _(sp):
                for b in range(2):
                    sp.dma_start(x1[b][:, :], tile(S["x1"], b)).then_inc(x_in[b], 16)

                def store(t, b):
                    sp.wait_ge(o_d, t + 1)
                    sp.dma_start(tile(out[0], t), ob[b][:, :]).then_inc(o_st[b], 16)
                with sp.Fori(0, NT // 2 - 1) as i:
                    for b in range(2):
                        store(2 * i + b, b)
                        sp.dma_start(x1[b][:, :], tile(S["x1"], 2 * i + b + 2)).then_inc(x_in[b], 16)
                for b in range(2):
                    store(NT - 2 + b, b)
                for b in range(2):
                    sp.wait_ge(o_st[b], 16 * NT // 2)

            @block.scalar
            def _(act):
                with act.Fori(0, NT // 2) as i:
                    for b in range(2):
                        t = 2 * i + b
                        act.wait_ge(y_d, t + 1)
                        nc.scalar.activation(junk[b][:, :], y[b][:, :], ACT.Square, accum_out=ssq[b][:, :]).then_inc(sq, 1)
                        act.wait_ge(ms_d, t + 1)
                        nc.scalar.activation(rt[b][:, :], ms[b][:, :], ACT.Sqrt).then_inc(rt_d, 1)

            @block.vector
            def _(v):
                def head(t, i, b):
                    v.wait_ge(y_in[b], 32 * i + 32)
                    v.tensor_scalar(y[b][:, :], yr[b][0][:, :], g["wgt"][:, 0, ds(t, 1)], None, ALU.mult).then_inc(ys, 1)
                    v.wait_ge(ys, t + 1)
                    v.scalar_tensor_tensor(out=y[b][:, :], in0=yr[b][1][:, :], scalar=g["wgt"][:, 1, ds(t, 1)], in1=y[b][:, :],
                                           op0=ALU.mult, op1=ALU.add).then_inc(y_d, 1)

                def tail(t, i, b):
                    v.wait_ge(sq, t + 1)
                    v.tensor_scalar(ms[b][:, :], ssq[b][:, :], 1.0 / D, EPS, ALU.mult, ALU.add).then_inc(ms_d, 1)
                    v.wait_ge(rt_d, t + 1)
                    v.reciprocal(rstd[b][:, :], rt[b][:, :]).then_inc(os_, 1)
                    v.wait_ge(os_, 2 * t + 1)
                    v.wait_ge(o_st[b], 16 * i)
                    v.scalar_tensor_tensor(out=ob[b][:, :], in0=y[b][:, :], scalar=rstd[b][:, 0:1], in1=g["grow"][:, 1, :],
                                           op0=ALU.mult, op1=ALU.mult).then_inc(os_, 1)
                    v.wait_ge(os_, 2 * t + 2)
                    v.wait_ge(x_in[b], 16 * i + 16)
                    v.tensor_tensor(ob[b][:, :], ob[b][:, :], x1[b][:, :], ALU.add).then_inc(o_d, 1)

                head(0, 0, 0)
                with v.Fori(0, NT // 2 - 1) as i:
                    head(2 * i + 1, i, 1)
                    tail(2 * i, i, 0)
                    head(2 * i + 2, i + 1, 0)
                    tail(2 * i + 1, i, 1)
                i = NT // 2 - 1
                head(NT - 1, i, 1)
                tail(NT - 2, i, 0)
                tail(NT - 1, i, 1)


def program(nc, A, out, scratch_kind="Internal"):
    def dram(name, shape, dt=F32):
        return nc.dram_tensor(name, shape, dt, kind=scratch_kind).ap()

    S = {
        "qkvu": dram("s_qkvu", (T, QKVU)),
        "gates": dram("s_gates", (T, 2 * D)),
        "rec": dram("s_rec", (NG_S, P, REC)),
        "kpad": dram("s_kpad", (NG_S, CH_S, 512)),
        "row_tok": dram("s_row_tok", (CAP + P, 1), I32),
        "yb": dram("s_yb", (CAP, D)),
        "x1": dram("s_x1", (T, D)),
        "xn2": dram("s_xn2", (T, D)),
        "y": dram("s_y", (T, SW)),
        "bias_rows": dram("s_bias_rows", (NH, len(DILS), 3 * P - 1)),
        "bias_copies": dram("s_bias_copies", (P, NH * len(DILS) * (3 * P - 1))),
        "o": [dram(f"s_o{p}", (T, AW + 2 * NH)) for p in range(len(DILS))],
    }
    with Ctx(nc) as c:
        g = {
            "ident": c.sb("ident", [P, P]),
            "acol": c.sb("acol", [P, 2, KD]),
            "bcol": c.sb("bcol", [P, 2, KD]),
            "grow": c.sb("grow", [P, 2, D]),
            "rstd": c.sb("rstd", [P, NT]),
            "logits": c.sb("logits", [P, NT, NR]),
            "dest": c.sb("dest", [P, 2, NT], I32),
            "wgt": c.sb("wgt", [P, 2, NT]),
            "rowtok": c.sb("rowtok", [P, NBLK + 1], I32),
            "blk": c.sb("blk", [1, 4, NBLK + 1], I32),
        }
        stage_modulation(nc, g, A)
        stage_projection(nc, g, A, S)
        with Ctx(nc) as cs:
            gs = {**g, "rot": [cs.sb(f"rot{n}", [P, NG_S, NC]) for n in range(2)], "rho": cs.sb("rho", [P, NG_S])}
            stage_ssm_tables(nc, gs, A, S)
            stage_ssm(nc, gs, A, S)
        with Ctx(nc) as ca:
            ga = {**g, "bias": ca.sb("bias", [P, len(DILS), NH, 2 * P]), "bias_in": ca.sem("bias_in")}
            stage_bias(nc, ga, A, S)
            stage_attention(nc, ga, A, S)
        stage_merge(nc, g, A, S)
        stage_route(nc, g, A, S)
        stage_experts(nc, g, A, S)
        stage_output(nc, g, A, S, out)


_INS = ['x', 'c', 'w_mod', 'b_mod', 'g_pre_mix', 'g_post_mix', 'g_pre_ffn', 'g_post_ffn', 'w_in', 'rel_bias', 'a_re', 'a_im', 'log_dt', 'ssm_b_re', 'ssm_b_im', 'ssm_c_re', 'ssm_c_im', 'd_skip', 'w_glu', 'b_glu', 'w_branch_attn', 'w_branch_ssm', 'w_out', 'w_router_group', 'b_router_group', 'w_router_expert', 'b_router_expert', 'w1', 'w3', 'w2']


def kernel(**inputs):
    import numpy as _np
    import concourse.bacc as _bacc
    from concourse import mybir as _mybir
    from concourse.bass_utils import run_bass_kernel_spmd as _run

    nc = _bacc.Bacc("TRN2", target_bir_lowering=False, num_devices=1)
    given = {name: _np.ascontiguousarray(inputs[name]) for name in _INS}
    given["bucket_hot"] = bucket_one_hot()
    arrays, A = {}, {}
    for name, a in given.items():
        arrays[f"in_{name}_dram"] = a
        A[name] = nc.dram_tensor(f"in_{name}_dram", a.shape, _mybir.dt.from_np(a.dtype), kind="ExternalInput").ap()
    out = nc.dram_tensor("out_0_dram", (1, T, D), _mybir.dt.float32, kind="ExternalOutput").ap()
    program(nc, A, out)
    r = _run(nc, [arrays], core_ids=[0])
    return r.results[0]["out_0_dram"]
```

```python
from contextlib import ExitStack

import numpy as np

import concourse.bass as bass
from concourse import mybir

ALU = mybir.AluOpType
ACT = mybir.ActivationFunctionType
F32 = mybir.dt.float32
FR = mybir.dt.float32r
I32 = mybir.dt.int32
AX_X = mybir.AxisListType.X

P = 128
D = 1024
KD = D // P
T = 2048
NT = T // P
NH, HD = 8, 64
AW = NH * HD
DILS = (1, 4, 16)
NEG = -1e30
NUM_B, MAX_DIST = 32, 2048
EPS = 1e-6
NG_S, CH_S, ST_S = 32, 16, 64
SW = NG_S * CH_S
LC = 16
NC = T // LC
QKVU = 3 * AW + SW
IN_W = QKVU + 2 * D
NGR, EPG = 4, 8
NE = NGR * EPG
DE = D // 2
KE = DE // P
NBLK = 64
CAP = NBLK * P


def ds(i, n):
    return bass.ds(i, n)


def bucket_one_hot():
    exact = NUM_B // 2
    hot = np.zeros((NUM_B + 1, len(DILS), 3 * P - 1), np.float32)
    hot[NUM_B] = 1.0
    for p, dil in enumerate(DILS):
        for d in range(P + 1):
            dist = d * dil
            large = exact + int(np.float32(np.log(np.float32(max(dist, exact)) / np.float32(exact)))
                                / np.float32(np.log(MAX_DIST / exact)) * np.float32(NUM_B - exact))
            b = dist if dist < exact else min(large, NUM_B - 1)
            at = P - 1 + P - d
            hot[NUM_B, p, at] = 0.0
            hot[b, p, at] = 1.0
    return hot


class Ctx:

    def __init__(self, nc):
        self.nc, self.stack, self.sems = nc, ExitStack(), []

    def __enter__(self):
        self.stack.__enter__()
        return self

    def __exit__(self, *a):
        if a[0] is None and self.sems:
            self.nc.all_engine_barrier()
            self.nc.clear_and_free_semaphores(self.sems)
            self.nc.all_engine_barrier()
        return self.stack.__exit__(*a)

    def sb(self, name, shape, dt=F32):
        return self.stack.enter_context(self.nc.sbuf_tensor(name, shape, dt))

    def ps(self, name, shape, dt=F32):
        return self.stack.enter_context(self.nc.psum_tensor(name, shape, dt))

    def sem(self, name):
        self.sems.append(self.nc.alloc_semaphore(name))
        return self.sems[-1]


REC = 2 * 192 + 4 * 256


def ssm_tables(nc, g, A, S, c):
    H = ST_S
    craw = [c.sb(f"craw{n}", [P, 4, 2, H]) for n in range(2)]
    araw = [c.sb(f"araw{n}", [NG_S, 2, H]) for n in range(2)]
    B = [c.sb(f"B{n}", [P, NG_S, CH_S]) for n in range(2)]
    C = [c.sb(f"C{n}", [P, NG_S, CH_S]) for n in range(2)]
    lam = [c.sb(f"lam{n}", [P, NG_S]) for n in range(2)]
    dt = c.sb("dt", [P, NG_S])
    dsk = c.sb("dskip", [CH_S, NG_S])
    sm = {n: c.sb(f"sm_{n}", [P, NG_S]) for n in
          ("zr", "zi", "n", "r", "ab", "cs", "sn", "ea", "nr", "ni", "den", "inv", "t0", "t1", "fr", "fi", "z16")}
    pw = [c.sb(f"pw{n}", [P, LC + 1, NG_S]) for n in range(2)]
    pt = [c.sb(f"pt{n}", [P, NC // 2 * NG_S]) for n in range(2)]
    un = [c.sb(f"un{n}", [P, NG_S]) for n in range(2)]
    q1, q2, s2 = (c.sb(n, [P, LC + 1, NG_S]) for n in ("q1", "q2", "s2"))
    s1 = c.sb("s1", [P, LC + 1, NG_S])
    Bb = [c.sb(f"Bb{n}", [P, NG_S, CH_S]) for n in range(2)]
    tmp = [c.sb(f"tmp{n}", [P, NG_S, CH_S]) for n in range(2)]
    G = c.sb("G", [P, NG_S, LC + 1, CH_S])
    E = c.sb("E", [P, NG_S, LC, CH_S])
    dm = c.sb("dm", [CH_S, NG_S, CH_S])
    K = c.sb("K", [CH_S, 4, 256])
    zer = c.sb("zer", [CH_S, 256])
    Est = [c.sb(f"Est{b}", [P, 2, 3, H]) for b in range(2)]
    psC = c.ps("psC", [P, 4, P])
    psK = [c.ps(f"psK{b}", [P, 2, 256]) for b in range(2)]
    psE = [c.ps(f"psE{b}", [P, 2, 2, H]) for b in range(2)]
    in_ = c.sem("ssm_in")
    tr, tr_out, dt_done = c.sem("ssm_tr"), c.sem("ssm_tr_out"), c.sem("dt_done")
    act_r, trig, step_n = c.sem("angle_ready"), c.sem("trig_done"), c.sem("ssm_step")
    k_ps, k_out, k_st = c.sem("k_psum"), c.sem("k_out"), c.sem("k_st")
    e_ps, e_out, e_st = c.sem("e_psum"), c.sem("e_out"), [c.sem(f"e_st{b}") for b in range(2)]
    g_done, e_done, zer_done, t_st = c.sem("G_done"), c.sem("E_done"), c.sem("zer_done"), c.sem("T_st")
    rot, rho = [c.sb(f"rot{n}", [P, NG_S, NC]) for n in range(2)], c.sb("rho", [P, NG_S])
    rot_done = c.sem("rot_done")
    rec = S["rec"]

    def loads(sp):
        for n, name in enumerate(("ssm_c_re", "ssm_c_im")):
            for d in range(2):
                sp.dma_start(craw[n][:, :, d, :], A[name][0].rearrange("(k g) c p -> (g c) k p", g=8)).then_inc(in_, 16)
        for n, name in enumerate(("a_re", "a_im")):
            for d in range(2):
                sp.dma_start(araw[n][:, d, :], A[name][0]).then_inc(in_, 16)
        for n, name in enumerate(("ssm_b_re", "ssm_b_im")):
            for d in range(2):
                sp.dma_start(B[n][H * d:H * d + H, :, :], A[name][0].rearrange("g p c -> p g c")).then_inc(in_, 16)
        sp.dma_start(dt[:, :], A["log_dt"].to_broadcast([P, NG_S])).then_inc(in_, 16)
        sp.dma_start(dsk[:, :], A["d_skip"].rearrange("a (g c) -> c (a g)", c=CH_S),
                     allow_slow_non_contiguous=True).then_inc(in_, 16)

    def stores(sp):
        sp.wait_ge(g_done, 1)
        gr = rec.rearrange("g p n -> p g n")
        sp.dma_start(gr[:, :, 384:640], G[:, :, 1:, :].rearrange("p g s c -> p g (s c)")).then_inc(t_st, 16)
        for d in range(2):
            sp.dma_start(gr[H * d:H * d + H, :, 640:896],
                         G[H * (1 - d):H * (1 - d) + H, :, 1:, :].rearrange("p g s c -> p g (s c)")).then_inc(t_st, 16)
        sp.wait_ge(zer_done, 1)
        kp = S["kpad"]
        for q in range(NG_S // 4):
            sp.wait_ge(k_out, 3 * q + 3)
            sp.dma_start(kp[4 * q:4 * q + 4, :, 256:512].rearrange("g c n -> c g n"), K[:, :, :]).then_inc(k_st, 16)
        for gi in range(NG_S):
            sp.dma_start(kp[gi, :, 0:256], zer[:, :]).then_inc(k_st, 16)
        sp.wait_ge(k_st, 16 * (NG_S // 4 + NG_S))
        for s in range(LC):
            k, r = s // 8, s % 8
            sp.dma_start(rec[:, CH_S * r:CH_S * r + CH_S, 896 + 256 * k:1152 + 256 * k],
                         kp[:, :, 256 - CH_S * s:512 - CH_S * s]).then_inc(t_st, 16)
        sp.wait_ge(rot_done, 1)
        for n in range(2):
            sp.dma_start(S["rot"][n], rot[n][:, :, :]).then_inc(t_st, 16)
        sp.dma_start(S["rho"], rho[:, :]).then_inc(t_st, 16)
        sp.wait_ge(t_st, 16 * (6 + LC))

    def store_E(pool):
        for gi in range(NG_S):
            b = gi % 2
            pool.wait_ge(e_out, 2 * gi + 2)
            pool.dma_start(rec[gi, :, 0:384], Est[b][:, :, :, :].rearrange("p k r h -> p (k r h)")).then_inc(e_st[b], 16)
        for b in range(2):
            pool.wait_ge(e_st[b], 16 * NG_S // 2)

    def turn_inputs(pe):
        pe.wait_ge(in_, 16 * 14)
        for n in range(2):
            mm = nc.tensor.transpose(psK[0][:, n, 0:NG_S], araw[n][:, :, :].rearrange("g d p -> g (d p)"),
                                     g["ident"][0:NG_S, 0:NG_S])
        mm.then_inc(tr, 1)
        for n in range(2):
            if n:
                pe.wait_ge(tr_out, 2)
            for k in range(4):
                mm = nc.tensor.transpose(psC[:, k, :], craw[n][:, k, :, :].rearrange("q d p -> q (d p)"), g["ident"][:, :])
            mm.then_inc(tr, 1)

    def impulse(pe):
        pe.wait_ge(g_done, 1)
        pe.wait_ge(e_done, 1)
        for gi in range(NG_S):
            q = gi // 2
            if gi % 2 == 0 and q >= 2:
                pe.wait_ge(k_out, 3 * (q // 2) - 1 if q % 2 == 1 else 3 * (q // 2) - 2)
            mm = nc.tensor.matmul(psK[q % 2][0:CH_S, gi % 2, :], E[:, gi, LC - 1, :],
                                  G[:, gi, 0:LC, :].rearrange("p s c -> p (s c)"), start=True, stop=True)
            if gi % 2:
                mm.then_inc(k_ps, 1)
        for gi in range(NG_S):
            b = gi % 2
            if gi >= 2:
                pe.wait_ge(e_out, 2 * gi - 2)
            for k in range(2):
                mm = nc.tensor.transpose(psE[b][:, k, :, :].rearrange("p r h -> p (r h)"),
                                         E[:, gi, 8 * k:8 * k + 8, :].rearrange("p s c -> p (s c)"), g["ident"][:, :])
            mm.then_inc(e_ps, 1)

    def trigonometry(act):
        act.wait_ge(in_, 16 * 14)
        nc.scalar.activation(dt[:, :], dt[:, :], ACT.Exp).then_inc(dt_done, 1)
        act.wait_ge(act_r, 1)
        nc.scalar.activation(sm["ea"][:, :], sm["zr"][:, :], ACT.Exp).then_inc(trig, 1)
        nc.scalar.activation(rho[:, :], sm["z16"][:, :], ACT.Exp).then_inc(trig, 1)
        nc.scalar.activation(sm["sn"][:, :], sm["r"][:, :], ACT.Sin).then_inc(trig, 1)
        nc.scalar.activation(sm["cs"][:, :], sm["ab"][:, :], ACT.Sin).then_inc(trig, 1)

    def evacuate_E(act):
        for gi in range(NG_S):
            b = gi % 2
            act.wait_ge(e_ps, gi + 1)
            if gi >= 2:
                act.wait_ge(e_st[b], 16 * (gi // 2))
            nc.scalar.activation(Est[b][:, :, 0:2, :], psE[b][:, :, :, :], ACT.Copy).then_inc(e_out, 1)
            nc.scalar.activation(Est[b][:, :, 2, :], psE[b][:, :, 0, :], ACT.Copy).then_inc(e_out, 1)

    def tables(v):
        n_steps = [0]

        def did(ins):
            n_steps[0] += 1
            ins.then_inc(step_n, 1)
            v.wait_ge(step_n, n_steps[0])

        def tt(o, a, b, op):
            did(v.tensor_tensor(o, a, b, op))

        def cmul(o, a, b, shape):
            x, y = (pt[n][:, 0:shape[0] * shape[1]].rearrange("p (m g) -> p m g", g=shape[1]) for n in range(2))
            tt(x, a[0], b[0], ALU.mult)
            tt(y, a[1], b[1], ALU.mult)
            tt(o[0], x, y, ALU.subtract)
            tt(x, a[0], b[1], ALU.mult)
            tt(y, a[1], b[0], ALU.mult)
            tt(o[1], x, y, ALU.add)

        v.memset(zer[:, :], 0.0).then_inc(zer_done, 1)
        v.wait_ge(tr, 1)
        did(v.tensor_copy(lam[0][:, :], psK[0][:, 0, 0:NG_S]))
        did(v.tensor_copy(lam[1][:, :], psK[0][:, 1, 0:NG_S]))
        for n in range(2):
            v.wait_ge(tr, n + 2)
            v.tensor_copy(C[n][:, :, :].rearrange("p g c -> p (g c)"), psC[:, :, :].rearrange("p k n -> p (k n)")).then_inc(tr_out, 2)
        v.wait_ge(tr_out, 4)
        v.wait_ge(dt_done, 1)
        t = {k: x[:, :] for k, x in sm.items()}
        tt(t["zr"], lam[0][:, :], dt[:, :], ALU.mult)
        tt(t["zi"], lam[1][:, :], dt[:, :], ALU.mult)
        did(v.tensor_scalar(t["z16"], t["zr"], float(LC), None, ALU.mult))
        big = 1.5 * 2 ** 23
        did(v.tensor_scalar(t["n"], t["zi"], 1 / (2 * np.pi), big, ALU.mult, ALU.add))
        did(v.tensor_scalar(t["n"], t["n"], big, None, ALU.subtract))
        c1 = 6.28125
        c2 = float(np.float32(np.round((2 * np.pi - c1) * 2 ** 20) / 2 ** 20))
        c3 = 2 * np.pi - c1 - c2
        did(v.scalar_tensor_tensor(out=t["r"], in0=t["n"], scalar=-c1, in1=t["zi"], op0=ALU.mult, op1=ALU.add))
        did(v.scalar_tensor_tensor(out=t["t0"], in0=t["n"], scalar=-c2, in1=t["r"], op0=ALU.mult, op1=ALU.add))
        did(v.scalar_tensor_tensor(out=t["r"], in0=t["n"], scalar=-c3, in1=t["t0"], op0=ALU.mult, op1=ALU.add))
        pi = float(np.float32(np.pi)) * (1 - 2 ** -23)
        did(v.tensor_scalar(t["r"], t["r"], pi, -pi, ALU.min, ALU.max))
        did(v.scalar_tensor_tensor(out=t["t0"], in0=t["r"], scalar=-1.0, in1=t["r"], op0=ALU.mult, op1=ALU.max))
        v.tensor_scalar(t["ab"], t["t0"], -1.0, np.pi / 2, ALU.mult, ALU.add).then_inc(act_r, 1)
        v.wait_ge(trig, 4)
        tt(pw[0][:, 1, :], t["ea"], t["cs"], ALU.mult)
        tt(pw[1][:, 1, :], t["ea"], t["sn"], ALU.mult)
        did(v.memset(pw[0][:, 0, :], 1.0))
        did(v.memset(pw[1][:, 0, :], 0.0))
        did(v.tensor_scalar(t["nr"], pw[0][:, 1, :], -1.0, None, ALU.add))
        ni = pw[1][:, 1, :]
        tt(t["t0"], lam[0][:, :], lam[0][:, :], ALU.mult)
        tt(t["t1"], lam[1][:, :], lam[1][:, :], ALU.mult)
        tt(t["den"], t["t0"], t["t1"], ALU.add)
        did(v.reciprocal(t["inv"], t["den"]))
        tt(t["t0"], t["nr"], lam[0][:, :], ALU.mult)
        tt(t["t1"], ni, lam[1][:, :], ALU.mult)
        tt(t["fr"], t["t0"], t["t1"], ALU.add)
        tt(t["fr"], t["fr"], t["inv"], ALU.mult)
        tt(t["t0"], ni, lam[0][:, :], ALU.mult)
        tt(t["t1"], t["nr"], lam[1][:, :], ALU.mult)
        tt(t["fi"], t["t0"], t["t1"], ALU.subtract)
        tt(t["fi"], t["fi"], t["inv"], ALU.mult)
        fr, fi = (sm[n][:, :].unsqueeze(2).to_broadcast([P, NG_S, CH_S]) for n in ("fr", "fi"))
        for o, (x, y, op) in enumerate(((0, 1, ALU.subtract), (1, 0, ALU.add))):
            tt(tmp[0][:, :, :], B[x][:, :, :], fr, ALU.mult)
            tt(tmp[1][:, :, :], B[y][:, :, :], fi, ALU.mult)
            tt(Bb[o][:, :, :], tmp[0][:, :, :], tmp[1][:, :, :], op)
        m = 1
        while m < LC:
            a_m = [x[:, m:m + 1, :].to_broadcast([P, m, NG_S]) for x in pw]
            cmul([x[:, m + 1:2 * m + 1, :] for x in pw], [x[:, 1:m + 1, :] for x in pw], a_m, (m, NG_S))
            m *= 2
        top, bot = slice(0, H), slice(H, P)
        for dst, half, src, sign in ((q1, top, 0, 1.0), (q1, bot, 1, -1.0), (q2, top, 1, -1.0), (q2, bot, 0, -1.0),
                                     (s1, top, 0, 1.0), (s1, bot, 1, 1.0), (s2, top, 1, -1.0), (s2, bot, 0, 1.0)):
            did(v.tensor_scalar(dst[half, :, :], pw[src][half, :, :], sign, None, ALU.mult))
        for s in range(LC + 1):
            pq = [x[:, s, :].unsqueeze(2).to_broadcast([P, NG_S, CH_S]) for x in (q1, q2)]
            tt(tmp[0][:, :, :], C[0][:, :, :], pq[0], ALU.mult)
            tt(tmp[1][:, :, :], C[1][:, :, :], pq[1], ALU.mult)
            tt(G[:, :, s, :], tmp[0][:, :, :], tmp[1][:, :, :], ALU.add)
        v.engine_nop().then_inc(g_done, 1)
        for s in range(LC):
            pq = [x[:, LC - 1 - s, :].unsqueeze(2).to_broadcast([P, NG_S, CH_S]) for x in (s1, s2)]
            tt(tmp[0][:, :, :], Bb[0][:, :, :], pq[0], ALU.mult)
            tt(tmp[1][:, :, :], Bb[1][:, :, :], pq[1], ALU.mult)
            tt(E[:, :, s, :], tmp[0][:, :, :], tmp[1][:, :, :], ALU.add)
        v.engine_nop().then_inc(e_done, 1)
        tt(dm[:, :, :], g["ident"][0:CH_S, 0:CH_S].unsqueeze(1).to_broadcast([CH_S, NG_S, CH_S]),
           dsk[:, :].unsqueeze(2).to_broadcast([CH_S, NG_S, CH_S]), ALU.mult)
        for q in range(NG_S // 4):
            if q:
                v.wait_ge(k_st, 16 * q)
            for b in range(2):
                v.wait_ge(k_ps, 2 * q + b + 1)
                v.tensor_copy(K[:, 2 * b:2 * b + 2, :], psK[b][0:CH_S, :, :]).then_inc(k_out, 1)
            v.wait_ge(k_out, 3 * q + 2)
            v.tensor_tensor(K[:, :, 0:CH_S], K[:, :, 0:CH_S], dm[:, 4 * q:4 * q + 4, :], ALU.add).then_inc(k_out, 1)
        x, y = (sm[n][:, :] for n in ("cs", "sn"))
        did(v.tensor_copy(un[0][:, :], x))
        did(v.tensor_copy(un[1][:, :], y))
        for _ in range(4):
            tt(t["t0"], un[0][:, :], un[0][:, :], ALU.mult)
            tt(t["t1"], un[1][:, :], un[1][:, :], ALU.mult)
            tt(t["nr"], un[0][:, :], un[1][:, :], ALU.mult)
            tt(un[0][:, :], t["t0"], t["t1"], ALU.subtract)
            did(v.tensor_scalar(un[1][:, :], t["nr"], 2.0, None, ALU.mult))
        for n in range(2):
            did(v.memset(rot[n][:, :, 0:1], 1.0 - n))
            did(v.tensor_copy(rot[n][:, :, 1:2], un[n][:, :].unsqueeze(2)))
        m = 1
        while m < NC:
            k = min(m, NC - 1 - m)
            if k <= 0:
                break
            a = [x[:, :, 1:k + 1] for x in rot]
            b = [x[:, :, m:m + 1].to_broadcast([P, NG_S, k]) for x in rot]
            o = [x[:, :, m + 1:m + k + 1] for x in rot]
            x, y = (pt[n][:, 0:NG_S * k].rearrange("p (g m) -> p g m", m=k) for n in range(2))
            tt(x, a[0], b[0], ALU.mult)
            tt(y, a[1], b[1], ALU.mult)
            tt(o[0], x, y, ALU.subtract)
            tt(x, a[0], b[1], ALU.mult)
            tt(y, a[1], b[0], ALU.mult)
            tt(o[1], x, y, ALU.add)
            m *= 2
        did(v.tensor_scalar(rot[1][bot, :, :], rot[1][bot, :, :], -1.0, None, ALU.mult))
        v.engine_nop().then_inc(rot_done, 1)

    return {"loads": loads, "stores": stores, "store_E": store_E, "turn_inputs": turn_inputs, "impulse": impulse,
            "trigonometry": trigonometry, "evacuate_E": evacuate_E, "tables": tables}


def stage_modulation(nc, g, A, S):
    with Ctx(nc) as c:
        tab = ssm_tables(nc, g, A, S, c)
        MW = 3 * D
        wm = [c.sb(f"wmod{b}", [P, MW]) for b in range(2)]
        ccol = c.sb("ccol", [P, KD])
        sig = c.sb("csig", [P, KD])
        scol = c.sb("scol", [P, KD])
        bmod = c.sb("bmod", [P, 6 * KD])
        mod = c.sb("mod", [P, 6 * KD])
        gains = c.sb("gains", [P, 4, KD])
        gcol = c.sb("gcol", [P, 2, KD])
        xs = [c.sb(f"xs{b}", [P, D]) for b in range(2)]
        ss = c.sb("ss", [P, NT])
        ms = c.sb("ms", [P, NT])
        psm = c.ps("psm", [P, 512])
        psr = [c.ps(f"psr{b}", [P, 512]) for b in range(2)]
        small_in = c.sem("mod_small_in")
        w_in = [c.sem(f"wmod_in{b}") for b in range(2)]
        w_used = c.sem("wmod_used")
        sig_done = c.sem("csig_done")
        silu_done = c.sem("csilu_done")
        mod_done = c.sem("mod_done")
        vstep = c.sem("mod_vstep")
        ident0 = c.sem("ident0")
        ident1 = c.sem("ident_done")
        rows_done = c.sem("rows_done")
        rows_out = c.sem("rows_out")
        x_in = [c.sem(f"xs_in{b}") for b in range(2)]
        sq = c.sem("x_sq")
        ms_done = c.sem("ms_done")
        rms_done = c.sem("rms_done")
        rstd_done = c.sem("rstd_done")
        xv = A["x"][0].rearrange("(t p) n -> t p n", p=P)
        wv = A["w_mod"][0].rearrange("(k p) n -> k p n", p=P)

        with nc.Block() as block:
            @block.sync
            def _(sp):
                sp.dma_start(ccol[:, :], A["c"].rearrange("a (k p) -> p (a k)", p=P),
                             allow_slow_non_contiguous=True).then_inc(small_in, 16)
                sp.dma_start(bmod[:, :], A["b_mod"].rearrange("a (k p) -> p (a k)", p=P),
                             allow_slow_non_contiguous=True).then_inc(small_in, 16)
                for n, name in enumerate(("g_pre_mix", "g_post_mix", "g_pre_ffn", "g_post_ffn")):
                    sp.dma_start(gains[:, n, :], A[name].rearrange("a (k p) -> p (a k)", p=P),
                                 allow_slow_non_contiguous=True).then_inc(small_in, 16)
                tab["loads"](sp)
                for b in range(2):
                    sp.dma_start(xs[b][:, :], xv[b]).then_inc(x_in[b], 16)
                with sp.Fori(1, NT // 2) as i:
                    for b in range(2):
                        sp.wait_ge(sq, 2 * i + b - 1)
                        sp.dma_start(xs[b][:, :], xv[ds(2 * i + b, 1)].rearrange("a p n -> (a p) n")).then_inc(x_in[b], 16)
                tab["stores"](sp)

            @block.gpsimd
            def _(pool):
                for b in range(2):
                    pool.dma_start(wm[b][:, :], wv[0, :, b * MW:(b + 1) * MW]).then_inc(w_in[b], 16)
                nc.gpsimd.memset(g["ident"][:, :], 0.0).then_inc(ident0, 1)
                pool.wait_ge(ident0, 1)
                nc.gpsimd.affine_select(out=g["ident"][:, :], in_=g["ident"][:, :], compare_op=ALU.not_equal,
                                        fill=1.0, base=0, pattern=[[-1, P]], channel_multiplier=1).then_inc(ident1, 1)
                for k in range(1, KD):
                    for b in range(2):
                        pool.wait_ge(w_used, 2 * k + b - 1)
                        pool.dma_start(wm[b][:, :], wv[k, :, b * MW:(b + 1) * MW]).then_inc(w_in[b], 16)
                tab["store_E"](pool)

            @block.scalar
            def _(act):
                act.wait_ge(small_in, 96)
                nc.scalar.activation(sig[:, :], ccol[:, :], ACT.Sigmoid).then_inc(sig_done, 1)
                tab["trigonometry"](act)
                with act.Fori(0, NT // 2) as i:
                    for b in range(2):
                        act.wait_ge(x_in[b], 16 * i + 16)
                        nc.scalar.activation(xs[b][:, :], xs[b][:, :], ACT.Square,
                                             accum_out=ss[:, ds(2 * i + b, 1)]).then_inc(sq, 1)
                tab["evacuate_E"](act)
                act.wait_ge(ms_done, 1)
                nc.scalar.activation(ms[:, :], ms[:, :], ACT.Sqrt).then_inc(rms_done, 1)

            @block.tensor
            def _(pe):
                pe.wait_ge(ident1, 1)
                tab["turn_inputs"](pe)
                pe.wait_ge(silu_done, 1)
                for k in range(KD):
                    for b in range(2):
                        pe.wait_ge(w_in[b], 16 * k + 16)
                        for n in range(MW // P):
                            col = b * MW // P + n
                            mm = nc.tensor.matmul(psm[:, col:col + 1], wm[b][:, n * P:(n + 1) * P], scol[:, k:k + 1],
                                                  start=k == 0 and col == 0, stop=k == KD - 1, skip_group_check=True)
                        mm.then_inc(w_used, 1)
                tab["impulse"](pe)
                pe.wait_ge(vstep, 6)
                for r in range(2):
                    if r:
                        pe.wait_ge(rows_out, 2)
                    for k in range(KD):
                        o = psr[k // 4][:, (k % 4) * P:(k % 4 + 1) * P]
                        mm = nc.tensor.matmul(o, gcol[:, r, k:k + 1].to_broadcast([P, P]), g["ident"][:, :],
                                              start=True, stop=True)
                    mm.then_inc(rows_done, 1)

            @block.vector
            def _(v):
                v.wait_ge(sig_done, 1)
                v.tensor_tensor(scol[:, :], ccol[:, :], sig[:, :], ALU.mult).then_inc(silu_done, 1)
                tab["tables"](v)
                v.wait_ge(sq, NT)
                v.tensor_scalar(ms[:, :], ss[:, :], 1.0 / D, EPS, ALU.mult, ALU.add).then_inc(ms_done, 1)
                v.wait_ge(rms_done, 1)
                v.reciprocal(g["rstd"][:, :], ms[:, :]).then_inc(rstd_done, 1)
                v.wait_ge(w_used, 2 * KD)
                v.tensor_tensor(mod[:, :], psm[:, 0:6 * KD], bmod[:, :], ALU.add).then_inc(mod_done, 1)
                v.wait_ge(mod_done, 1)
                for r in range(2):
                    sh, sc, gt = (mod[:, (3 * r + j) * KD:(3 * r + j + 1) * KD] for j in range(3))
                    v.scalar_tensor_tensor(out=g["acol"][:, r, :], in0=sc, scalar=1.0, in1=gains[:, 2 * r, :],
                                           op0=ALU.add, op1=ALU.mult).then_inc(vstep, 1)
                    v.tensor_copy(g["bcol"][:, r, :], sh).then_inc(vstep, 1)
                    v.tensor_tensor(gcol[:, r, :], gt, gains[:, 2 * r + 1, :], ALU.mult).then_inc(vstep, 1)
                for r in range(2):
                    v.wait_ge(rows_done, r + 1)
                    for j in range(2):
                        v.tensor_copy(g["grow"][:, r, j * 512:(j + 1) * 512], psr[j][:, :]).then_inc(rows_out, 1)
                v.wait_ge(rows_out, 4)
                v.wait_ge(rstd_done, 1)


def stage_projection(nc, g, A, S):
    HW = 1024
    with Ctx(nc) as c:
        wh, wl = (c.sb(f"w_in_{n}", [P, KD, QKVU], FR) for n in ("hi", "lo"))
        wr = [c.sb(f"w_raw{b}", [P, HW]) for b in range(2)]
        x = [c.sb(f"xt{b}", [P, D]) for b in range(2)]
        h = c.sb("h_exact", [P, KD, P])
        hh, hl = ([c.sb(f"h_{n}{b}", [P, KD, P], FR) for b in range(2)] for n in ("hi", "lo"))
        st = [c.sb(f"proj_st{b}", [P, QKVU]) for b in range(2)]
        pst = [c.ps(f"pst{b}", [P, 4, P]) for b in range(2)]
        pso = [c.ps(f"pso{b}", [P, 512]) for b in range(4)]
        w_ld = [c.sem(f"w_raw_in{b}") for b in range(2)]
        w_hi, w_lo, w_used = c.sem("w_hi_done"), c.sem("w_lo_done"), c.sem("w_chunk_used")
        x_in = [c.sem(f"x_in{b}") for b in range(2)]
        xnd, tp, ht = c.sem("xn_done"), c.sem("hT_psum"), c.sem("hT_done")
        hi_d, lo_d = c.sem("h_hi_done"), c.sem("h_lo_done")
        po, ev = c.sem("proj_psum"), c.sem("proj_evac")
        stored = [c.sem(f"proj_stored{b}") for b in range(2)]
        xv = A["x"][0].rearrange("(t p) n -> t p n", p=P)
        wv = A["w_in"][0].rearrange("(k p) n -> k p n", p=P)
        dst = [S[n].rearrange("(t p) n -> t p n", p=P) for n in ("qkvu", "gates")]

        def steps(eng, body):
            for r in range(2):
                lo, hi = NT * r // 2, NT * (r + 1) // 2
                for b in range(2):
                    body(2 * lo + b, r, b)
                with eng.Fori(lo + 1, hi - 1) as i:
                    for b in range(2):
                        body(2 * i + b, r, b)
                for b in range(2):
                    body(2 * hi - 2 + b, r, b)

        def known(u):
            return isinstance(u, int)

        with nc.Block() as block:
            @block.sync
            def _(sp):
                def load_x(u, r, b):
                    t = u - NT * r
                    sp.dma_start(x[b][:, :], xv[ds(t, 1)].rearrange("a p n -> (a p) n")).then_inc(x_in[b], 16)

                def weights(r):
                    for j in range(2 * KD):
                        n = 2 * KD * r + j
                        if n >= 2:
                            sp.wait_ge(w_lo, n - 1)
                        sp.dma_start(wr[j % 2][:, :], wv[j // 2, :, QKVU * r + HW * (j % 2):QKVU * r + HW * (j % 2) + HW]
                                     ).then_inc(w_ld[j % 2], 16)

                def body(u, r, b):
                    if not (known(u) and u == 2 * NT - 1) and not (known(u) and u == 2 * NT - 2):
                        sp.wait_ge(tp, 2 * u + 2)
                        last = known(u) and u >= NT * r + NT - 2
                        load_x(u + 2, r + 1 if last else r, b)
                    if known(u) and u == NT - 1:
                        weights(1)
                    sp.wait_ge(ev, 4 * u + 4)
                    sp.dma_start(dst[r][ds(u - NT * r, 1)].rearrange("a p n -> (a p) n"), st[b][:, :]).then_inc(stored[b], 16)

                load_x(0, 0, 0)
                load_x(1, 0, 1)
                weights(0)
                steps(sp, body)
                for b in range(2):
                    sp.wait_ge(stored[b], 16 * NT)

            def evacuate(eng, op, u, b):
                for n in range(4):
                    eng.wait_ge(po, 4 * u + n + 1)
                    if n == 0 and not (known(u) and u < 2):
                        eng.wait_ge(stored[b], 8 * (u - b))
                    op(n, st[b][:, n * 512:(n + 1) * 512], pso[n][:, :]).then_inc(ev, 1)

            @block.scalar
            def _(act):
                def split_h(u, b):
                    act.wait_ge(ht, 8 * u + 8)
                    if not (known(u) and u < 2):
                        act.wait_ge(po, 4 * u - 4)
                    nc.scalar.activation(hh[b][:, :, :], h[:, :, :], ACT.Copy).then_inc(hi_d, 1)

                def split_w(r):
                    for j in range(2 * KD):
                        if r:
                            if j // 2 < KD - 1:
                                act.wait_ge(w_used, j // 2 + 1)
                            else:
                                act.wait_ge(po, 4 * NT)
                        act.wait_ge(w_ld[j % 2], 16 * (KD * r + j // 2 + 1))
                        nc.scalar.activation(wh[:, j // 2, HW * (j % 2):HW * (j % 2) + HW], wr[j % 2][:, :],
                                             ACT.Copy).then_inc(w_hi, 1)

                def body(u, r, b):
                    if not (known(u) and u == 2 * NT - 1):
                        split_h(u + 1, 1 - b)
                    if known(u) and u == NT - 1:
                        split_w(1)
                    if r == 1:
                        evacuate(act, lambda n, o, a: nc.scalar.activation(o, a, ACT.Sigmoid), u, b)

                split_h(0, 0)
                split_w(0)
                steps(act, body)

            @block.gpsimd
            def _(pool):
                def split_h(u, b):
                    pool.wait_ge(hi_d, u + 1)
                    nc.gpsimd.tensor_tensor(hl[b][:, :, :], h[:, :, :], hh[b][:, :, :], ALU.subtract).then_inc(lo_d, 1)

                def body(u, r, b):
                    if not (known(u) and u == 2 * NT - 1):
                        split_h(u + 1, 1 - b)

                split_h(0, 0)
                steps(pool, body)

            @block.tensor
            def _(pe):
                def transposes(u, b):
                    pe.wait_ge(xnd, u + 1)
                    for half in range(2):
                        if not (known(u) and u == 0):
                            pe.wait_ge(ht, 8 * u - 4 + 4 * half)
                        for k in range(4):
                            mm = nc.tensor.transpose(pst[half][:, k, :], x[b][:, (4 * half + k) * P:(4 * half + k + 1) * P],
                                                     g["ident"][:, :])
                        mm.then_inc(tp, 1)

                def product(n, k, b):
                    cols = slice(n * 512, (n + 1) * 512)
                    for m, (a, w) in enumerate(((hh, wh), (hl, wh), (hh, wl))):
                        mm = nc.tensor.matmul(pso[n][:, :], a[b][:, k, :], w[:, k, cols],
                                              start=k == 0 and m == 0, stop=k == KD - 1 and m == 2)
                    return mm

                def body(u, r, b):
                    if not (known(u) and u == 2 * NT - 1):
                        transposes(u + 1, 1 - b)
                    pe.wait_ge(lo_d, u + 1)
                    if known(u) and u in (0, NT - 1, NT):
                        for k in range(KD):
                            for n in range(4):
                                if u:
                                    if k == 0:
                                        pe.wait_ge(ev, 4 * u - 3 + n)
                                if u != NT - 1 and n % 2 == 0:
                                    pe.wait_ge(w_lo, 2 * KD * r + 2 * k + n // 2 + 1)
                                mm = product(n, k, b)
                                if k == KD - 1:
                                    mm.then_inc(po, 1)
                            if u == NT - 1 and k < KD - 1:
                                mm.then_inc(w_used, 1)
                        return
                    for n in range(4):
                        pe.wait_ge(ev, 4 * u - 3 + n)
                        for k in range(KD):
                            mm = product(n, k, b)
                        mm.then_inc(po, 1)

                transposes(0, 0)
                steps(pe, body)

            @block.vector
            def _(v):
                def norm(u, r, b):
                    v.wait_ge(x_in[b], 8 * (u - b) + 16)
                    v.tensor_scalar(x[b][:, :], x[b][:, :], g["rstd"][:, ds(u - NT * r, 1)], None, ALU.mult).then_inc(xnd, 1)

                def affine(u):
                    for k in range(KD):
                        v.wait_ge(tp, 2 * u + k // 4 + 1)
                        if k == 0 and not (known(u) and u == 0):
                            v.wait_ge(lo_d, u)
                        v.tensor_scalar(h[:, k, :], pst[k // 4][:, k % 4, :], g["acol"][:, 0, k:k + 1],
                                        g["bcol"][:, 0, k:k + 1], ALU.mult, ALU.add).then_inc(ht, 1)

                def split_w(r):
                    for j in range(2 * KD):
                        cols = slice(HW * (j % 2), HW * (j % 2) + HW)
                        v.wait_ge(w_hi, 2 * KD * r + j + 1)
                        v.tensor_tensor(wl[:, j // 2, cols], wr[j % 2][:, :], wh[:, j // 2, cols], ALU.subtract).then_inc(w_lo, 1)

                def body(u, r, b):
                    if not (known(u) and u == 2 * NT - 1):
                        affine(u + 1)
                    if not (known(u) and u >= 2 * NT - 2):
                        norm(u + 2, r + 1 if known(u) and u >= NT * r + NT - 2 else r, b)
                    if known(u) and u == NT - 1:
                        split_w(1)
                    if r == 0:
                        evacuate(v, lambda n, o, a: v.tensor_scalar(o, a, HD ** -0.5 if n == 0 else 1.0, None, ALU.mult), u, b)

                norm(0, 0, 0)
                affine(0)
                norm(1, 0, 1)
                split_w(0)
                steps(v, body)


def stage_bias(nc, g, A, S):
    W = 3 * P - 1
    with Ctx(nc) as c:
        hot = c.sb("bucket_hot", [NUM_B + 1, len(DILS), W])
        rb = c.sb("rel_bias_sb", [NUM_B + 1, NH])
        row = c.sb("bias_row", [NH, len(DILS), W])
        ps = [c.ps(f"ps_bias{p}", [P, 512]) for p in range(len(DILS))]
        hot_in, neg_done, mm_done = c.sem("hot_in"), c.sem("neg_done"), c.sem("bias_mm")
        row_done, row_st, bias_in = c.sem("row_done"), c.sem("row_st"), g["bias_in"]
        with nc.Block() as block:
            @block.sync
            def _(sp):
                sp.dma_start(hot[:, :, :], A["bucket_hot"]).then_inc(hot_in, 16)
                sp.dma_start(rb[0:NUM_B, :], A["rel_bias"]).then_inc(hot_in, 16)
                sp.wait_ge(row_done, len(DILS))
                sp.dma_start(S["bias_rows"], row[:, :, :]).then_inc(row_st, 16)
                sp.wait_ge(row_st, 16)
                pitch = NH * len(DILS) * W
                one = S["bias_rows"]
                sp.dma_start(S["bias_copies"], bass.AP(tensor=one.tensor, offset=one.offset, ap=[[0, P], [1, pitch]])).then_inc(row_st, 16)
                sp.wait_ge(row_st, 32)
                src = S["bias_copies"]
                for p in range(len(DILS)):
                    view = bass.AP(tensor=src.tensor, offset=src.offset + p * W + P - 1,
                                   ap=[[pitch - 1, P], [len(DILS) * W, NH], [1, 2 * P]])
                    sp.dma_start(g["bias"][:, p, :, :], view).then_inc(bias_in, 16)
                sp.wait_ge(bias_in, 16 * len(DILS))

            @block.tensor
            def _(pe):
                pe.wait_ge(hot_in, 32)
                pe.wait_ge(neg_done, 1)
                for p in range(len(DILS)):
                    nc.tensor.matmul(ps[p][0:NH, 0:W], rb[:, :], hot[:, p, :], start=True, stop=True).then_inc(mm_done, 1)

            @block.vector
            def _(v):
                v.memset(rb[NUM_B:NUM_B + 1, :], NEG).then_inc(neg_done, 1)
                for p in range(len(DILS)):
                    v.wait_ge(mm_done, p + 1)
                    v.tensor_copy(row[:, p, :], ps[p][0:NH, 0:W]).then_inc(row_done, 1)


def stage_attention(nc, g, A, S):
    NP_ = NH // 2
    with Ctx(nc) as c:
        qk = [c.sb(f"qk{b}", [P, 2 * AW]) for b in range(2)]
        vv = [c.sb(f"v{b}", [P, AW]) for b in range(4)]
        qT = [c.sb(f"qT{b}", [P, NP_, P]) for b in range(2)]
        kT = c.sb("kT", [P, NP_, 5, P])
        pr = [c.sb(f"probs{b}", [P, 2, 2 * P]) for b in range(4)]
        pT = [c.sb(f"probsT{b}", [P, 2, 2, P]) for b in range(2)]
        nm = [c.sb(f"negmax{b}", [P, 2]) for b in range(4)]
        osb = [c.sb(f"osb{b}", [P, AW + 2 * NH]) for b in range(2)]
        tick = c.sb("tick", [P, 4])
        ps_t = c.ps("ps_qk", [P, NP_, P])
        ps_s = [c.ps(f"ps_s{b}", [P, 2, 2 * P]) for b in range(4)]
        ps_p = [c.ps(f"ps_p{b}", [P, 2, 2, P]) for b in range(2)]
        ps_o = c.ps("ps_o", [P, NH, HD])
        qk_in = [c.sem(f"qk_in{b}") for b in range(2)]
        v_in = [c.sem(f"v_in{b}") for b in range(4)]
        tq, qkT = c.sem("qk_psum"), c.sem("qkT_done")
        k_again = c.sem("k_again")
        mx = c.sem("max_done")
        s_ps, s_sb = c.sem("s_psum"), c.sem("s_biased")
        ex = c.sem("exp_done")
        p_ps, p_sb = c.sem("pT_psum"), c.sem("pT_done")
        pv, oe = c.sem("pv_done"), c.sem("o_evac")
        o_st = [c.sem(f"o_st{b}") for b in range(2)]

        rows = S["qkvu"]

        def head(j, h):
            return 4 * (j // 2) + j % 2 + 2 * h

        def tokens(dram, d, i, r, c0, c1):
            if d == 1:
                return dram.rearrange("(b p) n -> b p n", p=P)[ds(4 * i + r, 1), :, c0:c1].rearrange("a p n -> (a p) n")
            if d == 4:
                v = dram.rearrange("(b p s) n -> b s p n", p=P, s=4)
                return v[r, ds(i, 1), :, c0:c1].rearrange("a p n -> (a p) n")
            v = dram.rearrange("(p s) n -> s p n", s=16)
            return v[ds(4 * i + r, 1), :, c0:c1].rearrange("a p n -> (a p) n")

        def groups(eng, body):
            for p in range(len(DILS)):
                if p == 0:
                    body(p, 0, True)
                with eng.Fori(1 if p == 0 else 0, 4) as i:
                    body(p, i, False)

        def prev(p, r, first):
            return p == 0 and (r > 0 or not first) or p == 1 and r > 0

        with nc.Block() as block:
            @block.sync
            def _(sp):
                def body(p, i, first):
                    for r in range(4):
                        u = 16 * p + 4 * i + r
                        if not (first and r < 2):
                            sp.wait_ge(tq, 2 * u - 2)
                        sp.dma_start(qk[r % 2][:, :], tokens(rows, DILS[p], i, r, 0, 2 * AW)).then_inc(qk_in[r % 2], 16)
                        if not first:
                            sp.wait_ge(pv, NP_ * (u - 2))
                        sp.dma_start(vv[r][:, :], tokens(rows, DILS[p], i, r, 2 * AW, 3 * AW)).then_inc(v_in[r], 16)
                groups(sp, body)

            @block.gpsimd
            def _(pool):
                def body(p, i, first):
                    for r in range(4):
                        u = 16 * p + 4 * i + r
                        pool.wait_ge(oe, u + 1)
                        pool.dma_start(tokens(S["o"][p], DILS[p], i, r, 0, AW + 2 * NH), osb[r % 2][:, :]).then_inc(o_st[r % 2], 16)
                groups(pool, body)
                for b in range(2):
                    pool.wait_ge(o_st[b], 16 * 24)

            @block.tensor
            def _(pe):
                def body(p, i, first):
                    u0 = 16 * p + 4 * i
                    n0 = NP_ * u0

                    def turn_qk(r, h):
                        u = u0 + r
                        pe.wait_ge(qk_in[r % 2], 16 * (8 * p + 2 * i + r // 2 + 1))
                        if not (first and r == 0 and h == 0):
                            pe.wait_ge(qkT, 2 * u + h)
                        for n in range(NP_):
                            mm = nc.tensor.transpose(ps_t[:, n, :], qk[r % 2][:, (NP_ * h + n) * P:(NP_ * h + n + 1) * P],
                                                     g["ident"][:, :])
                        mm.then_inc(tq, 1)

                    def scores(m):
                        r, j = m // NP_, m % NP_
                        has = prev(p, r, first)
                        own = 4 if r == 0 and has else r
                        pe.wait_ge(qkT, 2 * (u0 + r) + 2)
                        if own == 4:
                            pe.wait_ge(k_again, i)
                        if not (first and m < 4):
                            pe.wait_ge(s_sb, n0 + m - 3)
                        for h in range(2):
                            hh = head(j, h)
                            lo, hi = HD * (hh % 2), HD * (hh % 2 + 1)
                            keys = slice(own - 1, own + 1) if has else slice(own, own + 1)
                            mm = nc.tensor.matmul(ps_s[m % 4][:, h, (0 if has else P):], qT[r % 2][lo:hi, hh // 2, :],
                                                  kT[lo:hi, hh // 2, keys, :], start=True, stop=True)
                        mm.then_inc(s_ps, 1)

                    def turn(m):
                        pe.wait_ge(ex, n0 + m + 1)
                        if not (first and m < 2):
                            pe.wait_ge(p_sb, n0 + m - 1)
                        for h in range(2):
                            for w in range(0 if prev(p, m // NP_, first) else 1, 2):
                                mm = nc.tensor.transpose(ps_p[m % 2][:, h, w, :], pr[m % 4][:, h, w * P:(w + 1) * P],
                                                         g["ident"][:, :])
                        mm.then_inc(p_ps, 1)

                    def values(m):
                        r, j = m // NP_, m % NP_
                        if j == 0:
                            pe.wait_ge(v_in[r], 16 * (4 * p + i + 1))
                            if not (first and r == 0):
                                pe.wait_ge(oe, u0 + r)
                        pe.wait_ge(p_sb, n0 + m + 1)
                        has = prev(p, r, first)
                        for h in range(2):
                            hh = head(j, h)
                            for w in range(0 if has else 1, 2):
                                mm = nc.tensor.matmul(ps_o[:, hh, :], pT[m % 2][:, h, w, :],
                                                      vv[(r - 1 + w) % 4][:, hh * HD:(hh + 1) * HD],
                                                      start=not (has and w), stop=w == 1)
                        mm.then_inc(pv, 1)

                    turn_qk(0, 0)
                    turn_qk(0, 1)
                    scores(0)
                    scores(1)
                    for m in range(4 * NP_):
                        r, j = m // NP_, m % NP_
                        if m + 2 < 4 * NP_:
                            scores(m + 2)
                        if j < 2 and r < 3:
                            turn_qk(r + 1, j)
                        turn(m)
                        if m:
                            values(m - 1)
                    values(4 * NP_ - 1)
                groups(pe, body)

            @block.vector
            def _(v):
                def body(p, i, first):
                    u0 = 16 * p + 4 * i
                    n0 = NP_ * u0

                    def evac_qk(r, h):
                        u = u0 + r
                        v.wait_ge(tq, 2 * u + h + 1)
                        if not (first and r < 2):
                            v.wait_ge(s_ps, NP_ * (u - 1))
                        dst = kT[:, :, r, :] if h else qT[r % 2][:, :, :]
                        v.tensor_copy(dst, ps_t[:, :, :]).then_inc(qkT, 1)
                        if h and r == 0 and p == 0 and not first:
                            v.wait_ge(qkT, 2 * u + 2)
                            v.tensor_copy(kT[:, :, 4, :], kT[:, :, 0, :]).then_inc(k_again, 1)

                    def bias_max(m):
                        r, j = m // NP_, m % NP_
                        u, n, b = u0 + r, n0 + m, m % 4
                        k0 = 0 if prev(p, r, first) else P
                        if j == 0 and not (first and r < 2):
                            v.wait_ge(o_st[r % 2], 16 * (8 * p + 2 * i + r // 2))
                        if not (first and m < 4):
                            v.wait_ge(p_ps, n - 3)
                        v.wait_ge(s_ps, n + 1)
                        v.memset(tick[:, b:b + 1], 0.0)
                        for h in range(2):
                            hh = head(j, h)
                            v.tensor_tensor_reduce(pr[b][:, h, k0:], ps_s[b][:, h, k0:], g["bias"][:, p, hh, k0:], 1.0, -3e38,
                                                   ALU.add, ALU.max, osb[r % 2][:, AW + hh:AW + hh + 1]).then_inc(mx, 1)
                        v.wait_ge(mx, 2 * n + 2)
                        v.tensor_scalar(nm[b][:, :], osb[r % 2][:, AW + head(j, 0):AW + head(j, 1) + 1:2], -1.0, None,
                                        ALU.mult).then_inc(s_sb, 1)

                    def evac_o(r):
                        u = u0 + r
                        v.wait_ge(pv, NP_ * u + NP_)
                        v.wait_ge(ex, NP_ * u + NP_)
                        v.tensor_copy(osb[r % 2][:, 0:AW], ps_o[:, :, :].rearrange("p h d -> p (h d)")).then_inc(oe, 1)

                    evac_qk(0, 0)
                    evac_qk(0, 1)
                    for m in range(4 * NP_):
                        r, j = m // NP_, m % NP_
                        bias_max(m)
                        if j == 1 and r:
                            evac_o(r - 1)
                        if j in (1, 2) and r < 3:
                            evac_qk(r + 1, j - 1)
                    evac_o(3)
                v.wait_ge(g["bias_in"], 16 * len(DILS))
                groups(v, body)

            @block.scalar
            def _(act):
                def body(p, i, first):
                    n0 = NP_ * (16 * p + 4 * i)
                    for m in range(4 * NP_ + 1):
                        if m < 4 * NP_:
                            r, j = m // NP_, m % NP_
                            k0 = 0 if prev(p, r, first) else P
                            act.wait_ge(s_sb, n0 + m + 1)
                            for h in range(2):
                                hh = head(j, h)
                                e = nc.scalar.activation(pr[m % 4][:, h, k0:], pr[m % 4][:, h, k0:], ACT.Exp,
                                                         bias=nm[m % 4][:, h:h + 1],
                                                         accum_out=osb[r % 2][:, AW + NH + hh:AW + NH + hh + 1])
                            e.then_inc(ex, 1)
                        if m:
                            q = m - 1
                            act.wait_ge(p_ps, n0 + m)
                            if not (first and q < 2):
                                act.wait_ge(pv, n0 + q - 1)
                            w0 = 0 if prev(p, q // NP_, first) else 1
                            nc.scalar.activation(pT[q % 2][:, :, w0:, :], ps_p[q % 2][:, :, w0:, :], ACT.Copy).then_inc(p_sb, 1)
                groups(act, body)


def stage_ssm(nc, g, A, S):
    with Ctx(nc) as c:
        u = c.sb("u_chunks", [P, LC, SW])
        y = c.sb("y_chunks", [P, LC, SW])
        rec = [c.sb(f"rec{b}", [P, REC]) for b in range(2)]
        ug = [c.sb(f"ug{b}", [P, LC, CH_S]) for b in range(2)]
        uT = [c.sb(f"uT{b}", [P, 2, P]) for b in range(2)]
        t = [[c.sb(f"rt{b}{n}", [P, NC]) for n in range(4)] for b in range(2)]
        hin = [c.sb(f"hin{b}", [P, 2, NC + 1]) for b in range(2)]
        psU = [c.ps(f"psU{b}", [P, 2, P]) for b in range(2)]
        psB = [c.ps(f"psB{b}", [P, 2, NC]) for b in range(2)]
        psY = [c.ps(f"psY{b}", [P, LC, CH_S]) for b in range(2)]
        u_in, rec_in = c.sem("u_in"), [c.sem(f"rec_in{b}") for b in range(2)]
        ugd, utp, utd = c.sem("ug_done"), c.sem("uT_psum"), c.sem("uT_done")
        b_ps, h_done, y_ps, y_done = c.sem("b_psum"), c.sem("h_done"), c.sem("y_psum"), c.sem("y_done")
        z0, rs, y_st = c.sem("hin_zero"), c.sem("rec_step"), c.sem("y_st")
        rot, rho = [c.sb(f"rot_sb{n}", [P, NG_S, NC]) for n in range(2)], c.sb("rho_sb", [P, NG_S])
        rot_in = c.sem("rot_in")
        with nc.Block() as block:
            @block.sync
            def _(sp):
                uv = S["qkvu"].rearrange("(j s) n -> j s n", s=LC)
                sp.dma_start(u[:, :, :], uv[:, :, 3 * AW:]).then_inc(u_in, 16)
                for n in range(2):
                    sp.dma_start(rot[n][:, :, :], S["rot"][n]).then_inc(rot_in, 16)
                sp.dma_start(rho[:, :], S["rho"]).then_inc(rot_in, 16)
                for b in range(2):
                    sp.dma_start(rec[b][:, :], S["rec"][b]).then_inc(rec_in[b], 16)
                with sp.Fori(1, NG_S // 2) as i:
                    for b in range(2):
                        sp.wait_ge(y_ps, 2 * i + b - 1)
                        sp.dma_start(rec[b][:, :], S["rec"][ds(2 * i + b, 1)].rearrange("a p n -> (a p) n")).then_inc(rec_in[b], 16)
                sp.wait_ge(y_done, NG_S)
                sp.dma_start(S["y"].rearrange("(j s) n -> j s n", s=LC), y[:, :, :]).then_inc(y_st, 16)
                sp.wait_ge(y_st, 16)

            def pairs(eng, body):
                for b in range(2):
                    body(b, b, True, 0)
                with eng.Fori(1, NG_S // 2) as i:
                    for b in range(2):
                        body(2 * i + b, b, False, i)

            @block.gpsimd
            def _(pool):
                pool.wait_ge(u_in, 16)

                def body(n, b, first, i):
                    if not first:
                        pool.wait_ge(utp, n - 1)
                    nc.gpsimd.tensor_copy(ug[b][:, :, :], u[:, :, ds(CH_S * n, CH_S)]).then_inc(ugd, 1)
                pairs(pool, body)

            @block.tensor
            def _(pe):
                def front(n, b, first, i):
                    pe.wait_ge(ugd, n + 1)
                    if not first:
                        pe.wait_ge(utd, n - 1)
                    for k in range(2):
                        mm = nc.tensor.transpose(psU[b][:, k, :], ug[b][:, 8 * k:8 * k + 8, :].rearrange("p s c -> p (s c)"),
                                                 g["ident"][:, :])
                    mm.then_inc(utp, 1)
                    pe.wait_ge(utd, n + 1)
                    pe.wait_ge(rec_in[b], 16 * i + 16)
                    if not first:
                        pe.wait_ge(h_done, n - 1)
                    for r in range(2):
                        for k in range(2):
                            mm = nc.tensor.matmul(psB[b][:, r, :], rec[b][:, 192 * k + 64 * r:192 * k + 64 * r + P],
                                                  uT[b][:, k, :], start=k == 0, stop=k == 1)
                    mm.then_inc(b_ps, 1)

                def back(n, b, first, i):
                    if not first:
                        pe.wait_ge(y_done, n - 1)
                    o = psY[b][:, :, :].rearrange("p s c -> p (s c)")
                    nc.tensor.matmul(o, uT[b][:, 0, :], rec[b][:, 896:1152], start=True, stop=False, skip_group_check=True)
                    nc.tensor.matmul(o[:, P:], uT[b][:, 1, :], rec[b][:, 1152 + P:1408], start=False, stop=False,
                                     skip_group_check=True)
                    pe.wait_ge(h_done, n + 1)
                    for r in range(2):
                        mm = nc.tensor.matmul(o, hin[b][:, r, 0:NC], rec[b][:, 384 + 256 * r:640 + 256 * r],
                                              start=False, stop=r == 1, skip_group_check=True)
                    mm.then_inc(y_ps, 1)

                front(0, 0, True, 0)
                front(1, 1, True, 0)
                back(0, 0, True, 0)
                with pe.Fori(1, NG_S // 2) as i:
                    front(2 * i, 0, False, i)
                    back(2 * i - 1, 1, False, i)
                    front(2 * i + 1, 1, False, i)
                    back(2 * i, 0, False, i)
                back(NG_S - 1, 1, False, 0)

            @block.scalar
            def _(act):
                def evac(n, b, first, i):
                    act.wait_ge(utp, n + 1)
                    if not first:
                        act.wait_ge(y_ps, n - 1)
                    nc.scalar.activation(uT[b][:, :, :], psU[b][:, :, :], ACT.Copy).then_inc(utd, 1)

                def gelu(n, b, first, i):
                    act.wait_ge(y_ps, n + 1)
                    nc.scalar.activation(y[:, :, ds(CH_S * n, CH_S)], psY[b][:, :, :], ACT.Gelu_apprx_tanh).then_inc(y_done, 1)

                evac(0, 0, True, 0)
                evac(1, 1, True, 0)
                gelu(0, 0, True, 0)
                with act.Fori(1, NG_S // 2) as i:
                    evac(2 * i, 0, False, i)
                    gelu(2 * i - 1, 1, False, i)
                    evac(2 * i + 1, 1, False, i)
                    gelu(2 * i, 0, False, i)
                gelu(NG_S - 1, 1, False, 0)

            @block.vector
            def _(v):
                for b in range(2):
                    v.memset(hin[b][:, :, 0:1], 0.0).then_inc(z0, 1)
                v.wait_ge(rot_in, 48)

                def body(n, b, first, i):
                    v.wait_ge(b_ps, n + 1)
                    x = [a[:, :] for a in t[b]]
                    rr, ri = (r[:, ds(n, 1), :].rearrange("p a j -> p (a j)") for r in rot)
                    v.tensor_tensor(x[0], psB[b][:, 0, :], rr, ALU.mult).then_inc(rs, 1)
                    v.tensor_tensor(x[1], psB[b][:, 1, :], ri, ALU.mult).then_inc(rs, 1)
                    v.wait_ge(rs, 4 * n + 2)
                    v.tensor_tensor(x[2], x[0], x[1], ALU.add).then_inc(rs, 1)
                    v.wait_ge(rs, 4 * n + 3)
                    v.tensor_tensor_scan(x[3], rho[:, ds(n, 1)].to_broadcast([P, NC]), x[2], 0.0, ALU.mult, ALU.add).then_inc(rs, 1)
                    v.wait_ge(rs, 4 * n + 4)
                    if not first:
                        v.wait_ge(y_ps, n - 1)
                    v.tensor_tensor(hin[b][:, 0, 1:], x[3], rr, ALU.mult)
                    v.tensor_tensor(hin[b][:, 1, 1:], x[3], ri, ALU.mult).then_inc(h_done, 1)
                pairs(v, body)


NR = NGR + NE


def stage_merge(nc, g, A, S):
    KA = AW // P
    with Ctx(nc) as c:
        wA = c.sb("w_branch_a", [P, KA, D])
        wS = c.sb("w_branch_s", [P, KA, D])
        wO = c.sb("w_out_sb", [P, KD, D])
        wG = c.sb("w_glu_sb", [P, KA, SW])
        wR = c.sb("w_router", [P, KD, NR])
        bG = c.sb("b_glu_row", [P, SW])
        bR = c.sb("b_router", [P, NR])
        o = [c.sb(f"o_in{b}", [P, 3, AW + 2 * NH]) for b in range(2)]
        y = [c.sb(f"y_in{b}", [P, SW]) for b in range(2)]
        gt = [c.sb(f"gt_in{b}", [P, 2, D]) for b in range(2)]
        x = [c.sb(f"x_in{b}", [P, D]) for b in range(2)]
        acc = [c.sb(f"acc{n}", [P, NH, HD]) for n in range(3)]
        at = c.sb("attn", [P, NH, HD])
        sm = c.sb("ssm_out", [P, SW])
        z = c.sb("glu_z", [P, SW])
        ez = c.sb("glu_e", [P, SW])
        mg = [c.sb(f"mg{n}", [P, D]) for n in range(2)]
        x1 = [c.sb(f"x1_{b}", [P, D]) for b in range(2)]
        xn = [c.sb(f"xn2_{b}", [P, D]) for b in range(2)]
        junk = c.sb("junk_m", [P, D])
        yT, aT, sT = (c.sb(n, [P, KA, P]) for n in ("yT", "aT", "sT"))
        mT = c.sb("mT", [P, KD, P])
        xT = c.sb("x2T", [P, KD, P])
        mx = c.sb("mx_all", [P, NH])
        df = c.sb("m_less", [P, 3, NH])
        wt = c.sb("pat_w", [P, 3, NH])
        wl = c.sb("pat_wl", [P, 3, NH])
        ll = c.sb("pat_l", [P, NH])
        li = c.sb("pat_li", [P, NH])
        wn = c.sb("pat_wn", [P, 3, NH])
        ssq = c.sb("ssq", [P, 3])
        st = {n: c.sb(f"st_{n}", [P, 1]) for n in ("s", "ms", "rt", "rstd", "ms2", "rt2", "rstd2")}
        psT = [c.ps(f"psT{b}", [P, 4, P]) for b in range(2)]
        psA = c.ps("psBA", [P, 2, 512])
        psS = c.ps("psBS", [P, 2, 512])
        psW = c.ps("psW", [P, 2, 512])
        w_in = c.sem("mw_in")
        o_in, y_in, g_in, x_in = ([c.sem(f"{n}{b}") for b in range(2)] for n in ("mo_in", "my_in", "mg_in", "mx_in"))
        y_tp, a_tp, s_tp, m_tp, x_tp = (c.sem(n) for n in ("y_tp", "a_tp", "s_tp", "m_tp", "x_tp"))
        y_T, a_T, s_T, m_T, x_T = (c.sem(n) for n in ("y_T", "a_T", "s_T", "m_T", "x_T"))
        glu_mm, a_mm, s_mm, w_mm, r_mm = (c.sem(n) for n in ("glu_mm", "a_mm", "s_mm", "w_mm", "r_mm"))
        cmb, cw, at_d = c.sem("comb_step"), c.sem("comb_exp"), c.sem("attn_done")
        z_d, ez_d, gl, s_d = c.sem("z_done"), c.sem("ez_done"), c.sem("glu_step"), c.sem("ssm_gated")
        mgs, m_d = c.sem("merge_step"), c.sem("merged")
        sq, ms_d, rt_d, x1s, x1_d, xn_d = (c.sem(n) for n in ("msq", "mms", "mrt", "x1_step", "x1_done", "xn2_done"))
        lg_d = c.sem("logits_done")
        x1_st, xn_st = ([c.sem(f"{n}{b}") for b in range(2)] for n in ("x1_st", "xn2_st"))
        NSTEP = NT + 2

        def real(t):
            return not isinstance(t, int) or 0 <= t < NT

        def past(t, n):
            return not isinstance(t, int) or t >= n

        def steps(eng, body):
            for s in range(4):
                body(s, s // 2, s % 2)
            with eng.Fori(2, NT // 2 - 1) as i:
                for b in range(2):
                    body(2 * i + b, i, b)
            for s in range(NT - 2, NSTEP):
                body(s, s // 2, s % 2)

        def tile(dram, t):
            return dram.rearrange("(t p) n -> t p n", p=P)[ds(t, 1)].rearrange("a p n -> (a p) n")

        with nc.Block() as block:
            @block.sync
            def _(sp):
                def load_oyg(t, b):
                    for n in range(3):
                        sp.dma_start(o[b][:, n, :], tile(S["o"][n], t)).then_inc(o_in[b], 16)
                    sp.dma_start(y[b][:, :], tile(S["y"], t)).then_inc(y_in[b], 16)
                    sp.dma_start(gt[b][:, :, :].rearrange("p a n -> p (a n)"), tile(S["gates"], t)).then_inc(g_in[b], 16)

                def load_x(t, b):
                    sp.dma_start(x[b][:, :], tile(A["x"][0], t)).then_inc(x_in[b], 16)

                sp.dma_start(wG[:, :, :], A["w_glu"][0].rearrange("(k p) n -> p k n", p=P)).then_inc(w_in, 16)
                sp.dma_start(bG[:, :], A["b_glu"].to_broadcast([P, SW])).then_inc(w_in, 16)
                load_oyg(0, 0)
                for dst, name in ((wA, "w_branch_attn"), (wS, "w_branch_ssm")):
                    sp.dma_start(dst[:, :, :], A[name][0].rearrange("(k p) n -> p k n", p=P)).then_inc(w_in, 16)
                load_oyg(1, 1)
                load_x(0, 0)
                load_x(1, 1)
                sp.dma_start(wO[:, :, :], A["w_out"][0].rearrange("(k p) n -> p k n", p=P)).then_inc(w_in, 16)
                sp.dma_start(wR[:, :, 0:NGR], A["w_router_group"][0].rearrange("(k p) n -> p k n", p=P)).then_inc(w_in, 16)
                sp.dma_start(wR[:, :, NGR:], A["w_router_expert"][0].rearrange("(k p) n -> p k n", p=P)).then_inc(w_in, 16)
                sp.dma_start(bR[:, 0:NGR], A["b_router_group"].to_broadcast([P, NGR])).then_inc(w_in, 16)
                sp.dma_start(bR[:, NGR:], A["b_router_expert"].to_broadcast([P, NE])).then_inc(w_in, 16)

                def body(s, i, b):
                    if real(s - 2):
                        sp.wait_ge(x1_d, s - 1)
                        sp.dma_start(tile(S["x1"], s - 2), x1[b][:, :]).then_inc(x1_st[b], 16)
                        if real(s):
                            load_x(s, b)
                        sp.wait_ge(xn_d, s - 1)
                        sp.dma_start(tile(S["xn2"], s - 2), xn[b][:, :]).then_inc(xn_st[b], 16)
                    if real(s) and real(s + 2):
                        sp.wait_ge(at_d, s + 1)
                        sp.wait_ge(s_d, s + 1)
                        sp.wait_ge(m_d, s + 1)
                        load_oyg(s + 2, b)
                steps(sp, body)
                for b in range(2):
                    sp.wait_ge(x1_st[b], 16 * NT // 2)
                    sp.wait_ge(xn_st[b], 16 * NT // 2)

            @block.tensor
            def _(pe):
                def turn(bank, src, sem):
                    n = src.shape[1] // P
                    for k in range(n):
                        mm = nc.tensor.transpose(psT[bank][:, k, :], src[:, k * P:(k + 1) * P], g["ident"][:, :])
                    mm.then_inc(sem, 1)

                def product(o_, xT_, w_, width):
                    for h in range((width + 511) // 512):
                        n = min(512, width - 512 * h)
                        for k in range(w_.shape[1]):
                            mm = nc.tensor.matmul(o_[:, h, 0:n], xT_[:, k, :], w_[:, k, 512 * h:512 * h + n],
                                                  start=k == 0, stop=k == w_.shape[1] - 1)
                    return mm

                def body(s, i, b):
                    if real(s):
                        pe.wait_ge(y_in[b], 16 * i + 16)
                        if past(s, 1):
                            pe.wait_ge(s_T, s)
                        turn(0, y[b], y_tp)
                        pe.wait_ge(at_d, s + 1)
                        if past(s, 2):
                            pe.wait_ge(m_T, 2 * s - 2)
                        turn(1, at[:, :, :].rearrange("p h d -> p (h d)"), a_tp)
                        pe.wait_ge(y_T, s + 1)
                        if past(s, 1):
                            pe.wait_ge(m_d, s)
                        product(psS, yT, wG, SW).then_inc(glu_mm, 1)
                        pe.wait_ge(a_T, s + 1)
                        product(psA, aT, wA, D).then_inc(a_mm, 1)
                    if real(s - 2):
                        pe.wait_ge(xn_d, s - 1)
                        if not real(s):
                            pe.wait_ge(s_T, NT)
                            pe.wait_ge(m_T, 2 * (s - 1))
                            pe.wait_ge(m_d, NT)
                        turn(0, xn[b][:, 0:512], x_tp)
                        turn(1, xn[b][:, 512:1024], x_tp)
                        pe.wait_ge(x_T, 2 * (s - 1))
                        for k in range(KD):
                            mm = nc.tensor.matmul(psS[:, 1, 0:NR], xT[:, k, :], wR[:, k, :], start=k == 0, stop=k == KD - 1)
                        mm.then_inc(r_mm, 1)
                    if real(s - 1):
                        pe.wait_ge(m_d, s)
                        turn(0, mg[0][:, 0:512], m_tp)
                        turn(1, mg[0][:, 512:1024], m_tp)
                    if real(s):
                        pe.wait_ge(s_d, s + 1)
                        if past(s, 1):
                            pe.wait_ge(m_T, 2 * s - 1)
                        turn(0, sm, s_tp)
                        pe.wait_ge(s_T, s + 1)
                        if past(s, 2):
                            pe.wait_ge(lg_d, s - 1)
                        product(psS, sT, wS, D).then_inc(s_mm, 1)
                    if real(s - 1):
                        pe.wait_ge(m_T, 2 * s)
                        if past(s, 2):
                            pe.wait_ge(x1_d, s - 1)
                        product(psW, mT, wO, D).then_inc(w_mm, 1)

                pe.wait_ge(w_in, 16 * 9)
                steps(pe, body)

            @block.scalar
            def _(act):
                def leave(bank, dst, tp, n_tp, used, n_used, done):
                    act.wait_ge(tp, n_tp)
                    if n_used is not None:
                        act.wait_ge(used, n_used)
                    nc.scalar.activation(dst, psT[bank][:, :, :], ACT.Copy).then_inc(done, 1)

                def weights(t):
                    act.wait_ge(cmb, 12 * t + 3)
                    nc.scalar.activation(wt[:, :, :], df[:, :, :], ACT.Exp).then_inc(cw, 1)

                def root(dst, src):
                    nc.scalar.activation(dst[:, :], src[:, :], ACT.Sqrt).then_inc(rt_d, 1)

                def body(s, i, b):
                    t = s - 2
                    if real(t):
                        act.wait_ge(w_mm, t + 1)
                        if past(t, 1):
                            act.wait_ge(sq, 2 * t)
                            act.wait_ge(ms_d, 2 * t)
                        nc.scalar.activation(junk[:, :], psW[:, :, :].rearrange("p a n -> p (a n)"), ACT.Square,
                                             accum_out=ssq[:, 0:1]).then_inc(sq, 1)
                    if real(s):
                        leave(0, yT[:, :, :], y_tp, s + 1, glu_mm, s if past(s, 1) else None, y_T)
                        leave(1, aT[:, :, :], a_tp, s + 1, a_mm, s if past(s, 1) else None, a_T)
                    if real(t):
                        act.wait_ge(ms_d, 2 * t + 1)
                        root(st["rt"], st["ms"])
                        act.wait_ge(x1_d, t + 1)
                        act.wait_ge(sq, 2 * t + 1)
                        nc.scalar.activation(junk[:, :], x1[b][:, :], ACT.Square, accum_out=ssq[:, 1:2]).then_inc(sq, 1)
                        act.wait_ge(ms_d, 2 * t + 2)
                        root(st["rt2"], st["ms2"])
                    if real(s):
                        act.wait_ge(z_d, s + 1)
                        nc.scalar.activation(ez[:, :], z[:, :], ACT.Exp, scale=-1.0).then_inc(ez_d, 1)
                    if real(t):
                        for h in range(2):
                            act.wait_ge(x_tp, 2 * t + h + 1)
                            if past(s, 3) and h == 0:
                                act.wait_ge(r_mm, t)
                            for k in range(4):
                                kk = 4 * h + k
                                e = nc.scalar.activation(xT[:, kk, :], psT[h][:, k, :], ACT.Identity,
                                                         bias=g["bcol"][:, 1, kk:kk + 1], scale=g["acol"][:, 1, kk:kk + 1])
                            e.then_inc(x_T, 1)
                    if real(s - 1):
                        for h in range(2):
                            leave(h, mT[:, 4 * h:4 * h + 4, :], m_tp, 2 * (s - 1) + h + 1, w_mm, s - 1 if past(s, 2) else None, m_T)
                    if real(s):
                        leave(0, sT[:, :, :], s_tp, s + 1, s_mm, s if past(s, 1) else None, s_T)
                    if real(s + 1) and real(s):
                        weights(s + 1)

                weights(0)
                steps(act, body)

            @block.vector
            def _(v):
                def did(ins, sem, n):
                    ins.then_inc(sem, 1)
                    v.wait_ge(sem, n)

                def combine(t, i, b):
                    n = 12 * t
                    v.wait_ge(o_in[b], 48 * i + 48)
                    m, l = o[b][:, :, AW:AW + NH], o[b][:, :, AW + NH:]
                    did(v.tensor_tensor(mx[:, :], m[:, 0, :], m[:, 1, :], ALU.max), cmb, n + 1)
                    did(v.tensor_tensor(mx[:, :], mx[:, :], m[:, 2, :], ALU.max), cmb, n + 2)
                    did(v.tensor_tensor(df[:, :, :], m, mx[:, :].unsqueeze(1).to_broadcast([P, 3, NH]), ALU.subtract), cmb, n + 3)
                    v.wait_ge(cw, t + 1)
                    did(v.tensor_tensor(wl[:, :, :], wt[:, :, :], l, ALU.mult), cmb, n + 4)
                    did(v.tensor_tensor(ll[:, :], wl[:, 0, :], wl[:, 1, :], ALU.add), cmb, n + 5)
                    did(v.tensor_tensor(ll[:, :], ll[:, :], wl[:, 2, :], ALU.add), cmb, n + 6)
                    did(v.reciprocal(li[:, :], ll[:, :]), cmb, n + 7)
                    did(v.tensor_tensor(wn[:, :, :], wt[:, :, :], li[:, :].unsqueeze(1).to_broadcast([P, 3, NH]), ALU.mult), cmb, n + 8)
                    for p in range(3):
                        v.tensor_tensor(acc[p][:, :, :], o[b][:, p, 0:AW].rearrange("p (h d) -> p h d", d=HD),
                                        wn[:, p, :].unsqueeze(2).to_broadcast([P, NH, HD]), ALU.mult).then_inc(cmb, 1)
                    v.wait_ge(cmb, n + 11)
                    did(v.tensor_tensor(acc[0][:, :, :], acc[0][:, :, :], acc[1][:, :, :], ALU.add), cmb, n + 12)
                    if past(t, 1):
                        v.wait_ge(a_tp, t)
                    v.tensor_tensor(at[:, :, :], acc[0][:, :, :], acc[2][:, :, :], ALU.add).then_inc(at_d, 1)

                def gated(t, b):
                    v.wait_ge(glu_mm, t + 1)
                    if past(t, 1):
                        v.wait_ge(ez_d, t)
                    v.tensor_tensor(z[:, :], psS[:, 0, :], bG[:, :], ALU.add).then_inc(z_d, 1)
                    v.wait_ge(ez_d, t + 1)
                    did(v.tensor_scalar(ez[:, :], ez[:, :], 1.0, None, ALU.add), gl, 2 * t + 1)
                    did(v.reciprocal(ez[:, :], ez[:, :]), gl, 2 * t + 2)
                    if past(t, 1):
                        v.wait_ge(s_tp, t)
                    v.tensor_tensor(sm[:, :], ez[:, :], y[b][:, :], ALU.mult).then_inc(s_d, 1)

                def logits(t):
                    v.wait_ge(r_mm, t + 1)
                    v.tensor_tensor(g["logits"][:, ds(t, 1), :].rearrange("p a n -> p (a n)"), psS[:, 1, 0:NR], bR[:, :],
                                    ALU.add).then_inc(lg_d, 1)

                def residual(t, i, b):
                    v.wait_ge(sq, 2 * t + 1)
                    if past(t, 1):
                        v.wait_ge(rt_d, 2 * t)
                    v.tensor_scalar(st["ms"][:, :], ssq[:, 0:1], 1.0 / D, EPS, ALU.mult, ALU.add).then_inc(ms_d, 1)
                    v.wait_ge(rt_d, 2 * t + 1)
                    did(v.reciprocal(st["rstd"][:, :], st["rt"][:, :]), x1s, 3 * t + 1)
                    if past(t, 2):
                        v.wait_ge(x1_st[b], 16 * i)
                    v.wait_ge(x_in[b], 16 * i + 16)
                    did(v.scalar_tensor_tensor(out=x1[b][:, :], in0=psW[:, :, :].rearrange("p a n -> p (a n)"),
                                               scalar=st["rstd"][:, 0:1], in1=g["grow"][:, 0, :], op0=ALU.mult, op1=ALU.mult),
                        x1s, 3 * t + 2)
                    v.tensor_tensor(x1[b][:, :], x1[b][:, :], x[b][:, :], ALU.add).then_inc(x1_d, 1)
                    v.wait_ge(sq, 2 * t + 2)
                    v.tensor_scalar(st["ms2"][:, :], ssq[:, 1:2], 1.0 / D, EPS, ALU.mult, ALU.add).then_inc(ms_d, 1)
                    v.wait_ge(rt_d, 2 * t + 2)
                    did(v.reciprocal(st["rstd2"][:, :], st["rt2"][:, :]), x1s, 3 * t + 3)
                    if past(t, 2):
                        v.wait_ge(xn_st[b], 16 * i)
                        v.wait_ge(x_tp, 2 * t - 2)
                    v.tensor_scalar(xn[b][:, :], x1[b][:, :], st["rstd2"][:, 0:1], None, ALU.mult).then_inc(xn_d, 1)

                def merge(t, i, b):
                    v.wait_ge(s_mm, t + 1)
                    v.wait_ge(a_mm, t + 1)
                    v.wait_ge(g_in[b], 16 * i + 16)
                    if past(t, 1):
                        v.wait_ge(m_tp, 2 * t)
                    flat = [p_[:, :, :].rearrange("p a n -> p (a n)") for p_ in (psA, psS)]
                    v.tensor_tensor(mg[0][:, :], flat[0], gt[b][:, 0, :], ALU.mult).then_inc(mgs, 1)
                    v.tensor_tensor(mg[1][:, :], flat[1], gt[b][:, 1, :], ALU.mult).then_inc(mgs, 1)
                    v.wait_ge(mgs, 2 * t + 2)
                    v.tensor_tensor(mg[0][:, :], mg[0][:, :], mg[1][:, :], ALU.add).then_inc(m_d, 1)

                def body(s, i, b):
                    if real(s - 2):
                        residual(s - 2, i - 1, b)
                    if real(s):
                        gated(s, b)
                    if real(s - 2):
                        logits(s - 2)
                    if real(s + 1) and real(s):
                        combine(s + 1, i + b, 1 - b)
                    if real(s):
                        merge(s, i, b)

                v.wait_ge(w_in, 16 * 9)
                combine(0, 0, 0)
                steps(v, body)


def stage_route(nc, g, A, S):
    with Ctx(nc) as c:
        def sb(name, shape, dt=F32):
            return c.sb("r_" + name, shape, dt)

        lg = g["logits"]
        w8, w8i = sb("w8", [P, EPG]), sb("w8i", [P, EPG], I32)
        bi, bf = sb("bi", [P, NBLK], I32), sb("bf", [P, NBLK])
        tok = sb("tok", [P, NT], I32)
        tri, one = sb("tri", [P, P]), sb("one", [P, P])
        gm, gs, gate = (sb(n, [P, NT]) for n in ("gm", "gs", "gate"))
        gd, ohg, gt = (sb(n, [P, NT, NGR]) for n in ("gd", "ohg", "gt"))
        fm = sb("fm", [P, NT])
        full = sb("full", [P, NT, NGR, EPG])
        ein, e2, ohk, et = sb("ein", [P, NT, EPG]), sb("e2", [P, NT, EPG]), [sb(f"ohk{k}", [P, NT, EPG]) for k in range(2)], sb("et", [P, NT, EPG])
        v12 = [sb(f"v{k}", [P, NT]) for k in range(2)]
        dv, p1 = sb("dv", [P, NT]), sb("p1", [P, NT])
        OH = [sb(f"OH{k}", [P, NT, NGR, EPG]) for k in range(2)]
        oh = sb("OHs", [P, NT, NE])
        tot = sb("tot", [P, NT, NE])
        pre = sb("pre", [P, NT + 1, NE])
        rank = sb("rank", [P, NT, NE])
        nb, cum, st0 = (sb(n, [P, NE]) for n in ("nb", "cum", "st0"))
        cmp_ = sb("cmp", [P, NBLK, NE])
        be, nr, rn, par = (sb(n, [P, NBLK]) for n in ("be", "nr", "rn", "par"))
        npf = sb("npf", [P, 1])
        dest_f = sb("dest_f", [P, NT])
        zi = sb("zi", [P, NBLK + 1], I32)
        ps = [c.ps(f"ps_rank{n}", [P, 512]) for n in range(2)]
        io, tri0 = c.sem("r_iota"), c.sem("r_tri0")
        st_, ex, exd, mm = c.sem("r_step"), c.sem("r_exp_in"), c.sem("r_exp"), c.sem("rank_mm")
        ohd, z_st, sc, ready, tb = c.sem("r_oh"), c.sem("r_zero_st"), c.sem("r_scatter"), c.sem("r_dest"), c.sem("r_table")
        zd = c.sem("r_zero")
        rows = S["row_tok"]

        with nc.Block() as block:
            @block.gpsimd
            def _(pool):
                nc.gpsimd.iota(w8i[:, :], [[-1, EPG]], base=EPG, channel_multiplier=0).then_inc(io, 1)
                nc.gpsimd.iota(bi[:, :], [[1, NBLK]], base=0, channel_multiplier=0).then_inc(io, 1)
                nc.gpsimd.iota(tok[:, :], [[P, NT]], base=0, channel_multiplier=1).then_inc(io, 1)
                nc.gpsimd.memset(one[:, :], 1.0).then_inc(io, 1)
                nc.gpsimd.memset(tri[:, :], 1.0).then_inc(tri0, 1)
                pool.wait_ge(tri0, 1)
                nc.gpsimd.affine_select(out=tri[:, :], in_=tri[:, :], compare_op=ALU.is_gt, fill=0.0, base=0,
                                        pattern=[[1, P]], channel_multiplier=-1).then_inc(io, 1)
                pool.wait_ge(io, 5)
                pool.wait_ge(z_st, 16)
                pool.wait_ge(ready, 2)
                for k in range(2):
                    for t in range(NT):
                        pool.indirect_dma_start(rows, bass.IndirectOffsetOnAxis(g["dest"][:, k, t:t + 1], 0),
                                                tok[:, t:t + 1], None).then_inc(sc, 16)
                pool.wait_ge(sc, 16 * 2 * NT)

            @block.sync
            def _(sp):
                sp.wait_ge(zd, 1)
                sp.dma_start(rows.rearrange("(b p) a -> p (b a)", p=P), zi[:, :],
                             allow_slow_non_contiguous=True).then_inc(z_st, 16)
                sp.wait_ge(sc, 16 * 2 * NT)
                sp.dma_start(g["rowtok"][:, :], rows.rearrange("(b p) a -> p (b a)", p=P),
                             allow_slow_non_contiguous=True).then_inc(tb, 16)
                sp.wait_ge(tb, 16)

            @block.scalar
            def _(act):
                act.wait_ge(ex, 1)
                nc.scalar.activation(gd[:, :, :], gd[:, :, :], ACT.Exp).then_inc(exd, 1)
                act.wait_ge(ex, 2)
                nc.scalar.activation(dv[:, :], dv[:, :], ACT.Exp).then_inc(exd, 1)

            @block.tensor
            def _(pe):
                pe.wait_ge(io, 5)
                pe.wait_ge(ohd, 1)
                f = oh[:, :, :].rearrange("p t e -> p (t e)")
                nc.tensor.matmul(ps[0][:, :], tri[:, :], f, start=True, stop=True).then_inc(mm, 1)
                nc.tensor.matmul(ps[1][:, :], one[:, :], f, start=True, stop=True).then_inc(mm, 1)

            @block.vector
            def _(v):
                n_ = [0]

                def did(ins):
                    n_[0] += 1
                    ins.then_inc(st_, 1)
                    v.wait_ge(st_, n_[0])

                def tt(o, a, b, op):
                    did(v.tensor_tensor(o, a, b, op))

                def ts(o, a, s1, s2, op0, op1=None):
                    did(v.tensor_scalar(o, a, s1, s2, op0, op1) if op1 is not None else v.tensor_scalar(o, a, s1, None, op0))

                def floor(o, a, scale, off):
                    big = 1.5 * 2 ** 23
                    ts(o, a, scale, off, ALU.mult, ALU.add)
                    ts(o, o, big, None, ALU.add)
                    ts(o, o, big, None, ALU.subtract)

                def first_max(o, vals, top, tmp, k):
                    w = w8[:, EPG - k:].unsqueeze(1).to_broadcast([P, NT, k])
                    did(v.tensor_reduce(top, vals, AX_X, ALU.max))
                    tt(tmp, vals, top.unsqueeze(2).to_broadcast([P, NT, k]), ALU.is_equal)
                    tt(tmp, tmp, w, ALU.mult)
                    did(v.tensor_reduce(fm[:, :], tmp, AX_X, ALU.max))
                    tt(o, w, fm[:, :].unsqueeze(2).to_broadcast([P, NT, k]), ALU.is_equal)

                v.memset(zi[:, :], 0).then_inc(zd, 1)
                v.wait_ge(io, 5)
                did(v.tensor_copy(w8[:, :], w8i[:, :]))
                did(v.tensor_copy(bf[:, :], bi[:, :]))
                gl, el = lg[:, :, 0:NGR], lg[:, :, NGR:].rearrange("p t (a b) -> p t a b", b=EPG)
                first_max(ohg[:, :, :], gl, gm[:, :], gt[:, :, :], NGR)
                v.tensor_tensor(gd[:, :, :], gl, gm[:, :].unsqueeze(2).to_broadcast([P, NT, NGR]), ALU.subtract).then_inc(ex, 1)
                tt(full[:, :, :, :], el, ohg[:, :, :].unsqueeze(3).to_broadcast([P, NT, NGR, EPG]), ALU.mult)
                tt(ein[:, :, :], full[:, :, 0, :], full[:, :, 1, :], ALU.add)
                tt(et[:, :, :], full[:, :, 2, :], full[:, :, 3, :], ALU.add)
                tt(ein[:, :, :], ein[:, :, :], et[:, :, :], ALU.add)
                first_max(ohk[0][:, :, :], ein[:, :, :], v12[0][:, :], et[:, :, :], EPG)
                did(v.scalar_tensor_tensor(out=e2[:, :, :], in0=ohk[0][:, :, :], scalar=-3e38, in1=ein[:, :, :],
                                           op0=ALU.mult, op1=ALU.add))
                first_max(ohk[1][:, :, :], e2[:, :, :], v12[1][:, :], et[:, :, :], EPG)
                for k in range(2):
                    tt(OH[k][:, :, :, :], ohg[:, :, :].unsqueeze(3).to_broadcast([P, NT, NGR, EPG]),
                       ohk[k][:, :, :].unsqueeze(2).to_broadcast([P, NT, NGR, EPG]), ALU.mult)
                flat = [x[:, :, :, :].rearrange("p t a b -> p t (a b)") for x in OH]
                tt(oh[:, :, :], flat[0], flat[1], ALU.add)
                v.engine_nop().then_inc(ohd, 1)
                tt(dv[:, :], v12[1][:, :], v12[0][:, :], ALU.subtract)
                v.engine_nop().then_inc(ex, 1)
                v.wait_ge(exd, 1)
                did(v.tensor_reduce(gs[:, :], gd[:, :, :], AX_X, ALU.add))
                did(v.reciprocal(gate[:, :], gs[:, :]))
                v.wait_ge(exd, 2)
                ts(p1[:, :], dv[:, :], 1.0, None, ALU.add)
                did(v.reciprocal(p1[:, :], p1[:, :]))
                tt(g["wgt"][:, 0, :], p1[:, :], gate[:, :], ALU.mult)
                tt(g["wgt"][:, 1, :], g["wgt"][:, 0, :], dv[:, :], ALU.mult)
                v.wait_ge(mm, 2)
                did(v.tensor_copy(tot[:, :, :].rearrange("p t e -> p (t e)"), ps[1][:, :]))
                did(v.memset(pre[:, 0, :], 0.0))
                for t in range(NT):
                    tt(pre[:, t + 1, :], pre[:, t, :], tot[:, t, :], ALU.add)
                tt(rank[:, :, :].rearrange("p t e -> p (t e)"), ps[0][:, :], pre[:, 0:NT, :].rearrange("p t e -> p (t e)"), ALU.add)
                floor(nb[:, :], pre[:, NT, :], 1.0 / P, (P - 1) / P - 0.5 + 0.5 / P)
                did(v.tensor_tensor_scan(cum[:, :], one[:, 0:NE], nb[:, :], 0.0, ALU.mult, ALU.add))
                tt(st0[:, :], cum[:, :], nb[:, :], ALU.subtract)
                ts(st0[:, :], st0[:, :], float(P), None, ALU.mult)
                tt(rank[:, :, :], rank[:, :, :], st0[:, :].unsqueeze(1).to_broadcast([P, NT, NE]), ALU.add)
                for k in range(2):
                    tt(tot[:, :, :], flat[k], rank[:, :, :], ALU.mult)
                    did(v.tensor_reduce(dest_f[:, :], tot[:, :, :], AX_X, ALU.add))
                    v.tensor_copy(g["dest"][:, k, :], dest_f[:, :]).then_inc(ready, 1)
                    v.wait_ge(ready, k + 1)
                tt(cmp_[:, :, :], cum[:, :].unsqueeze(1).to_broadcast([P, NBLK, NE]),
                   bf[:, :].unsqueeze(2).to_broadcast([P, NBLK, NE]), ALU.is_le)
                did(v.tensor_reduce(be[:, :], cmp_[:, :, :], AX_X, ALU.add))
                ts(be[:, :], be[:, :], float(NE - 1), None, ALU.min)
                did(v.memset(nr[:, 0:1], 1.0))
                tt(nr[:, 1:], be[:, 1:], be[:, 0:NBLK - 1], ALU.not_equal)
                did(v.tensor_tensor_scan(rn[:, :], one[:, 0:NBLK], nr[:, :], 0.0, ALU.mult, ALU.add))
                floor(par[:, :], rn[:, :], 0.5, -0.25)
                did(v.scalar_tensor_tensor(out=par[:, :], in0=par[:, :], scalar=-2.0, in1=rn[:, :], op0=ALU.mult, op1=ALU.add))
                floor(npf[:, :], cum[:, NE - 1:NE], 0.5, 0.25)
                did(v.tensor_copy(g["blk"][0:1, 0, 0:NBLK], be[0:1, :]))
                did(v.tensor_copy(g["blk"][0:1, 1, 0:NBLK], nr[0:1, :]))
                did(v.tensor_copy(g["blk"][0:1, 2, 0:NBLK], par[0:1, :]))
                did(v.tensor_copy(g["blk"][0:1, 3, 0:1], npf[0:1, :]))
                ts(npf[:, :], npf[:, :], -1.0, NBLK / 2, ALU.mult, ALU.add)
                did(v.tensor_copy(g["blk"][0:1, 3, 1:2], npf[0:1, :]))
                did(v.memset(g["blk"][0:1, 0:3, NBLK:NBLK + 1], 0))


def stage_experts(nc, g, A, S):
    with Ctx(nc) as c:
        w13 = c.sb("w13", [P, 2, 2, KD, DE])
        w2 = c.sb("w2_sb", [P, 2, KE, D])
        idx = [c.sb(f"idx{b}", [P, 1], I32) for b in range(2)]
        tick, tick0 = c.sb("tick_x", [P, 1]), c.sem("tick_x0")
        xg = [c.sb(f"xg{b}", [P, D]) for b in range(2)]
        xT = [c.sb(f"xgT{b}", [P, KD, P]) for b in range(2)]
        si = c.sb("silu", [P, DE])
        ac = c.sb("act", [P, DE])
        aT = c.sb("actT", [P, KE, P])
        yo = [c.sb(f"yo{b}", [P, D]) for b in range(2)]
        psT = [c.ps(f"ps_xT{h}", [P, 4, P]) for h in range(2)]
        psA = c.ps("ps_aT", [P, KE, P])
        psG, psU = c.ps("ps_g", [P, 512]), c.ps("ps_u", [P, 512])
        psY = c.ps("ps_y", [P, 2, 512])
        w_in = [c.sem(f"we_in{b}") for b in range(2)]
        x_in = [c.sem(f"xg_in{b}") for b in range(2)]
        ix, x_tp, x_T = c.sem("idx_done"), c.sem("xg_tp"), [c.sem(f"xgT_done{h}") for h in range(2)]
        g_mm, u_mm, si_d, ac_d = c.sem("g_mm"), c.sem("u_mm"), c.sem("silu_done"), c.sem("act_done")
        a_tp, a_T, y_mm, y_d = c.sem("a_tp2"), c.sem("a_T2"), c.sem("y_mm"), c.sem("yo_done")
        y_st = [c.sem(f"yo_st{b}") for b in range(2)]
        zero, pad_st = c.sb("zero_rows", [P, D]), c.sem("pad_st")
        blk = g["blk"]

        def pairs(eng):
            return eng.value_load(blk[0:1, 3, 0:1], min_val=1, max_val=NBLK // 2)

        with nc.Block() as block:
            @block.sync
            def _(sp):
                n_pairs = pairs(sp)

                def weights(n, b):
                    e = sp.value_load(blk[0:1, 0, ds(n, 1)], min_val=0, max_val=NE - 1)
                    new = sp.value_load(blk[0:1, 1, ds(n, 1)], min_val=0, max_val=1)
                    side = sp.value_load(blk[0:1, 2, ds(n, 1)], min_val=0, max_val=1)
                    for m, name in enumerate(("w1", "w3")):
                        src = A[name][0].rearrange("e (k p) n -> e p k n", p=P)[ds(e, 1)].rearrange("a p k n -> (a p) k n")
                        dst = w13[:, ds(side, 1), m, :, :].rearrange("p a k n -> p (a k) n")
                        sp.dma_start(dst, src, cond=new > 0).then_inc(w_in[b], 16)
                    src = A["w2"][0].rearrange("e (k p) n -> e p k n", p=P)[ds(e, 1)].rearrange("a p k n -> (a p) k n")
                    sp.dma_start(w2[:, ds(side, 1), :, :].rearrange("p a k n -> p (a k) n"), src, cond=new > 0).then_inc(w_in[b], 16)

                weights(0, 0)
                sp.wait_ge(pad_st, 16)
                with sp.Fori(n_pairs, NBLK // 2) as i:
                    for b in range(2):
                        sp.dma_start(S["yb"].rearrange("(t p) n -> t p n", p=P)[ds(2 * i + b, 1)].rearrange("a p n -> (a p) n"),
                                     zero[:, :]).then_inc(pad_st, 16)
                with sp.Fori(0, n_pairs) as i:
                    for b in range(2):
                        n = 2 * i + b
                        sp.wait_ge(y_mm, n)
                        weights(n + 1, 1 - b)
                        sp.wait_ge(y_d, n + 1)
                        sp.dma_start(S["yb"].rearrange("(t p) n -> t p n", p=P)[ds(n, 1)].rearrange("a p n -> (a p) n"),
                                     yo[b][:, :]).then_inc(y_st[b], 16)

            @block.gpsimd
            def _(pool):
                n_pairs = pairs(pool)
                nc.gpsimd.memset(tick[:, :], 0.0).then_inc(tick0, 1)
                pool.wait_ge(tick0, 1)

                def gather(n, b):
                    nc.gpsimd.tensor_copy(idx[b][:, :], g["rowtok"][:, ds(n, 1)]).then_inc(ix, 1)
                    pool.wait_ge(ix, n + 1)
                    nc.gpsimd.tensor_tensor(tick[:, :], tick[:, :], tick[:, :], ALU.add)
                    pool.indirect_dma_start(xg[b][:, :], None, S["xn2"],
                                            bass.IndirectOffsetOnAxis(idx[b][:, 0:1], 0)).then_inc(x_in[b], 16)

                gather(0, 0)
                with pool.Fori(0, n_pairs) as i:
                    for b in range(2):
                        n = 2 * i + b
                        pool.wait_ge(x_tp, 2 * n)
                        gather(n + 1, 1 - b)

            @block.tensor
            def _(pe):
                n_pairs = pairs(pe)
                n_empty = pe.value_load(blk[0:1, 3, 1:2], min_val=0, max_val=NBLK // 2)

                def turn(n, b, i):
                    pe.wait_ge(x_in[b], 16 * i + 16)
                    for h in range(2):
                        pe.wait_ge(x_T[h], n)
                        for k in range(4):
                            mm = nc.tensor.transpose(psT[h][:, k, :], xg[b][:, (4 * h + k) * P:(4 * h + k + 1) * P], g["ident"][:, :])
                        mm.then_inc(x_tp, 1)

                turn(0, 0, 0)
                with pe.Fori(0, n_pairs) as i:
                    for b in range(2):
                        n = 2 * i + b
                        side = pe.value_load(blk[0:1, 2, ds(n, 1)], min_val=0, max_val=1)
                        pe.wait_ge(w_in[b], 48 * i + 48)
                        for h in range(2):
                            pe.wait_ge(x_T[h], n + 1)
                        for m, (o, s, free) in enumerate(((psG, g_mm, ac_d), (psU, u_mm, ac_d))):
                            pe.wait_ge(free, n)
                            for k in range(KD):
                                mm = nc.tensor.matmul(o[:, :], xT[b][:, k, :],
                                                      w13[:, ds(side, 1), m, k, :].rearrange("p a n -> p (a n)"),
                                                      start=k == 0, stop=k == KD - 1)
                            mm.then_inc(s, 1)
                        turn(n + 1, 1 - b, i + b)
                        pe.wait_ge(ac_d, n + 1)
                        pe.wait_ge(a_T, n)
                        for k in range(KE):
                            mm = nc.tensor.transpose(psA[:, k, :], ac[:, k * P:(k + 1) * P], g["ident"][:, :])
                        mm.then_inc(a_tp, 1)
                        pe.wait_ge(a_T, n + 1)
                        pe.wait_ge(y_d, n)
                        for h in range(2):
                            for k in range(KE):
                                mm = nc.tensor.matmul(psY[:, h, :], aT[:, k, :],
                                                      w2[:, ds(side, 1), k, 512 * h:512 * h + 512].rearrange("p a n -> p (a n)"),
                                                      start=k == 0, stop=k == KE - 1)
                        mm.then_inc(y_mm, 1)
                for b in range(2):
                    pe.wait_ge(x_in[b], 16 * n_pairs + 16 * (1 - b))
                    pe.wait_ge(w_in[b], 48 * n_pairs + 48 * (1 - b))
                    pe.wait_ge(y_st[b], 16 * n_pairs)
                pe.wait_ge(pad_st, 32 * n_empty + 16)

            def leave(eng, op, h, n, b):
                eng.wait_ge(x_tp, 2 * n + h + 1)
                for k in range(4 * h, 4 * h + 4):
                    e = op(xT[b][:, k, :], psT[h][:, k % 4, :], g["acol"][:, 1, k:k + 1], g["bcol"][:, 1, k:k + 1])
                e.then_inc(x_T[h], 1)

            @block.scalar
            def _(act):
                n_pairs = pairs(act)

                def op(o, a, s, t):
                    return nc.scalar.activation(o, a, ACT.Identity, bias=t, scale=s)

                leave(act, op, 0, 0, 0)
                with act.Fori(0, n_pairs) as i:
                    for b in range(2):
                        n = 2 * i + b
                        act.wait_ge(g_mm, n + 1)
                        act.wait_ge(ac_d, n)
                        nc.scalar.activation(si[:, :], psG[:, :], ACT.Silu).then_inc(si_d, 1)
                        act.wait_ge(u_mm, n)
                        leave(act, op, 0, n + 1, 1 - b)
                        act.wait_ge(y_mm, n + 1)
                        act.wait_ge(y_st[b], 16 * i)
                        nc.scalar.activation(yo[b][:, :], psY[:, :, :].rearrange("p a n -> p (a n)"), ACT.Copy).then_inc(y_d, 1)

            @block.vector
            def _(v):
                n_pairs = pairs(v)
                v.memset(zero[:, :], 0.0).then_inc(pad_st, 16)

                def op(o, a, s, t):
                    return v.tensor_scalar(o, a, s, t, ALU.mult, ALU.add)

                leave(v, op, 1, 0, 0)
                with v.Fori(0, n_pairs) as i:
                    for b in range(2):
                        n = 2 * i + b
                        v.wait_ge(si_d, n + 1)
                        v.wait_ge(u_mm, n + 1)
                        v.wait_ge(a_tp, n)
                        v.tensor_tensor(ac[:, :], si[:, :], psU[:, :], ALU.mult).then_inc(ac_d, 1)
                        leave(v, op, 1, n + 1, 1 - b)
                        v.wait_ge(a_tp, n + 1)
                        v.wait_ge(y_mm, n)
                        v.tensor_copy(aT[:, :, :], psA[:, :, :]).then_inc(a_T, 1)


def stage_output(nc, g, A, S, out):
    with Ctx(nc) as c:
        idx = [[c.sb(f"di{b}{k}", [P, 1], I32) for k in range(2)] for b in range(2)]
        yr = [[c.sb(f"yr{b}{k}", [P, D]) for k in range(2)] for b in range(2)]
        x1 = [c.sb(f"x1o{b}", [P, D]) for b in range(2)]
        y = [c.sb(f"ysum{b}", [P, D]) for b in range(2)]
        ob = [c.sb(f"ob{b}", [P, D]) for b in range(2)]
        junk = [c.sb(f"junk_o{b}", [P, D]) for b in range(2)]
        ssq, ms, rt, rstd = ([c.sb(f"{n}{b}", [P, 1]) for b in range(2)] for n in ("o_ss", "o_ms", "o_rt", "o_rstd"))
        ix = c.sem("di_done")
        tick, tick0 = c.sb("tick_o", [P, 1]), c.sem("tick_o0")
        y_in = [c.sem(f"yr_in{b}") for b in range(2)]
        x_in = [c.sem(f"x1o_in{b}") for b in range(2)]
        ys, y_d, sq, ms_d, rt_d, os_, o_d = (c.sem(n) for n in ("y_scaled", "y_sum", "o_sq", "o_ms_d", "o_rt_d", "o_step", "o_done"))
        o_st = [c.sem(f"out_st{b}") for b in range(2)]

        def tile(dram, t):
            return dram.rearrange("(t p) n -> t p n", p=P)[ds(t, 1)].rearrange("a p n -> (a p) n")

        with nc.Block() as block:
            @block.gpsimd
            def _(pool):
                nc.gpsimd.memset(tick[:, :], 0.0).then_inc(tick0, 1)
                pool.wait_ge(tick0, 1)
                with pool.Fori(0, NT // 2) as i:
                    for b in range(2):
                        t = 2 * i + b
                        for k in range(2):
                            if b == 0 and k == 0:
                                pool.wait_ge(y_d, 2 * i)
                            nc.gpsimd.tensor_copy(idx[b][k][:, :], g["dest"][:, k, ds(t, 1)]).then_inc(ix, 1)
                            pool.wait_ge(ix, 2 * t + k + 1)
                            nc.gpsimd.tensor_tensor(tick[:, :], tick[:, :], tick[:, :], ALU.add)
                            pool.indirect_dma_start(yr[b][k][:, :], None, S["yb"],
                                                    bass.IndirectOffsetOnAxis(idx[b][k][:, 0:1], 0)).then_inc(y_in[b], 16)

            @block.sync
            def _(sp):
                for b in range(2):
                    sp.dma_start(x1[b][:, :], tile(S["x1"], b)).then_inc(x_in[b], 16)

                def store(t, b):
                    sp.wait_ge(o_d, t + 1)
                    sp.dma_start(tile(out[0], t), ob[b][:, :]).then_inc(o_st[b], 16)
                with sp.Fori(0, NT // 2 - 1) as i:
                    for b in range(2):
                        store(2 * i + b, b)
                        sp.dma_start(x1[b][:, :], tile(S["x1"], 2 * i + b + 2)).then_inc(x_in[b], 16)
                for b in range(2):
                    store(NT - 2 + b, b)
                for b in range(2):
                    sp.wait_ge(o_st[b], 16 * NT // 2)

            @block.scalar
            def _(act):
                with act.Fori(0, NT // 2) as i:
                    for b in range(2):
                        t = 2 * i + b
                        act.wait_ge(y_d, t + 1)
                        nc.scalar.activation(junk[b][:, :], y[b][:, :], ACT.Square, accum_out=ssq[b][:, :]).then_inc(sq, 1)
                        act.wait_ge(ms_d, t + 1)
                        nc.scalar.activation(rt[b][:, :], ms[b][:, :], ACT.Sqrt).then_inc(rt_d, 1)

            @block.vector
            def _(v):
                def head(t, i, b):
                    v.wait_ge(y_in[b], 32 * i + 32)
                    v.tensor_scalar(y[b][:, :], yr[b][0][:, :], g["wgt"][:, 0, ds(t, 1)], None, ALU.mult).then_inc(ys, 1)
                    v.wait_ge(ys, t + 1)
                    v.scalar_tensor_tensor(out=y[b][:, :], in0=yr[b][1][:, :], scalar=g["wgt"][:, 1, ds(t, 1)], in1=y[b][:, :],
                                           op0=ALU.mult, op1=ALU.add).then_inc(y_d, 1)

                def tail(t, i, b):
                    v.wait_ge(sq, t + 1)
                    v.tensor_scalar(ms[b][:, :], ssq[b][:, :], 1.0 / D, EPS, ALU.mult, ALU.add).then_inc(ms_d, 1)
                    v.wait_ge(rt_d, t + 1)
                    v.reciprocal(rstd[b][:, :], rt[b][:, :]).then_inc(os_, 1)
                    v.wait_ge(os_, 2 * t + 1)
                    v.wait_ge(o_st[b], 16 * i)
                    v.scalar_tensor_tensor(out=ob[b][:, :], in0=y[b][:, :], scalar=rstd[b][:, 0:1], in1=g["grow"][:, 1, :],
                                           op0=ALU.mult, op1=ALU.mult).then_inc(os_, 1)
                    v.wait_ge(os_, 2 * t + 2)
                    v.wait_ge(x_in[b], 16 * i + 16)
                    v.tensor_tensor(ob[b][:, :], ob[b][:, :], x1[b][:, :], ALU.add).then_inc(o_d, 1)

                head(0, 0, 0)
                with v.Fori(0, NT // 2 - 1) as i:
                    head(2 * i + 1, i, 1)
                    tail(2 * i, i, 0)
                    head(2 * i + 2, i + 1, 0)
                    tail(2 * i + 1, i, 1)
                i = NT // 2 - 1
                head(NT - 1, i, 1)
                tail(NT - 2, i, 0)
                tail(NT - 1, i, 1)


def program(nc, A, out, scratch_kind="Internal"):
    def dram(name, shape, dt=F32):
        return nc.dram_tensor(name, shape, dt, kind=scratch_kind).ap()

    S = {
        "qkvu": dram("s_qkvu", (T, QKVU)),
        "gates": dram("s_gates", (T, 2 * D)),
        "rec": dram("s_rec", (NG_S, P, REC)),
        "kpad": dram("s_kpad", (NG_S, CH_S, 512)),
        "row_tok": dram("s_row_tok", (CAP + P, 1), I32),
        "rot": dram("s_rot", (2, P, NG_S, NC)),
        "rho": dram("s_rho", (P, NG_S)),
        "yb": dram("s_yb", (CAP, D)),
        "x1": dram("s_x1", (T, D)),
        "xn2": dram("s_xn2", (T, D)),
        "y": dram("s_y", (T, SW)),
        "bias_rows": dram("s_bias_rows", (NH, len(DILS), 3 * P - 1)),
        "bias_copies": dram("s_bias_copies", (P, NH * len(DILS) * (3 * P - 1))),
        "o": [dram(f"s_o{p}", (T, AW + 2 * NH)) for p in range(len(DILS))],
    }
    with Ctx(nc) as c:
        g = {
            "ident": c.sb("ident", [P, P]),
            "acol": c.sb("acol", [P, 2, KD]),
            "bcol": c.sb("bcol", [P, 2, KD]),
            "grow": c.sb("grow", [P, 2, D]),
            "rstd": c.sb("rstd", [P, NT]),
            "logits": c.sb("logits", [P, NT, NR]),
            "dest": c.sb("dest", [P, 2, NT], I32),
            "wgt": c.sb("wgt", [P, 2, NT]),
            "rowtok": c.sb("rowtok", [P, NBLK + 1], I32),
            "blk": c.sb("blk", [1, 4, NBLK + 1], I32),
        }
        stage_modulation(nc, g, A, S)
        stage_projection(nc, g, A, S)
        stage_ssm(nc, g, A, S)
        with Ctx(nc) as ca:
            ga = {**g, "bias": ca.sb("bias", [P, len(DILS), NH, 2 * P]), "bias_in": ca.sem("bias_in")}
            stage_bias(nc, ga, A, S)
            stage_attention(nc, ga, A, S)
        stage_merge(nc, g, A, S)
        stage_route(nc, g, A, S)
        stage_experts(nc, g, A, S)
        stage_output(nc, g, A, S, out)


_INS = ['x', 'c', 'w_mod', 'b_mod', 'g_pre_mix', 'g_post_mix', 'g_pre_ffn', 'g_post_ffn', 'w_in', 'rel_bias', 'a_re', 'a_im', 'log_dt', 'ssm_b_re', 'ssm_b_im', 'ssm_c_re', 'ssm_c_im', 'd_skip', 'w_glu', 'b_glu', 'w_branch_attn', 'w_branch_ssm', 'w_out', 'w_router_group', 'b_router_group', 'w_router_expert', 'b_router_expert', 'w1', 'w3', 'w2']


def kernel(**inputs):
    import numpy as _np
    import concourse.bacc as _bacc
    from concourse import mybir as _mybir
    from concourse.bass_utils import run_bass_kernel_spmd as _run

    nc = _bacc.Bacc("TRN2", target_bir_lowering=False, num_devices=1)
    given = {name: _np.ascontiguousarray(inputs[name]) for name in _INS}
    given["bucket_hot"] = bucket_one_hot()
    arrays, A = {}, {}
    for name, a in given.items():
        arrays[f"in_{name}_dram"] = a
        A[name] = nc.dram_tensor(f"in_{name}_dram", a.shape, _mybir.dt.from_np(a.dtype), kind="ExternalInput").ap()
    out = nc.dram_tensor("out_0_dram", (1, T, D), _mybir.dt.float32, kind="ExternalOutput").ap()
    program(nc, A, out)
    r = _run(nc, [arrays], core_ids=[0])
    return r.results[0]["out_0_dram"]
```

```python
from contextlib import ExitStack

import numpy as np

import concourse.bass as bass
from concourse import mybir

ALU = mybir.AluOpType
ACT = mybir.ActivationFunctionType
F32 = mybir.dt.float32
FR = mybir.dt.float32r
I32 = mybir.dt.int32
AX_X = mybir.AxisListType.X

P = 128
D = 1024
KD = D // P
T = 2048
NT = T // P
NH, HD = 8, 64
AW = NH * HD
DILS = (1, 4, 16)
NEG = -1e30
NUM_B, MAX_DIST = 32, 2048
EPS = 1e-6
NG_S, CH_S, ST_S = 32, 16, 64
SW = NG_S * CH_S
LC = 16
NC = T // LC
QKVU = 3 * AW + SW
IN_W = QKVU + 2 * D
NGR, EPG = 4, 8
NE = NGR * EPG
DE = D // 2
KE = DE // P
NBLK = 64
CAP = NBLK * P
SIDE, OTHER, JOB, N_SPLIT, W2_A, W2_B, NEXT_A, NEXT_B, R_EXPERT, R_START, META = range(11)
PIECES = 4


def ds(i, n):
    return bass.ds(i, n)


def bucket_one_hot():
    exact = NUM_B // 2
    hot = np.zeros((NUM_B + 1, len(DILS), 3 * P - 1), np.float32)
    hot[NUM_B] = 1.0
    for p, dil in enumerate(DILS):
        for d in range(P + 1):
            dist = d * dil
            large = exact + int(np.float32(np.log(np.float32(max(dist, exact)) / np.float32(exact)))
                                / np.float32(np.log(MAX_DIST / exact)) * np.float32(NUM_B - exact))
            b = dist if dist < exact else min(large, NUM_B - 1)
            at = P - 1 + P - d
            hot[NUM_B, p, at] = 0.0
            hot[b, p, at] = 1.0
    return hot


class Ctx:

    def __init__(self, nc):
        self.nc, self.stack, self.sems = nc, ExitStack(), []

    def __enter__(self):
        self.stack.__enter__()
        return self

    def __exit__(self, *a):
        if a[0] is None and self.sems:
            self.nc.all_engine_barrier()
            self.nc.clear_and_free_semaphores(self.sems)
            self.nc.all_engine_barrier()
        return self.stack.__exit__(*a)

    def sb(self, name, shape, dt=F32):
        return self.stack.enter_context(self.nc.sbuf_tensor(name, shape, dt))

    def ps(self, name, shape, dt=F32):
        return self.stack.enter_context(self.nc.psum_tensor(name, shape, dt))

    def sem(self, name):
        self.sems.append(self.nc.alloc_semaphore(name))
        return self.sems[-1]


REC = 2 * 192 + 4 * 256


def ssm_tables(nc, g, A, S, c):
    H = ST_S
    craw = [c.sb(f"craw{n}", [P, 4, 2, H]) for n in range(2)]
    araw = [c.sb(f"araw{n}", [NG_S, 2, H]) for n in range(2)]
    B = [c.sb(f"B{n}", [P, NG_S, CH_S]) for n in range(2)]
    C = [c.sb(f"C{n}", [P, NG_S, CH_S]) for n in range(2)]
    lam = [c.sb(f"lam{n}", [P, NG_S]) for n in range(2)]
    dt = c.sb("dt", [P, NG_S])
    dsk = c.sb("dskip", [CH_S, NG_S])
    sm = {n: c.sb(f"sm_{n}", [P, NG_S]) for n in
          ("zr", "zi", "n", "r", "ab", "cs", "sn", "ea", "nr", "ni", "den", "inv", "t0", "t1", "fr", "fi", "z16")}
    pw = [c.sb(f"pw{n}", [P, LC + 1, NG_S]) for n in range(2)]
    pt = [c.sb(f"pt{n}", [P, NC // 2 * NG_S]) for n in range(2)]
    un = [c.sb(f"un{n}", [P, NG_S]) for n in range(2)]
    q1, q2, s2 = (c.sb(n, [P, LC + 1, NG_S]) for n in ("q1", "q2", "s2"))
    s1 = c.sb("s1", [P, LC + 1, NG_S])
    Bb = [c.sb(f"Bb{n}", [P, NG_S, CH_S]) for n in range(2)]
    tmp = [c.sb(f"tmp{n}", [P, NG_S, CH_S]) for n in range(2)]
    G = c.sb("G", [P, NG_S, LC + 1, CH_S])
    E = c.sb("E", [P, NG_S, LC, CH_S])
    dm = c.sb("dm", [CH_S, NG_S, CH_S])
    K = [pt[0][0:CH_S, 1024 * b:1024 * b + 1024].rearrange("c (g n) -> c g n", g=4) for b in range(2)]
    zer = c.sb("zer", [CH_S, 256])
    Est = [c.sb(f"Est{b}", [P, 2, 3, H]) for b in range(4)]
    tmp_e = [c.sb(f"tmp_e{n}", [P, NG_S, CH_S]) for n in range(2)]
    psC = c.ps("psC", [P, 4, P])
    psK = [c.ps(f"psK{b}", [P, 2, 256]) for b in range(2)]
    psE = [c.ps(f"psE{b}", [P, 2, 2, H]) for b in range(2)]
    in_ = c.sem("ssm_in")
    tr, tr_out, dt_done = c.sem("ssm_tr"), c.sem("ssm_tr_out"), c.sem("dt_done")
    act_r, trig, step_n = c.sem("angle_ready"), c.sem("trig_done"), c.sem("ssm_step")
    k_ps, k_out, k_st = c.sem("k_psum"), c.sem("k_out"), [c.sem(f"k_st{b}") for b in range(2)]
    e_ps, e_out, e_st = c.sem("e_psum"), c.sem("e_out"), [c.sem(f"e_st{b}") for b in range(4)]
    s_done, e_step, z_st = c.sem("s12_done"), c.sem("E_step"), c.sem("zer_st")
    g_done, e_done, zer_done, t_st = c.sem("G_done"), c.sem("E_done"), c.sem("zer_done"), c.sem("T_st")
    rot, rho = [c.sb(f"rot{n}", [P, NG_S, NC]) for n in range(2)], c.sb("rho", [P, NG_S])
    rot_done = c.sem("rot_done")
    rec = S["rec"]

    def loads(sp):
        for n, name in enumerate(("ssm_c_re", "ssm_c_im")):
            for d in range(2):
                sp.dma_start(craw[n][:, :, d, :], A[name][0].rearrange("(k g) c p -> (g c) k p", g=8)).then_inc(in_, 16)
        for n, name in enumerate(("a_re", "a_im")):
            for d in range(2):
                sp.dma_start(araw[n][:, d, :], A[name][0]).then_inc(in_, 16)
        for n, name in enumerate(("ssm_b_re", "ssm_b_im")):
            for d in range(2):
                sp.dma_start(B[n][H * d:H * d + H, :, :], A[name][0].rearrange("g p c -> p g c")).then_inc(in_, 16)
        sp.dma_start(dt[:, :], A["log_dt"].to_broadcast([P, NG_S])).then_inc(in_, 16)
        sp.dma_start(dsk[:, :], A["d_skip"].rearrange("a (g c) -> c (a g)", c=CH_S),
                     allow_slow_non_contiguous=True).then_inc(in_, 16)

    def store_zeros(sp):
        sp.wait_ge(zer_done, 1)
        for gi in range(NG_S):
            sp.dma_start(S["kpad"][gi, :, 0:256], zer[:, :]).then_inc(z_st, 16)

    def store_G(sp):
        sp.wait_ge(g_done, 1)
        gr = rec.rearrange("g p n -> p g n")
        sp.dma_start(gr[:, :, 384:640], G[:, :, 1:, :].rearrange("p g s c -> p g (s c)")).then_inc(t_st, 16)
        for d in range(2):
            sp.dma_start(gr[H * d:H * d + H, :, 640:896],
                         G[H * (1 - d):H * (1 - d) + H, :, 1:, :].rearrange("p g s c -> p g (s c)")).then_inc(t_st, 16)

    def store_rot(sp):
        sp.wait_ge(rot_done, 1)
        for n in range(2):
            sp.dma_start(S["rot"][n], rot[n][:, :, :]).then_inc(t_st, 16)
        sp.dma_start(S["rho"], rho[:, :]).then_inc(t_st, 16)

    def store_T(sp):
        kp = S["kpad"]
        for q in range(NG_S // 4):
            sp.wait_ge(k_out, 3 * q + 3)
            sp.dma_start(kp[4 * q:4 * q + 4, :, 256:512].rearrange("g c n -> c g n"), K[q % 2]).then_inc(k_st[q % 2], 16)
        for b in range(2):
            sp.wait_ge(k_st[b], 16 * NG_S // 8)
        sp.wait_ge(z_st, 16 * NG_S)
        for s in range(LC):
            k, r = s // 8, s % 8
            sp.dma_start(rec[:, CH_S * r:CH_S * r + CH_S, 896 + 256 * k:1152 + 256 * k],
                         kp[:, :, 256 - CH_S * s:512 - CH_S * s]).then_inc(t_st, 16)
        sp.wait_ge(t_st, 16 * (6 + LC))

    def turn_inputs(pe):
        pe.wait_ge(in_, 16 * 14)
        for n in range(2):
            mm = nc.tensor.transpose(psK[0][:, n, 0:NG_S], araw[n][:, :, :].rearrange("g d p -> g (d p)"),
                                     g["ident"][0:NG_S, 0:NG_S])
        mm.then_inc(tr, 1)
        for n in range(2):
            if n:
                pe.wait_ge(tr_out, 2)
            for k in range(4):
                mm = nc.tensor.transpose(psC[:, k, :], craw[n][:, k, :, :].rearrange("q d p -> q (d p)"), g["ident"][:, :])
            mm.then_inc(tr, 1)

    def impulse(pe):
        pe.wait_ge(g_done, 1)
        pe.wait_ge(e_done, 1)
        for gi in range(NG_S):
            q = gi // 2
            if gi % 2 == 0 and q >= 2:
                pe.wait_ge(k_out, 3 * (q // 2) - 1 if q % 2 == 1 else 3 * (q // 2) - 2)
            mm = nc.tensor.matmul(psK[q % 2][0:CH_S, gi % 2, :], E[:, gi, LC - 1, :],
                                  G[:, gi, 0:LC, :].rearrange("p s c -> p (s c)"), start=True, stop=True)
            if gi % 2:
                mm.then_inc(k_ps, 1)

    def turn_E(pe, groups):
        pe.wait_ge(e_done, LC)
        for gi in groups:
            b = gi % 2
            if gi >= 2:
                pe.wait_ge(e_out, 2 * gi - 2)
            for k in range(2):
                mm = nc.tensor.transpose(psE[b][:, k, :, :].rearrange("p r h -> p (r h)"),
                                         E[:, gi, 8 * k:8 * k + 8, :].rearrange("p s c -> p (s c)"), g["ident"][:, :])
            mm.then_inc(e_ps, 1)

    def trigonometry(act):
        act.wait_ge(in_, 16 * 14)
        nc.scalar.activation(dt[:, :], dt[:, :], ACT.Exp).then_inc(dt_done, 1)
        act.wait_ge(act_r, 1)
        nc.scalar.activation(sm["ea"][:, :], sm["zr"][:, :], ACT.Exp).then_inc(trig, 1)
        nc.scalar.activation(rho[:, :], sm["z16"][:, :], ACT.Exp).then_inc(trig, 1)
        nc.scalar.activation(sm["sn"][:, :], sm["r"][:, :], ACT.Sin).then_inc(trig, 1)
        nc.scalar.activation(sm["cs"][:, :], sm["ab"][:, :], ACT.Sin).then_inc(trig, 1)

    def evacuate_E(act, groups):
        for gi in groups:
            b = gi % 4
            act.wait_ge(e_ps, gi + 1)
            if gi >= 4:
                act.wait_ge(e_st[b], 16 * (gi // 4))
            nc.scalar.activation(Est[b][:, :, 0:2, :], psE[gi % 2][:, :, :, :], ACT.Copy).then_inc(e_out, 1)
            nc.scalar.activation(Est[b][:, :, 2, :], psE[gi % 2][:, :, 0, :], ACT.Copy).then_inc(e_out, 1)
            act.wait_ge(e_out, 2 * gi + 2)
            act.dma_start(rec[gi, :, 0:384], Est[b][:, :, :, :].rearrange("p k r h -> p (k r h)")).then_inc(e_st[b], 16)

    def stored_E(act):
        for b in range(4):
            act.wait_ge(e_st[b], 16 * NG_S // 4)

    def build_E(pool):
        pool.wait_ge(s_done, 1)
        for n, s in enumerate(reversed(range(LC))):
            pq = [x[:, LC - 1 - s, :].unsqueeze(2).to_broadcast([P, NG_S, CH_S]) for x in (s1, s2)]
            for m in range(2):
                nc.gpsimd.tensor_tensor(tmp_e[m][:, :, :], Bb[m][:, :, :], pq[m], ALU.mult).then_inc(e_step, 1)
            pool.wait_ge(e_step, 2 * n + 2)
            nc.gpsimd.tensor_tensor(E[:, :, s, :], tmp_e[0][:, :, :], tmp_e[1][:, :, :], ALU.add).then_inc(e_done, 1)
            pool.wait_ge(e_done, n + 1)

    def tables(v):
        n_steps = [0]

        def did(ins):
            n_steps[0] += 1
            ins.then_inc(step_n, 1)
            v.wait_ge(step_n, n_steps[0])

        def tt(o, a, b, op):
            did(v.tensor_tensor(o, a, b, op))

        def cmul(o, a, b, shape):
            x, y = (pt[n][:, 0:shape[0] * shape[1]].rearrange("p (m g) -> p m g", g=shape[1]) for n in range(2))
            tt(x, a[0], b[0], ALU.mult)
            tt(y, a[1], b[1], ALU.mult)
            tt(o[0], x, y, ALU.subtract)
            tt(x, a[0], b[1], ALU.mult)
            tt(y, a[1], b[0], ALU.mult)
            tt(o[1], x, y, ALU.add)

        v.memset(zer[:, :], 0.0).then_inc(zer_done, 1)
        v.wait_ge(tr, 1)
        did(v.tensor_copy(lam[0][:, :], psK[0][:, 0, 0:NG_S]))
        did(v.tensor_copy(lam[1][:, :], psK[0][:, 1, 0:NG_S]))
        for n in range(2):
            v.wait_ge(tr, n + 2)
            v.tensor_copy(C[n][:, :, :].rearrange("p g c -> p (g c)"), psC[:, :, :].rearrange("p k n -> p (k n)")).then_inc(tr_out, 2)
        v.wait_ge(tr_out, 4)
        v.wait_ge(dt_done, 1)
        t = {k: x[:, :] for k, x in sm.items()}
        tt(t["zr"], lam[0][:, :], dt[:, :], ALU.mult)
        tt(t["zi"], lam[1][:, :], dt[:, :], ALU.mult)
        did(v.tensor_scalar(t["z16"], t["zr"], float(LC), None, ALU.mult))
        big = 1.5 * 2 ** 23
        did(v.tensor_scalar(t["n"], t["zi"], 1 / (2 * np.pi), big, ALU.mult, ALU.add))
        did(v.tensor_scalar(t["n"], t["n"], big, None, ALU.subtract))
        c1 = 6.28125
        c2 = float(np.float32(np.round((2 * np.pi - c1) * 2 ** 20) / 2 ** 20))
        c3 = 2 * np.pi - c1 - c2
        did(v.scalar_tensor_tensor(out=t["r"], in0=t["n"], scalar=-c1, in1=t["zi"], op0=ALU.mult, op1=ALU.add))
        did(v.scalar_tensor_tensor(out=t["t0"], in0=t["n"], scalar=-c2, in1=t["r"], op0=ALU.mult, op1=ALU.add))
        did(v.scalar_tensor_tensor(out=t["r"], in0=t["n"], scalar=-c3, in1=t["t0"], op0=ALU.mult, op1=ALU.add))
        pi = float(np.float32(np.pi)) * (1 - 2 ** -23)
        did(v.tensor_scalar(t["r"], t["r"], pi, -pi, ALU.min, ALU.max))
        did(v.scalar_tensor_tensor(out=t["t0"], in0=t["r"], scalar=-1.0, in1=t["r"], op0=ALU.mult, op1=ALU.max))
        v.tensor_scalar(t["ab"], t["t0"], -1.0, np.pi / 2, ALU.mult, ALU.add).then_inc(act_r, 1)
        v.wait_ge(trig, 4)
        tt(pw[0][:, 1, :], t["ea"], t["cs"], ALU.mult)
        tt(pw[1][:, 1, :], t["ea"], t["sn"], ALU.mult)
        did(v.memset(pw[0][:, 0, :], 1.0))
        did(v.memset(pw[1][:, 0, :], 0.0))
        did(v.tensor_scalar(t["nr"], pw[0][:, 1, :], -1.0, None, ALU.add))
        ni = pw[1][:, 1, :]
        tt(t["t0"], lam[0][:, :], lam[0][:, :], ALU.mult)
        tt(t["t1"], lam[1][:, :], lam[1][:, :], ALU.mult)
        tt(t["den"], t["t0"], t["t1"], ALU.add)
        did(v.reciprocal(t["inv"], t["den"]))
        tt(t["t0"], t["nr"], lam[0][:, :], ALU.mult)
        tt(t["t1"], ni, lam[1][:, :], ALU.mult)
        tt(t["fr"], t["t0"], t["t1"], ALU.add)
        tt(t["fr"], t["fr"], t["inv"], ALU.mult)
        tt(t["t0"], ni, lam[0][:, :], ALU.mult)
        tt(t["t1"], t["nr"], lam[1][:, :], ALU.mult)
        tt(t["fi"], t["t0"], t["t1"], ALU.subtract)
        tt(t["fi"], t["fi"], t["inv"], ALU.mult)
        fr, fi = (sm[n][:, :].unsqueeze(2).to_broadcast([P, NG_S, CH_S]) for n in ("fr", "fi"))
        for o, (x, y, op) in enumerate(((0, 1, ALU.subtract), (1, 0, ALU.add))):
            tt(tmp[0][:, :, :], B[x][:, :, :], fr, ALU.mult)
            tt(tmp[1][:, :, :], B[y][:, :, :], fi, ALU.mult)
            tt(Bb[o][:, :, :], tmp[0][:, :, :], tmp[1][:, :, :], op)
        m = 1
        while m < LC:
            a_m = [x[:, m:m + 1, :].to_broadcast([P, m, NG_S]) for x in pw]
            cmul([x[:, m + 1:2 * m + 1, :] for x in pw], [x[:, 1:m + 1, :] for x in pw], a_m, (m, NG_S))
            m *= 2
        top, bot = slice(0, H), slice(H, P)
        for dst, half, src, sign in ((q1, top, 0, 1.0), (q1, bot, 1, -1.0), (q2, top, 1, -1.0), (q2, bot, 0, -1.0),
                                     (s1, top, 0, 1.0), (s1, bot, 1, 1.0), (s2, top, 1, -1.0), (s2, bot, 0, 1.0)):
            did(v.tensor_scalar(dst[half, :, :], pw[src][half, :, :], sign, None, ALU.mult))
        v.engine_nop().then_inc(s_done, 1)
        for s in range(LC + 1):
            pq = [x[:, s, :].unsqueeze(2).to_broadcast([P, NG_S, CH_S]) for x in (q1, q2)]
            tt(tmp[0][:, :, :], C[0][:, :, :], pq[0], ALU.mult)
            tt(tmp[1][:, :, :], C[1][:, :, :], pq[1], ALU.mult)
            tt(G[:, :, s, :], tmp[0][:, :, :], tmp[1][:, :, :], ALU.add)
        v.engine_nop().then_inc(g_done, 1)
        x, y = (sm[n][:, :] for n in ("cs", "sn"))
        did(v.tensor_copy(un[0][:, :], x))
        did(v.tensor_copy(un[1][:, :], y))
        for _ in range(4):
            tt(t["t0"], un[0][:, :], un[0][:, :], ALU.mult)
            tt(t["t1"], un[1][:, :], un[1][:, :], ALU.mult)
            tt(t["nr"], un[0][:, :], un[1][:, :], ALU.mult)
            tt(un[0][:, :], t["t0"], t["t1"], ALU.subtract)
            did(v.tensor_scalar(un[1][:, :], t["nr"], 2.0, None, ALU.mult))
        for n in range(2):
            did(v.memset(rot[n][:, :, 0:1], 1.0 - n))
            did(v.tensor_copy(rot[n][:, :, 1:2], un[n][:, :].unsqueeze(2)))
        m = 1
        while m < NC:
            k = min(m, NC - 1 - m)
            if k <= 0:
                break
            a = [x[:, :, 1:k + 1] for x in rot]
            b = [x[:, :, m:m + 1].to_broadcast([P, NG_S, k]) for x in rot]
            o = [x[:, :, m + 1:m + k + 1] for x in rot]
            x, y = (pt[n][:, 0:NG_S * k].rearrange("p (g m) -> p g m", m=k) for n in range(2))
            tt(x, a[0], b[0], ALU.mult)
            tt(y, a[1], b[1], ALU.mult)
            tt(o[0], x, y, ALU.subtract)
            tt(x, a[0], b[1], ALU.mult)
            tt(y, a[1], b[0], ALU.mult)
            tt(o[1], x, y, ALU.add)
            m *= 2
        did(v.tensor_scalar(rot[1][bot, :, :], rot[1][bot, :, :], -1.0, None, ALU.mult))
        v.engine_nop().then_inc(rot_done, 1)
        tt(dm[:, :, :], g["ident"][0:CH_S, 0:CH_S].unsqueeze(1).to_broadcast([CH_S, NG_S, CH_S]),
           dsk[:, :].unsqueeze(2).to_broadcast([CH_S, NG_S, CH_S]), ALU.mult)
        for q in range(NG_S // 4):
            if q >= 2:
                v.wait_ge(k_st[q % 2], 16 * (q // 2))
            for b in range(2):
                v.wait_ge(k_ps, 2 * q + b + 1)
                v.tensor_copy(K[q % 2][:, 2 * b:2 * b + 2, :], psK[b][0:CH_S, :, :]).then_inc(k_out, 1)
            v.wait_ge(k_out, 3 * q + 2)
            v.tensor_tensor(K[q % 2][:, :, 0:CH_S], K[q % 2][:, :, 0:CH_S], dm[:, 4 * q:4 * q + 4, :], ALU.add).then_inc(k_out, 1)

    return {"bank": psK[1][:, :, :].rearrange("p a n -> p (a n)"), "loads": loads, "store_T": store_T, "turn_inputs": turn_inputs, "impulse": impulse, "build_E": build_E, "turn_E": turn_E, "stored_E": stored_E, "store_zeros": store_zeros, "store_G": store_G, "store_rot": store_rot,
            "trigonometry": trigonometry, "evacuate_E": evacuate_E, "tables": tables}


def bias_rows(nc, A, S, c, ps):
    W = 3 * P - 1
    hot = c.sb("bucket_hot", [NUM_B + 1, len(DILS), W])
    rb = c.sb("rel_bias_sb", [NUM_B + 1, NH])
    row = c.sb("bias_row", [NH, len(DILS), W])
    hot_in, neg_done, mm_done = c.sem("hot_in"), c.sem("neg_done"), c.sem("bias_mm")
    row_done, row_st = c.sem("row_done"), c.sem("row_st")

    def loads(sp):
        sp.dma_start(hot[:, :, :], A["bucket_hot"]).then_inc(hot_in, 16)
        sp.dma_start(rb[0:NUM_B, :], A["rel_bias"]).then_inc(hot_in, 16)

    def store_rows(sp):
        sp.wait_ge(row_done, len(DILS))
        sp.dma_start(S["bias_rows"], row[:, :, :]).then_inc(row_st, 16)

    def copy_rows(sp):
        sp.wait_ge(row_st, 16)
        one = S["bias_rows"]
        sp.dma_start(S["bias_copies"], bass.AP(tensor=one.tensor, offset=one.offset,
                                               ap=[[0, P], [1, NH * len(DILS) * W]])).then_inc(row_st, 16)

    def wait(sp):
        sp.wait_ge(row_st, 32)

    def products(pe):
        pe.wait_ge(hot_in, 32)
        pe.wait_ge(neg_done, 1)
        for p in range(len(DILS)):
            if p:
                pe.wait_ge(row_done, p)
            nc.tensor.matmul(ps[0:NH, 0:W], rb[:, :], hot[:, p, :], start=True, stop=True).then_inc(mm_done, 1)

    def no_band(v):
        v.memset(rb[NUM_B:NUM_B + 1, :], NEG).then_inc(neg_done, 1)

    def evacuate(v):
        for p in range(len(DILS)):
            v.wait_ge(mm_done, p + 1)
            v.tensor_copy(row[:, p, :], ps[0:NH, 0:W]).then_inc(row_done, 1)

    return {"loads": loads, "store_rows": store_rows, "copy_rows": copy_rows, "wait": wait, "products": products, "no_band": no_band, "evacuate": evacuate}


def load_bias(sp, g, S):
    W = 3 * P - 1
    pitch = NH * len(DILS) * W
    src = S["bias_copies"]
    for p in range(len(DILS)):
        view = bass.AP(tensor=src.tensor, offset=src.offset + p * W + P - 1,
                       ap=[[pitch - 1, P], [len(DILS) * W, NH], [1, 2 * P]])
        sp.dma_start(g["bias"][:, p, :, :], view).then_inc(g["bias_in"], 16)


def stage_modulation(nc, g, A, S):
    with Ctx(nc) as c:
        tab = ssm_tables(nc, g, A, S, c)
        bias = bias_rows(nc, A, S, c, tab["bank"])
        MW, NWB = D, 3
        NL = 6 * D // MW
        E0 = NL * KD // 2 + NL
        mrow = c.sb("mod_row", [1, MW])
        row_mm, row_d, col_mm = c.sem("mod_row_mm"), c.sem("mod_row_done"), c.sem("mod_col_mm")
        wm = [c.sb(f"wmod{b}", [P, MW]) for b in range(NWB)]
        ccol = c.sb("ccol", [P, KD])
        sig = c.sb("csig", [P, KD])
        scol = c.sb("scol", [P, KD])
        bmod = c.sb("bmod", [P, 6 * KD])
        mod = c.sb("mod", [P, 6 * KD])
        gains = c.sb("gains", [P, 4, KD])
        gcol = c.sb("gcol", [P, 2, KD])
        xs = c.sb("xs", [P, D])
        ss = c.sb("ss", [P, NT])
        ms = c.sb("ms", [P, NT])
        psm = c.ps("psm", [P, 512])
        psw = c.ps("ps_mod_row", [P, 2, 512])
        small_in = c.sem("mod_small_in")
        w_in = [c.sem(f"wmod_in{b}") for b in range(NWB)]
        w_used = c.sem("wmod_used")
        sig_done = c.sem("csig_done")
        silu_done = c.sem("csilu_done")
        mod_done = c.sem("mod_done")
        vstep = c.sem("mod_vstep")
        ident0 = c.sem("ident0")
        ident1 = c.sem("ident_done")
        rows_done = c.sem("rows_done")
        rows_out = c.sem("rows_out")
        x_in = c.sem("xs_in")
        sq = c.sem("x_sq")
        ms_done = c.sem("ms_done")
        rms_done = c.sem("rms_done")
        rstd_done = c.sem("rstd_done")
        xv = A["x"][0].rearrange("(t p) n -> t p n", p=P)
        wv = A["w_mod"][0].rearrange("(k p) n -> k p n", p=P)

        with nc.Block() as block:
            @block.sync
            def _(sp):
                sp.dma_start(ccol[:, :], A["c"].rearrange("a (k p) -> p (a k)", p=P),
                             allow_slow_non_contiguous=True).then_inc(small_in, 16)
                sp.dma_start(bmod[:, :], A["b_mod"].rearrange("a (k p) -> p (a k)", p=P),
                             allow_slow_non_contiguous=True).then_inc(small_in, 16)
                for n, name in enumerate(("g_pre_mix", "g_post_mix", "g_pre_ffn", "g_post_ffn")):
                    sp.dma_start(gains[:, n, :], A[name].rearrange("a (k p) -> p (a k)", p=P),
                                 allow_slow_non_contiguous=True).then_inc(small_in, 16)
                bias["loads"](sp)
                tab["loads"](sp)
                def load_w(j):
                    if j >= NWB:
                        sp.wait_ge(w_used, j - NWB + 1)
                    b = j % NWB
                    sp.dma_start(wm[b][:, :], wv[j % KD, :, j // KD * MW:(j // KD + 1) * MW]).then_inc(w_in[b], 16)

                per = NL * KD // NT
                for t in range(NT):
                    if t:
                        sp.wait_ge(sq, t)
                    sp.dma_start(xs[:, :], xv[t]).then_inc(x_in, 16)
                    for j in range(per * t, per * t + per):
                        load_w(j)
                    if t == 1:
                        tab["store_zeros"](sp)
                    if t == 2:
                        bias["store_rows"](sp)
                    if t == 4:
                        bias["copy_rows"](sp)
                    if t == 10:
                        tab["store_G"](sp)
                    if t == 14:
                        tab["store_rot"](sp)
                tab["store_T"](sp)
                bias["wait"](sp)

            @block.gpsimd
            def _(pool):
                nc.gpsimd.memset(g["ident"][:, :], 0.0).then_inc(ident0, 1)
                pool.wait_ge(ident0, 1)
                nc.gpsimd.affine_select(out=g["ident"][:, :], in_=g["ident"][:, :], compare_op=ALU.not_equal,
                                        fill=1.0, base=0, pattern=[[-1, P]], channel_multiplier=1).then_inc(ident1, 1)
                tab["build_E"](pool)

            @block.scalar
            def _(act):
                act.wait_ge(small_in, 96)
                nc.scalar.activation(sig[:, :], ccol[:, :], ACT.Sigmoid).then_inc(sig_done, 1)
                tab["trigonometry"](act)
                per = NL * KD // NT
                for t in range(NT):
                    if t * per > E0:
                        tab["evacuate_E"](act, range((t - 1) * per - E0, t * per - E0))
                    act.wait_ge(x_in, 16 * t + 16)
                    nc.scalar.activation(xs[:, :], xs[:, :], ACT.Square, accum_out=ss[:, t:t + 1]).then_inc(sq, 1)
                    if t * NL // NT != (t + 1) * NL // NT:
                        n = t * NL // NT
                        act.wait_ge(w_used, KD * n + KD)
                        if n:
                            act.wait_ge(col_mm, n)
                        nc.scalar.activation(mrow[0:1, :], psw[0:1, :, :].rearrange("p a n -> p (a n)"), ACT.Copy).then_inc(row_d, 1)
                tab["evacuate_E"](act, range(t * per - E0, NG_S))
                tab["stored_E"](act)
                act.wait_ge(ms_done, 1)
                nc.scalar.activation(ms[:, :], ms[:, :], ACT.Sqrt).then_inc(rms_done, 1)

            @block.tensor
            def _(pe):
                pe.wait_ge(ident1, 1)
                bias["products"](pe)
                tab["turn_inputs"](pe)
                pe.wait_ge(silu_done, 1)
                for n in range(NL):
                    if n:
                        pe.wait_ge(row_d, n)
                    for k in range(KD):
                        j = KD * n + k
                        pe.wait_ge(w_in[j % NWB], 16 * (j // NWB) + 16)
                        for h in range(2):
                            mm = nc.tensor.matmul(psw[0:1, h, :], scol[:, k:k + 1], wm[j % NWB][:, 512 * h:512 * h + 512],
                                                  start=k == 0, stop=k == KD - 1)
                        mm.then_inc(w_used, 1)
                        if j >= E0:
                            tab["turn_E"](pe, range(j - E0, j - E0 + 1))
                    pe.wait_ge(row_d, n + 1)
                    for k in range(KD):
                        mm = nc.tensor.matmul(psm[:, KD * n + k:KD * n + k + 1], mrow[0:1, k * P:(k + 1) * P], g["ident"][0:1, 0:1],
                                              start=n == 0 and k == 0, stop=True, skip_group_check=True)
                    mm.then_inc(col_mm, 1)
                tab["turn_E"](pe, range(NL * KD - E0, NG_S))
                tab["impulse"](pe)
                pe.wait_ge(vstep, 6)
                for j in range(4):
                    if j:
                        pe.wait_ge(rows_out, j)
                    for k in range(4):
                        col = (j % 2) * 4 + k
                        mm = nc.tensor.matmul(psw[:, 0, k * P:(k + 1) * P], gcol[:, j // 2, col:col + 1].to_broadcast([P, P]),
                                              g["ident"][:, :], start=True, stop=True)
                    mm.then_inc(rows_done, 1)

            @block.vector
            def _(v):
                bias["no_band"](v)
                v.wait_ge(sig_done, 1)
                v.tensor_tensor(scol[:, :], ccol[:, :], sig[:, :], ALU.mult).then_inc(silu_done, 1)
                bias["evacuate"](v)
                tab["tables"](v)
                v.wait_ge(sq, NT)
                v.tensor_scalar(ms[:, :], ss[:, :], 1.0 / D, EPS, ALU.mult, ALU.add).then_inc(ms_done, 1)
                v.wait_ge(rms_done, 1)
                v.reciprocal(g["rstd"][:, :], ms[:, :]).then_inc(rstd_done, 1)
                v.wait_ge(col_mm, NL)
                v.tensor_tensor(mod[:, :], psm[:, 0:6 * KD], bmod[:, :], ALU.add).then_inc(mod_done, 1)
                v.wait_ge(mod_done, 1)
                for r in range(2):
                    sh, sc, gt = (mod[:, (3 * r + j) * KD:(3 * r + j + 1) * KD] for j in range(3))
                    v.scalar_tensor_tensor(out=g["acol"][:, r, :], in0=sc, scalar=1.0, in1=gains[:, 2 * r, :],
                                           op0=ALU.add, op1=ALU.mult).then_inc(vstep, 1)
                    v.tensor_copy(g["bcol"][:, r, :], sh).then_inc(vstep, 1)
                    v.tensor_tensor(gcol[:, r, :], gt, gains[:, 2 * r + 1, :], ALU.mult).then_inc(vstep, 1)
                for j in range(4):
                    v.wait_ge(rows_done, j + 1)
                    v.tensor_copy(g["grow"][:, j // 2, (j % 2) * 512:(j % 2 + 1) * 512], psw[:, 0, :]).then_inc(rows_out, 1)
                v.wait_ge(rows_out, 4)
                v.wait_ge(rstd_done, 1)


def stage_projection(nc, g, A, S):
    HW = 1024
    with Ctx(nc) as c:
        wh, wl = (c.sb(f"w_in_{n}", [P, KD, QKVU], FR) for n in ("hi", "lo"))
        wr = [c.sb(f"w_raw{b}", [P, HW]) for b in range(2)]
        x = [c.sb(f"xt{b}", [P, D]) for b in range(2)]
        h = c.sb("h_exact", [P, KD, P])
        hh, hl = ([c.sb(f"h_{n}{b}", [P, KD, P], FR) for b in range(2)] for n in ("hi", "lo"))
        st = [c.sb(f"proj_st{b}", [P, QKVU]) for b in range(2)]
        pst = [c.ps(f"pst{b}", [P, 4, P]) for b in range(2)]
        pso = [c.ps(f"pso{b}", [P, 512]) for b in range(4)]
        w_ld = [c.sem(f"w_raw_in{b}") for b in range(2)]
        w_hi, w_lo, w_used = c.sem("w_hi_done"), c.sem("w_lo_done"), c.sem("w_chunk_used")
        x_in = [c.sem(f"x_in{b}") for b in range(2)]
        xnd, tp, ht = c.sem("xn_done"), c.sem("hT_psum"), c.sem("hT_done")
        hi_d, lo_d = c.sem("h_hi_done"), c.sem("h_lo_done")
        po, ev = c.sem("proj_psum"), c.sem("proj_evac")
        stored = [c.sem(f"proj_stored{b}") for b in range(2)]
        xv = A["x"][0].rearrange("(t p) n -> t p n", p=P)
        wv = A["w_in"][0].rearrange("(k p) n -> k p n", p=P)
        dst = [S[n].rearrange("(t p) n -> t p n", p=P) for n in ("qkvu", "gates")]

        def steps(eng, body):
            for r in range(2):
                lo, hi = NT * r // 2, NT * (r + 1) // 2
                for b in range(2):
                    body(2 * lo + b, r, b)
                with eng.Fori(lo + 1, hi - 1) as i:
                    for b in range(2):
                        body(2 * i + b, r, b)
                for b in range(2):
                    body(2 * hi - 2 + b, r, b)

        def known(u):
            return isinstance(u, int)

        with nc.Block() as block:
            @block.sync
            def _(sp):
                def load_x(u, r, b):
                    t = u - NT * r
                    sp.dma_start(x[b][:, :], xv[ds(t, 1)].rearrange("a p n -> (a p) n")).then_inc(x_in[b], 16)

                def weights(r):
                    for j in range(2 * KD):
                        n = 2 * KD * r + j
                        if n >= 2:
                            sp.wait_ge(w_lo, n - 1)
                        sp.dma_start(wr[j % 2][:, :], wv[j // 2, :, QKVU * r + HW * (j % 2):QKVU * r + HW * (j % 2) + HW]
                                     ).then_inc(w_ld[j % 2], 16)

                def body(u, r, b):
                    if not (known(u) and u == 2 * NT - 1) and not (known(u) and u == 2 * NT - 2):
                        sp.wait_ge(tp, 2 * u + 2)
                        last = known(u) and u >= NT * r + NT - 2
                        load_x(u + 2, r + 1 if last else r, b)
                    if known(u) and u == NT - 1:
                        weights(1)
                    sp.wait_ge(ev, 4 * u + 4)
                    sp.dma_start(dst[r][ds(u - NT * r, 1)].rearrange("a p n -> (a p) n"), st[b][:, :]).then_inc(stored[b], 16)

                load_x(0, 0, 0)
                load_x(1, 0, 1)
                weights(0)
                steps(sp, body)
                for b in range(2):
                    sp.wait_ge(stored[b], 16 * NT)

            def evacuate(eng, op, u, b):
                for n in range(4):
                    eng.wait_ge(po, 4 * u + n + 1)
                    if n == 0 and not (known(u) and u < 2):
                        eng.wait_ge(stored[b], 8 * (u - b))
                    op(n, st[b][:, n * 512:(n + 1) * 512], pso[n][:, :]).then_inc(ev, 1)

            @block.scalar
            def _(act):
                def split_h(u, b):
                    act.wait_ge(ht, 8 * u + 8)
                    if not (known(u) and u < 2):
                        act.wait_ge(po, 4 * u - 4)
                    nc.scalar.activation(hh[b][:, :, :], h[:, :, :], ACT.Copy).then_inc(hi_d, 1)

                def split_w(r):
                    for j in range(2 * KD):
                        if r:
                            if j // 2 < KD - 1:
                                act.wait_ge(w_used, j // 2 + 1)
                            else:
                                act.wait_ge(po, 4 * NT)
                        act.wait_ge(w_ld[j % 2], 16 * (KD * r + j // 2 + 1))
                        nc.scalar.activation(wh[:, j // 2, HW * (j % 2):HW * (j % 2) + HW], wr[j % 2][:, :],
                                             ACT.Copy).then_inc(w_hi, 1)

                def body(u, r, b):
                    if not (known(u) and u == 2 * NT - 1):
                        split_h(u + 1, 1 - b)
                    if known(u) and u == NT - 1:
                        split_w(1)
                    if r == 1:
                        evacuate(act, lambda n, o, a: nc.scalar.activation(o, a, ACT.Sigmoid), u, b)

                split_h(0, 0)
                split_w(0)
                steps(act, body)

            @block.gpsimd
            def _(pool):
                def split_h(u, b):
                    pool.wait_ge(hi_d, u + 1)
                    nc.gpsimd.tensor_tensor(hl[b][:, :, :], h[:, :, :], hh[b][:, :, :], ALU.subtract).then_inc(lo_d, 1)

                def body(u, r, b):
                    if not (known(u) and u == 2 * NT - 1):
                        split_h(u + 1, 1 - b)

                split_h(0, 0)
                steps(pool, body)

            @block.tensor
            def _(pe):
                def transposes(u, b):
                    pe.wait_ge(xnd, u + 1)
                    for half in range(2):
                        if not (known(u) and u == 0):
                            pe.wait_ge(ht, 8 * u - 4 + 4 * half)
                        for k in range(4):
                            mm = nc.tensor.transpose(pst[half][:, k, :], x[b][:, (4 * half + k) * P:(4 * half + k + 1) * P],
                                                     g["ident"][:, :])
                        mm.then_inc(tp, 1)

                def product(n, k, b):
                    cols = slice(n * 512, (n + 1) * 512)
                    for m, (a, w) in enumerate(((hh, wh), (hl, wh), (hh, wl))):
                        mm = nc.tensor.matmul(pso[n][:, :], a[b][:, k, :], w[:, k, cols],
                                              start=k == 0 and m == 0, stop=k == KD - 1 and m == 2)
                    return mm

                def body(u, r, b):
                    if not (known(u) and u == 2 * NT - 1):
                        transposes(u + 1, 1 - b)
                    pe.wait_ge(lo_d, u + 1)
                    if known(u) and u in (0, NT - 1, NT):
                        for k in range(KD):
                            for n in range(4):
                                if u:
                                    if k == 0:
                                        pe.wait_ge(ev, 4 * u - 3 + n)
                                if u != NT - 1 and n % 2 == 0:
                                    pe.wait_ge(w_lo, 2 * KD * r + 2 * k + n // 2 + 1)
                                mm = product(n, k, b)
                                if k == KD - 1:
                                    mm.then_inc(po, 1)
                            if u == NT - 1 and k < KD - 1:
                                mm.then_inc(w_used, 1)
                        return
                    for n in range(4):
                        pe.wait_ge(ev, 4 * u - 3 + n)
                        for k in range(KD):
                            mm = product(n, k, b)
                        mm.then_inc(po, 1)

                transposes(0, 0)
                steps(pe, body)

            @block.vector
            def _(v):
                def norm(u, r, b):
                    v.wait_ge(x_in[b], 8 * (u - b) + 16)
                    v.tensor_scalar(x[b][:, :], x[b][:, :], g["rstd"][:, ds(u - NT * r, 1)], None, ALU.mult).then_inc(xnd, 1)

                def affine(u):
                    for k in range(KD):
                        v.wait_ge(tp, 2 * u + k // 4 + 1)
                        if k == 0 and not (known(u) and u == 0):
                            v.wait_ge(lo_d, u)
                        v.tensor_scalar(h[:, k, :], pst[k // 4][:, k % 4, :], g["acol"][:, 0, k:k + 1],
                                        g["bcol"][:, 0, k:k + 1], ALU.mult, ALU.add).then_inc(ht, 1)

                def split_w(r):
                    for j in range(2 * KD):
                        cols = slice(HW * (j % 2), HW * (j % 2) + HW)
                        v.wait_ge(w_hi, 2 * KD * r + j + 1)
                        v.tensor_tensor(wl[:, j // 2, cols], wr[j % 2][:, :], wh[:, j // 2, cols], ALU.subtract).then_inc(w_lo, 1)

                def body(u, r, b):
                    if not (known(u) and u == 2 * NT - 1):
                        affine(u + 1)
                    if not (known(u) and u >= 2 * NT - 2):
                        norm(u + 2, r + 1 if known(u) and u >= NT * r + NT - 2 else r, b)
                    if known(u) and u == NT - 1:
                        split_w(1)
                    if r == 0:
                        evacuate(v, lambda n, o, a: v.tensor_scalar(o, a, HD ** -0.5 if n == 0 else 1.0, None, ALU.mult), u, b)

                norm(0, 0, 0)
                affine(0)
                norm(1, 0, 1)
                split_w(0)
                steps(v, body)


def stage_attention(nc, g, A, S):
    NP_ = NH // 2
    with Ctx(nc) as c:
        qk = [c.sb(f"qk{b}", [P, 2 * AW]) for b in range(2)]
        vv = [c.sb(f"v{b}", [P, AW]) for b in range(4)]
        qT = [c.sb(f"qT{b}", [P, NP_, P]) for b in range(2)]
        kT = c.sb("kT", [P, NP_, 5, P])
        pr = [c.sb(f"probs{b}", [P, 2, 2 * P]) for b in range(4)]
        pT = [c.sb(f"probsT{b}", [P, 2, 2, P]) for b in range(2)]
        nm = [c.sb(f"negmax{b}", [P, 2]) for b in range(4)]
        osb = [c.sb(f"osb{b}", [P, AW + 2 * NH]) for b in range(2)]
        tick = c.sb("tick", [P, 4])
        ps_t = c.ps("ps_qk", [P, NP_, P])
        ps_s = [c.ps(f"ps_s{b}", [P, 2, 2 * P]) for b in range(4)]
        ps_p = [c.ps(f"ps_p{b}", [P, 2, 2, P]) for b in range(2)]
        ps_o = c.ps("ps_o", [P, NH, HD])
        qk_in = [c.sem(f"qk_in{b}") for b in range(2)]
        v_in = [c.sem(f"v_in{b}") for b in range(4)]
        tq, qkT = c.sem("qk_psum"), c.sem("qkT_done")
        k_again = c.sem("k_again")
        mx = c.sem("max_done")
        s_ps, s_sb = c.sem("s_psum"), c.sem("s_biased")
        ex = c.sem("exp_done")
        p_ps, p_sb = c.sem("pT_psum"), c.sem("pT_done")
        pv, oe = c.sem("pv_done"), c.sem("o_evac")
        o_st = [c.sem(f"o_st{b}") for b in range(2)]

        rows = S["qkvu"]

        def head(j, h):
            return 4 * (j // 2) + j % 2 + 2 * h

        def tokens(dram, d, i, r, c0, c1):
            if d == 1:
                return dram.rearrange("(b p) n -> b p n", p=P)[ds(4 * i + r, 1), :, c0:c1].rearrange("a p n -> (a p) n")
            if d == 4:
                v = dram.rearrange("(b p s) n -> b s p n", p=P, s=4)
                return v[r, ds(i, 1), :, c0:c1].rearrange("a p n -> (a p) n")
            v = dram.rearrange("(p s) n -> s p n", s=16)
            return v[ds(4 * i + r, 1), :, c0:c1].rearrange("a p n -> (a p) n")

        def groups(eng, body):
            for p in range(len(DILS)):
                if p == 0:
                    body(p, 0, True)
                with eng.Fori(1 if p == 0 else 0, 4) as i:
                    body(p, i, False)

        def prev(p, r, first):
            return p == 0 and (r > 0 or not first) or p == 1 and r > 0

        with nc.Block() as block:
            @block.sync
            def _(sp):
                def body(p, i, first):
                    for r in range(4):
                        u = 16 * p + 4 * i + r
                        if not (first and r < 2):
                            sp.wait_ge(tq, 2 * u - 2)
                        sp.dma_start(qk[r % 2][:, :], tokens(rows, DILS[p], i, r, 0, 2 * AW)).then_inc(qk_in[r % 2], 16)
                        if not first:
                            sp.wait_ge(pv, NP_ * (u - 2))
                        sp.dma_start(vv[r][:, :], tokens(rows, DILS[p], i, r, 2 * AW, 3 * AW)).then_inc(v_in[r], 16)
                groups(sp, body)

            @block.gpsimd
            def _(pool):
                def body(p, i, first):
                    for r in range(4):
                        u = 16 * p + 4 * i + r
                        pool.wait_ge(oe, u + 1)
                        pool.dma_start(tokens(S["o"][p], DILS[p], i, r, 0, AW + 2 * NH), osb[r % 2][:, :]).then_inc(o_st[r % 2], 16)
                groups(pool, body)
                for b in range(2):
                    pool.wait_ge(o_st[b], 16 * 24)

            @block.tensor
            def _(pe):
                def body(p, i, first):
                    u0 = 16 * p + 4 * i
                    n0 = NP_ * u0

                    def turn_qk(r, h):
                        u = u0 + r
                        pe.wait_ge(qk_in[r % 2], 16 * (8 * p + 2 * i + r // 2 + 1))
                        if not (first and r == 0 and h == 0):
                            pe.wait_ge(qkT, 2 * u + h)
                        for n in range(NP_):
                            mm = nc.tensor.transpose(ps_t[:, n, :], qk[r % 2][:, (NP_ * h + n) * P:(NP_ * h + n + 1) * P],
                                                     g["ident"][:, :])
                        mm.then_inc(tq, 1)

                    def scores(m):
                        r, j = m // NP_, m % NP_
                        has = prev(p, r, first)
                        own = 4 if r == 0 and has else r
                        pe.wait_ge(qkT, 2 * (u0 + r) + 2)
                        if own == 4:
                            pe.wait_ge(k_again, i)
                        if not (first and m < 4):
                            pe.wait_ge(s_sb, n0 + m - 3)
                        for h in range(2):
                            hh = head(j, h)
                            lo, hi = HD * (hh % 2), HD * (hh % 2 + 1)
                            keys = slice(own - 1, own + 1) if has else slice(own, own + 1)
                            mm = nc.tensor.matmul(ps_s[m % 4][:, h, (0 if has else P):], qT[r % 2][lo:hi, hh // 2, :],
                                                  kT[lo:hi, hh // 2, keys, :], start=True, stop=True)
                        mm.then_inc(s_ps, 1)

                    def turn(m):
                        pe.wait_ge(ex, n0 + m + 1)
                        if not (first and m < 2):
                            pe.wait_ge(p_sb, n0 + m - 1)
                        for h in range(2):
                            for w in range(0 if prev(p, m // NP_, first) else 1, 2):
                                mm = nc.tensor.transpose(ps_p[m % 2][:, h, w, :], pr[m % 4][:, h, w * P:(w + 1) * P],
                                                         g["ident"][:, :])
                        mm.then_inc(p_ps, 1)

                    def values(m):
                        r, j = m // NP_, m % NP_
                        if j == 0:
                            pe.wait_ge(v_in[r], 16 * (4 * p + i + 1))
                            if not (first and r == 0):
                                pe.wait_ge(oe, u0 + r)
                        pe.wait_ge(p_sb, n0 + m + 1)
                        has = prev(p, r, first)
                        for h in range(2):
                            hh = head(j, h)
                            for w in range(0 if has else 1, 2):
                                mm = nc.tensor.matmul(ps_o[:, hh, :], pT[m % 2][:, h, w, :],
                                                      vv[(r - 1 + w) % 4][:, hh * HD:(hh + 1) * HD],
                                                      start=not (has and w), stop=w == 1)
                        mm.then_inc(pv, 1)

                    turn_qk(0, 0)
                    turn_qk(0, 1)
                    scores(0)
                    scores(1)
                    for m in range(4 * NP_):
                        r, j = m // NP_, m % NP_
                        if m + 2 < 4 * NP_:
                            scores(m + 2)
                        if j < 2 and r < 3:
                            turn_qk(r + 1, j)
                        turn(m)
                        if m:
                            values(m - 1)
                    values(4 * NP_ - 1)
                groups(pe, body)

            @block.vector
            def _(v):
                def body(p, i, first):
                    u0 = 16 * p + 4 * i
                    n0 = NP_ * u0

                    def evac_qk(r, h):
                        u = u0 + r
                        v.wait_ge(tq, 2 * u + h + 1)
                        if not (first and r < 2):
                            v.wait_ge(s_ps, NP_ * (u - 1))
                        dst = kT[:, :, r, :] if h else qT[r % 2][:, :, :]
                        v.tensor_copy(dst, ps_t[:, :, :]).then_inc(qkT, 1)
                        if h and r == 0 and p == 0 and not first:
                            v.wait_ge(qkT, 2 * u + 2)
                            v.tensor_copy(kT[:, :, 4, :], kT[:, :, 0, :]).then_inc(k_again, 1)

                    def bias_max(m):
                        r, j = m // NP_, m % NP_
                        u, n, b = u0 + r, n0 + m, m % 4
                        k0 = 0 if prev(p, r, first) else P
                        if j == 0 and not (first and r < 2):
                            v.wait_ge(o_st[r % 2], 16 * (8 * p + 2 * i + r // 2))
                        if not (first and m < 4):
                            v.wait_ge(p_ps, n - 3)
                        v.wait_ge(s_ps, n + 1)
                        v.memset(tick[:, b:b + 1], 0.0)
                        for h in range(2):
                            hh = head(j, h)
                            v.tensor_tensor_reduce(pr[b][:, h, k0:], ps_s[b][:, h, k0:], g["bias"][:, p, hh, k0:], 1.0, -3e38,
                                                   ALU.add, ALU.max, osb[r % 2][:, AW + hh:AW + hh + 1]).then_inc(mx, 1)
                        v.wait_ge(mx, 2 * n + 2)
                        v.tensor_scalar(nm[b][:, :], osb[r % 2][:, AW + head(j, 0):AW + head(j, 1) + 1:2], -1.0, None,
                                        ALU.mult).then_inc(s_sb, 1)

                    def evac_o(r):
                        u = u0 + r
                        v.wait_ge(pv, NP_ * u + NP_)
                        v.wait_ge(ex, NP_ * u + NP_)
                        v.tensor_copy(osb[r % 2][:, 0:AW], ps_o[:, :, :].rearrange("p h d -> p (h d)")).then_inc(oe, 1)

                    evac_qk(0, 0)
                    evac_qk(0, 1)
                    for m in range(4 * NP_):
                        r, j = m // NP_, m % NP_
                        bias_max(m)
                        if j == 1 and r:
                            evac_o(r - 1)
                        if j in (1, 2) and r < 3:
                            evac_qk(r + 1, j - 1)
                    evac_o(3)
                v.wait_ge(g["bias_in"], 16 * len(DILS))
                groups(v, body)

            @block.scalar
            def _(act):
                def body(p, i, first):
                    n0 = NP_ * (16 * p + 4 * i)
                    for m in range(4 * NP_ + 1):
                        if m < 4 * NP_:
                            r, j = m // NP_, m % NP_
                            k0 = 0 if prev(p, r, first) else P
                            act.wait_ge(s_sb, n0 + m + 1)
                            for h in range(2):
                                hh = head(j, h)
                                e = nc.scalar.activation(pr[m % 4][:, h, k0:], pr[m % 4][:, h, k0:], ACT.Exp,
                                                         bias=nm[m % 4][:, h:h + 1],
                                                         accum_out=osb[r % 2][:, AW + NH + hh:AW + NH + hh + 1])
                            e.then_inc(ex, 1)
                        if m:
                            q = m - 1
                            act.wait_ge(p_ps, n0 + m)
                            if not (first and q < 2):
                                act.wait_ge(pv, n0 + q - 1)
                            w0 = 0 if prev(p, q // NP_, first) else 1
                            nc.scalar.activation(pT[q % 2][:, :, w0:, :], ps_p[q % 2][:, :, w0:, :], ACT.Copy).then_inc(p_sb, 1)
                groups(act, body)


def stage_ssm(nc, g, A, S):
    with Ctx(nc) as c:
        u = c.sb("u_chunks", [P, LC, SW])
        y = c.sb("y_chunks", [P, LC, SW])
        rec = [c.sb(f"rec{b}", [P, REC]) for b in range(4)]
        ug = [c.sb(f"ug{b}", [P, LC, CH_S]) for b in range(2)]
        uT = [c.sb(f"uT{b}", [P, 2, P]) for b in range(4)]
        t = [[c.sb(f"rt{b}{n}", [P, NC]) for n in range(4)] for b in range(2)]
        hin = [c.sb(f"hin{b}", [P, 2, NC + 1]) for b in range(2)]
        psU = [c.ps(f"psU{b}", [P, 2, P]) for b in range(2)]
        psB = [c.ps(f"psB{b}", [P, 2, NC]) for b in range(2)]
        psY = [c.ps(f"psY{b}", [P, LC, CH_S]) for b in range(2)]
        u_in, rec_in = c.sem("u_in"), [c.sem(f"rec_in{b}") for b in range(4)]
        ugd, utp, utd = c.sem("ug_done"), c.sem("uT_psum"), c.sem("uT_done")
        b_ps, h_done, y_ps, y_done = c.sem("b_psum"), c.sem("h_done"), c.sem("y_psum"), c.sem("y_done")
        z0, rs, y_st = c.sem("hin_zero"), c.sem("rec_step"), c.sem("y_st")
        rot, rho = [c.sb(f"rot_sb{n}", [P, NG_S, NC]) for n in range(2)], c.sb("rho_sb", [P, NG_S])
        rot_in = c.sem("rot_in")

        def known(n):
            return isinstance(n, int)

        def past(n, k):
            return not known(n) or n >= k

        def groups(eng, body):
            for q in range(4):
                body(q, q, 0)
            with eng.Fori(1, NG_S // 4 - 1) as i:
                for q in range(4):
                    body(4 * i + q, q, i)
            for q in range(4):
                body(NG_S - 4 + q, q, NG_S // 4 - 1)

        with nc.Block() as block:
            @block.sync
            def _(sp):
                uv = S["qkvu"].rearrange("(j s) n -> j s n", s=LC)
                sp.dma_start(u[:, :, :], uv[:, :, 3 * AW:]).then_inc(u_in, 16)
                for n in range(2):
                    sp.dma_start(rot[n][:, :, :], S["rot"][n]).then_inc(rot_in, 16)
                sp.dma_start(rho[:, :], S["rho"]).then_inc(rot_in, 16)
                load_bias(sp, g, S)

                def body(n, q, i):
                    if past(n, 4):
                        sp.wait_ge(y_ps, n - 3)
                    sp.dma_start(rec[q][:, :], S["rec"][ds(n, 1)].rearrange("a p n -> (a p) n")).then_inc(rec_in[q], 16)
                groups(sp, body)
                sp.wait_ge(y_done, NG_S)
                sp.dma_start(S["y"].rearrange("(j s) n -> j s n", s=LC), y[:, :, :]).then_inc(y_st, 16)
                sp.wait_ge(y_st, 16)

            @block.gpsimd
            def _(pool):
                pool.wait_ge(u_in, 16)

                def body(n, q, i):
                    if past(n, 2):
                        pool.wait_ge(utp, n - 1)
                    nc.gpsimd.tensor_copy(ug[q % 2][:, :, :], u[:, :, ds(CH_S * n, CH_S)]).then_inc(ugd, 1)
                groups(pool, body)

            @block.tensor
            def _(pe):
                def turn(n, q):
                    pe.wait_ge(ugd, n + 1)
                    if past(n, 2):
                        pe.wait_ge(utd, n - 1)
                    for k in range(2):
                        mm = nc.tensor.transpose(psU[q % 2][:, k, :], ug[q % 2][:, 8 * k:8 * k + 8, :].rearrange("p s c -> p (s c)"),
                                                 g["ident"][:, :])
                    mm.then_inc(utp, 1)

                def states(n, q, i):
                    pe.wait_ge(utd, n + 1)
                    pe.wait_ge(rec_in[q], 16 * i + 16)
                    if past(n, 2):
                        pe.wait_ge(h_done, n - 1)
                    for r in range(2):
                        for k in range(2):
                            mm = nc.tensor.matmul(psB[q % 2][:, r, :], rec[q][:, 192 * k + 64 * r:192 * k + 64 * r + P],
                                                  uT[q][:, k, :], start=k == 0, stop=k == 1)
                    mm.then_inc(b_ps, 1)

                def outputs(n, q):
                    if past(n, 2):
                        pe.wait_ge(y_done, n - 1)
                    o = psY[q % 2][:, :, :].rearrange("p s c -> p (s c)")
                    nc.tensor.matmul(o, uT[q][:, 0, :], rec[q][:, 896:1152], start=True, stop=False, skip_group_check=True)
                    nc.tensor.matmul(o[:, P:], uT[q][:, 1, :], rec[q][:, 1152 + P:1408], start=False, stop=False,
                                     skip_group_check=True)
                    pe.wait_ge(h_done, n + 1)
                    for r in range(2):
                        mm = nc.tensor.matmul(o, hin[q % 2][:, r, 0:NC], rec[q][:, 384 + 256 * r:640 + 256 * r],
                                              start=False, stop=r == 1, skip_group_check=True)
                    mm.then_inc(y_ps, 1)

                def body(n, q, i):
                    if not (known(n) and n == NG_S - 1):
                        turn(n + 1, (q + 1) % 4)
                    states(n, q, i)
                    if past(n, 1):
                        outputs(n - 1, (q - 1) % 4)

                turn(0, 0)
                groups(pe, body)
                outputs(NG_S - 1, 3)

            @block.scalar
            def _(act):
                def evac(n, q):
                    act.wait_ge(utp, n + 1)
                    if past(n, 4):
                        act.wait_ge(y_ps, n - 3)
                    nc.scalar.activation(uT[q][:, :, :], psU[q % 2][:, :, :], ACT.Copy).then_inc(utd, 1)

                def gelu(n, q):
                    act.wait_ge(y_ps, n + 1)
                    nc.scalar.activation(y[:, :, ds(CH_S * n, CH_S)], psY[q % 2][:, :, :], ACT.Gelu_apprx_tanh).then_inc(y_done, 1)

                def body(n, q, i):
                    if not (known(n) and n == NG_S - 1):
                        evac(n + 1, (q + 1) % 4)
                    if past(n, 1):
                        gelu(n - 1, (q - 1) % 4)

                evac(0, 0)
                groups(act, body)
                gelu(NG_S - 1, 3)

            @block.vector
            def _(v):
                for b in range(2):
                    v.memset(hin[b][:, :, 0:1], 0.0).then_inc(z0, 1)
                v.wait_ge(rot_in, 48)

                def body(n, q, i):
                    b = q % 2
                    v.wait_ge(b_ps, n + 1)
                    x = [a[:, :] for a in t[b]]
                    rr, ri = (r[:, ds(n, 1), :].rearrange("p a j -> p (a j)") for r in rot)
                    v.tensor_tensor(x[0], psB[b][:, 0, :], rr, ALU.mult).then_inc(rs, 1)
                    v.tensor_tensor(x[1], psB[b][:, 1, :], ri, ALU.mult).then_inc(rs, 1)
                    v.wait_ge(rs, 4 * n + 2)
                    v.tensor_tensor(x[2], x[0], x[1], ALU.add).then_inc(rs, 1)
                    v.wait_ge(rs, 4 * n + 3)
                    v.tensor_tensor_scan(x[3], rho[:, ds(n, 1)].to_broadcast([P, NC]), x[2], 0.0, ALU.mult, ALU.add).then_inc(rs, 1)
                    v.wait_ge(rs, 4 * n + 4)
                    if past(n, 2):
                        v.wait_ge(y_ps, n - 1)
                    v.tensor_tensor(hin[b][:, 0, 1:], x[3], rr, ALU.mult)
                    v.tensor_tensor(hin[b][:, 1, 1:], x[3], ri, ALU.mult).then_inc(h_done, 1)
                groups(v, body)


NR = NGR + NE


def stage_merge(nc, g, A, S):
    KA = AW // P
    with Ctx(nc) as c:
        wA = c.sb("w_branch_a", [P, KA, D])
        wS = c.sb("w_branch_s", [P, KA, D])
        wO = c.sb("w_out_sb", [P, KD, D])
        wG = c.sb("w_glu_sb", [P, KA, SW])
        wR = c.sb("w_router", [P, KD, NR])
        bG = c.sb("b_glu_row", [P, SW])
        bR = c.sb("b_router", [P, NR])
        o = [c.sb(f"o_in{b}", [P, 3, AW + 2 * NH]) for b in range(2)]
        y = [c.sb(f"y_in{b}", [P, SW]) for b in range(2)]
        gt = [c.sb(f"gt_in{b}", [P, 2, D]) for b in range(2)]
        x = [c.sb(f"x_in{b}", [P, D]) for b in range(2)]
        acc = [c.sb(f"acc{n}", [P, NH, HD]) for n in range(3)]
        at = c.sb("attn", [P, NH, HD])
        sm = c.sb("ssm_out", [P, SW])
        z = c.sb("glu_z", [P, SW])
        ez = c.sb("glu_e", [P, SW])
        mg = [c.sb(f"mg{n}", [P, D]) for n in range(2)]
        x1 = [c.sb(f"x1_{b}", [P, D]) for b in range(2)]
        xn = [c.sb(f"xn2_{b}", [P, D]) for b in range(2)]
        junk = c.sb("junk_m", [P, D])
        yT, aT, sT = (c.sb(n, [P, KA, P]) for n in ("yT", "aT", "sT"))
        mT = c.sb("mT", [P, KD, P])
        xT = c.sb("x2T", [P, KD, P])
        mx = c.sb("mx_all", [P, NH])
        df = c.sb("m_less", [P, 3, NH])
        wt = c.sb("pat_w", [P, 3, NH])
        wl = c.sb("pat_wl", [P, 3, NH])
        ll = c.sb("pat_l", [P, NH])
        li = c.sb("pat_li", [P, NH])
        wn = c.sb("pat_wn", [P, 3, NH])
        ssq = c.sb("ssq", [P, 3])
        st = {n: c.sb(f"st_{n}", [P, 1]) for n in ("s", "ms", "rt", "rstd", "ms2", "rt2", "rstd2")}
        psT = [c.ps(f"psT{b}", [P, 4, P]) for b in range(2)]
        psA = c.ps("psBA", [P, 2, 512])
        psS = c.ps("psBS", [P, 2, 512])
        psW = c.ps("psW", [P, 2, 512])
        w_in = c.sem("mw_in")
        o_in, y_in, g_in, x_in = ([c.sem(f"{n}{b}") for b in range(2)] for n in ("mo_in", "my_in", "mg_in", "mx_in"))
        y_tp, a_tp, s_tp, m_tp, x_tp = (c.sem(n) for n in ("y_tp", "a_tp", "s_tp", "m_tp", "x_tp"))
        y_T, a_T, s_T, m_T, x_T = (c.sem(n) for n in ("y_T", "a_T", "s_T", "m_T", "x_T"))
        glu_mm, a_mm, s_mm, w_mm, r_mm = (c.sem(n) for n in ("glu_mm", "a_mm", "s_mm", "w_mm", "r_mm"))
        cmb, cw, at_d = c.sem("comb_step"), c.sem("comb_exp"), c.sem("attn_done")
        z_d, ez_d, gl, s_d = c.sem("z_done"), c.sem("ez_done"), c.sem("glu_step"), c.sem("ssm_gated")
        mgs, m_d = c.sem("merge_step"), c.sem("merged")
        sq, ms_d, rt_d, x1s, x1_d, xn_d = (c.sem(n) for n in ("msq", "mms", "mrt", "x1_step", "x1_done", "xn2_done"))
        lg_d = c.sem("logits_done")
        x1_st, xn_st = ([c.sem(f"{n}{b}") for b in range(2)] for n in ("x1_st", "xn2_st"))
        NSTEP = NT + 2

        def real(t):
            return not isinstance(t, int) or 0 <= t < NT

        def past(t, n):
            return not isinstance(t, int) or t >= n

        def steps(eng, body):
            for s in range(4):
                body(s, s // 2, s % 2)
            with eng.Fori(2, NT // 2 - 1) as i:
                for b in range(2):
                    body(2 * i + b, i, b)
            for s in range(NT - 2, NSTEP):
                body(s, s // 2, s % 2)

        def tile(dram, t):
            return dram.rearrange("(t p) n -> t p n", p=P)[ds(t, 1)].rearrange("a p n -> (a p) n")

        with nc.Block() as block:
            @block.sync
            def _(sp):
                def load_oyg(t, b):
                    for n in range(3):
                        sp.dma_start(o[b][:, n, :], tile(S["o"][n], t)).then_inc(o_in[b], 16)
                    sp.dma_start(y[b][:, :], tile(S["y"], t)).then_inc(y_in[b], 16)
                    sp.dma_start(gt[b][:, :, :].rearrange("p a n -> p (a n)"), tile(S["gates"], t)).then_inc(g_in[b], 16)

                def load_x(t, b):
                    sp.dma_start(x[b][:, :], tile(A["x"][0], t)).then_inc(x_in[b], 16)

                sp.dma_start(wG[:, :, :], A["w_glu"][0].rearrange("(k p) n -> p k n", p=P)).then_inc(w_in, 16)
                sp.dma_start(bG[:, :], A["b_glu"].to_broadcast([P, SW])).then_inc(w_in, 16)
                load_oyg(0, 0)
                for dst, name in ((wA, "w_branch_attn"), (wS, "w_branch_ssm")):
                    sp.dma_start(dst[:, :, :], A[name][0].rearrange("(k p) n -> p k n", p=P)).then_inc(w_in, 16)
                load_oyg(1, 1)
                load_x(0, 0)
                load_x(1, 1)
                sp.dma_start(wO[:, :, :], A["w_out"][0].rearrange("(k p) n -> p k n", p=P)).then_inc(w_in, 16)
                sp.dma_start(wR[:, :, 0:NGR], A["w_router_group"][0].rearrange("(k p) n -> p k n", p=P)).then_inc(w_in, 16)
                sp.dma_start(wR[:, :, NGR:], A["w_router_expert"][0].rearrange("(k p) n -> p k n", p=P)).then_inc(w_in, 16)
                sp.dma_start(bR[:, 0:NGR], A["b_router_group"].to_broadcast([P, NGR])).then_inc(w_in, 16)
                sp.dma_start(bR[:, NGR:], A["b_router_expert"].to_broadcast([P, NE])).then_inc(w_in, 16)

                def body(s, i, b):
                    if real(s - 2):
                        sp.wait_ge(x1_d, s - 1)
                        sp.dma_start(tile(S["x1"], s - 2), x1[b][:, :]).then_inc(x1_st[b], 16)
                        if real(s):
                            load_x(s, b)
                        sp.wait_ge(xn_d, s - 1)
                        sp.dma_start(tile(S["xn2"], s - 2), xn[b][:, :]).then_inc(xn_st[b], 16)
                    if real(s) and real(s + 2):
                        sp.wait_ge(at_d, s + 1)
                        sp.wait_ge(s_d, s + 1)
                        sp.wait_ge(m_d, s + 1)
                        load_oyg(s + 2, b)
                steps(sp, body)
                for b in range(2):
                    sp.wait_ge(x1_st[b], 16 * NT // 2)
                    sp.wait_ge(xn_st[b], 16 * NT // 2)

            @block.tensor
            def _(pe):
                def turn(bank, src, sem):
                    n = src.shape[1] // P
                    for k in range(n):
                        mm = nc.tensor.transpose(psT[bank][:, k, :], src[:, k * P:(k + 1) * P], g["ident"][:, :])
                    mm.then_inc(sem, 1)

                def product(o_, xT_, w_, width):
                    for h in range((width + 511) // 512):
                        n = min(512, width - 512 * h)
                        for k in range(w_.shape[1]):
                            mm = nc.tensor.matmul(o_[:, h, 0:n], xT_[:, k, :], w_[:, k, 512 * h:512 * h + n],
                                                  start=k == 0, stop=k == w_.shape[1] - 1)
                    return mm

                def body(s, i, b):
                    if real(s):
                        pe.wait_ge(y_in[b], 16 * i + 16)
                        if past(s, 1):
                            pe.wait_ge(s_T, s)
                        turn(0, y[b], y_tp)
                        pe.wait_ge(at_d, s + 1)
                        if past(s, 2):
                            pe.wait_ge(m_T, 2 * s - 2)
                        turn(1, at[:, :, :].rearrange("p h d -> p (h d)"), a_tp)
                        pe.wait_ge(y_T, s + 1)
                        if past(s, 1):
                            pe.wait_ge(m_d, s)
                        product(psS, yT, wG, SW).then_inc(glu_mm, 1)
                        pe.wait_ge(a_T, s + 1)
                        product(psA, aT, wA, D).then_inc(a_mm, 1)
                    if real(s - 2):
                        pe.wait_ge(xn_d, s - 1)
                        if not real(s):
                            pe.wait_ge(s_T, NT)
                            pe.wait_ge(m_T, 2 * (s - 1))
                            pe.wait_ge(m_d, NT)
                        turn(0, xn[b][:, 0:512], x_tp)
                        turn(1, xn[b][:, 512:1024], x_tp)
                        pe.wait_ge(x_T, 2 * (s - 1))
                        for k in range(KD):
                            mm = nc.tensor.matmul(psS[:, 1, 0:NR], xT[:, k, :], wR[:, k, :], start=k == 0, stop=k == KD - 1)
                        mm.then_inc(r_mm, 1)
                    if real(s - 1):
                        pe.wait_ge(m_d, s)
                        turn(0, mg[0][:, 0:512], m_tp)
                        turn(1, mg[0][:, 512:1024], m_tp)
                    if real(s):
                        pe.wait_ge(s_d, s + 1)
                        if past(s, 1):
                            pe.wait_ge(m_T, 2 * s - 1)
                        turn(0, sm, s_tp)
                        pe.wait_ge(s_T, s + 1)
                        if past(s, 2):
                            pe.wait_ge(lg_d, s - 1)
                        product(psS, sT, wS, D).then_inc(s_mm, 1)
                    if real(s - 1):
                        pe.wait_ge(m_T, 2 * s)
                        if past(s, 2):
                            pe.wait_ge(x1_d, s - 1)
                        product(psW, mT, wO, D).then_inc(w_mm, 1)

                pe.wait_ge(w_in, 16 * 9)
                steps(pe, body)

            @block.scalar
            def _(act):
                def leave(bank, dst, tp, n_tp, used, n_used, done):
                    act.wait_ge(tp, n_tp)
                    if n_used is not None:
                        act.wait_ge(used, n_used)
                    nc.scalar.activation(dst, psT[bank][:, :, :], ACT.Copy).then_inc(done, 1)

                def weights(t):
                    act.wait_ge(cmb, 12 * t + 3)
                    nc.scalar.activation(wt[:, :, :], df[:, :, :], ACT.Exp).then_inc(cw, 1)

                def root(dst, src):
                    nc.scalar.activation(dst[:, :], src[:, :], ACT.Sqrt).then_inc(rt_d, 1)

                def body(s, i, b):
                    t = s - 2
                    if real(t):
                        act.wait_ge(w_mm, t + 1)
                        if past(t, 1):
                            act.wait_ge(sq, 2 * t)
                            act.wait_ge(ms_d, 2 * t)
                        nc.scalar.activation(junk[:, :], psW[:, :, :].rearrange("p a n -> p (a n)"), ACT.Square,
                                             accum_out=ssq[:, 0:1]).then_inc(sq, 1)
                    if real(s):
                        leave(0, yT[:, :, :], y_tp, s + 1, glu_mm, s if past(s, 1) else None, y_T)
                        leave(1, aT[:, :, :], a_tp, s + 1, a_mm, s if past(s, 1) else None, a_T)
                    if real(t):
                        act.wait_ge(ms_d, 2 * t + 1)
                        root(st["rt"], st["ms"])
                        act.wait_ge(x1_d, t + 1)
                        act.wait_ge(sq, 2 * t + 1)
                        nc.scalar.activation(junk[:, :], x1[b][:, :], ACT.Square, accum_out=ssq[:, 1:2]).then_inc(sq, 1)
                        act.wait_ge(ms_d, 2 * t + 2)
                        root(st["rt2"], st["ms2"])
                    if real(s):
                        act.wait_ge(z_d, s + 1)
                        nc.scalar.activation(ez[:, :], z[:, :], ACT.Exp, scale=-1.0).then_inc(ez_d, 1)
                    if real(t):
                        for h in range(2):
                            act.wait_ge(x_tp, 2 * t + h + 1)
                            if past(s, 3) and h == 0:
                                act.wait_ge(r_mm, t)
                            for k in range(4):
                                kk = 4 * h + k
                                e = nc.scalar.activation(xT[:, kk, :], psT[h][:, k, :], ACT.Identity,
                                                         bias=g["bcol"][:, 1, kk:kk + 1], scale=g["acol"][:, 1, kk:kk + 1])
                            e.then_inc(x_T, 1)
                    if real(s - 1):
                        for h in range(2):
                            leave(h, mT[:, 4 * h:4 * h + 4, :], m_tp, 2 * (s - 1) + h + 1, w_mm, s - 1 if past(s, 2) else None, m_T)
                    if real(s):
                        leave(0, sT[:, :, :], s_tp, s + 1, s_mm, s if past(s, 1) else None, s_T)
                    if real(s + 1) and real(s):
                        weights(s + 1)

                weights(0)
                steps(act, body)

            @block.vector
            def _(v):
                def did(ins, sem, n):
                    ins.then_inc(sem, 1)
                    v.wait_ge(sem, n)

                def combine(t, i, b):
                    n = 12 * t
                    v.wait_ge(o_in[b], 48 * i + 48)
                    m, l = o[b][:, :, AW:AW + NH], o[b][:, :, AW + NH:]
                    did(v.tensor_tensor(mx[:, :], m[:, 0, :], m[:, 1, :], ALU.max), cmb, n + 1)
                    did(v.tensor_tensor(mx[:, :], mx[:, :], m[:, 2, :], ALU.max), cmb, n + 2)
                    did(v.tensor_tensor(df[:, :, :], m, mx[:, :].unsqueeze(1).to_broadcast([P, 3, NH]), ALU.subtract), cmb, n + 3)
                    v.wait_ge(cw, t + 1)
                    did(v.tensor_tensor(wl[:, :, :], wt[:, :, :], l, ALU.mult), cmb, n + 4)
                    did(v.tensor_tensor(ll[:, :], wl[:, 0, :], wl[:, 1, :], ALU.add), cmb, n + 5)
                    did(v.tensor_tensor(ll[:, :], ll[:, :], wl[:, 2, :], ALU.add), cmb, n + 6)
                    did(v.reciprocal(li[:, :], ll[:, :]), cmb, n + 7)
                    did(v.tensor_tensor(wn[:, :, :], wt[:, :, :], li[:, :].unsqueeze(1).to_broadcast([P, 3, NH]), ALU.mult), cmb, n + 8)
                    for p in range(3):
                        v.tensor_tensor(acc[p][:, :, :], o[b][:, p, 0:AW].rearrange("p (h d) -> p h d", d=HD),
                                        wn[:, p, :].unsqueeze(2).to_broadcast([P, NH, HD]), ALU.mult).then_inc(cmb, 1)
                    v.wait_ge(cmb, n + 11)
                    did(v.tensor_tensor(acc[0][:, :, :], acc[0][:, :, :], acc[1][:, :, :], ALU.add), cmb, n + 12)
                    if past(t, 1):
                        v.wait_ge(a_tp, t)
                    v.tensor_tensor(at[:, :, :], acc[0][:, :, :], acc[2][:, :, :], ALU.add).then_inc(at_d, 1)

                def gated(t, b):
                    v.wait_ge(glu_mm, t + 1)
                    if past(t, 1):
                        v.wait_ge(ez_d, t)
                    v.tensor_tensor(z[:, :], psS[:, 0, :], bG[:, :], ALU.add).then_inc(z_d, 1)
                    v.wait_ge(ez_d, t + 1)
                    did(v.tensor_scalar(ez[:, :], ez[:, :], 1.0, None, ALU.add), gl, 2 * t + 1)
                    did(v.reciprocal(ez[:, :], ez[:, :]), gl, 2 * t + 2)
                    if past(t, 1):
                        v.wait_ge(s_tp, t)
                    v.tensor_tensor(sm[:, :], ez[:, :], y[b][:, :], ALU.mult).then_inc(s_d, 1)

                def logits(t):
                    v.wait_ge(r_mm, t + 1)
                    v.tensor_tensor(g["logits"][:, ds(t, 1), :].rearrange("p a n -> p (a n)"), psS[:, 1, 0:NR], bR[:, :],
                                    ALU.add).then_inc(lg_d, 1)

                def residual(t, i, b):
                    v.wait_ge(sq, 2 * t + 1)
                    if past(t, 1):
                        v.wait_ge(rt_d, 2 * t)
                    v.tensor_scalar(st["ms"][:, :], ssq[:, 0:1], 1.0 / D, EPS, ALU.mult, ALU.add).then_inc(ms_d, 1)
                    v.wait_ge(rt_d, 2 * t + 1)
                    did(v.reciprocal(st["rstd"][:, :], st["rt"][:, :]), x1s, 3 * t + 1)
                    if past(t, 2):
                        v.wait_ge(x1_st[b], 16 * i)
                    v.wait_ge(x_in[b], 16 * i + 16)
                    did(v.scalar_tensor_tensor(out=x1[b][:, :], in0=psW[:, :, :].rearrange("p a n -> p (a n)"),
                                               scalar=st["rstd"][:, 0:1], in1=g["grow"][:, 0, :], op0=ALU.mult, op1=ALU.mult),
                        x1s, 3 * t + 2)
                    v.tensor_tensor(x1[b][:, :], x1[b][:, :], x[b][:, :], ALU.add).then_inc(x1_d, 1)
                    v.wait_ge(sq, 2 * t + 2)
                    v.tensor_scalar(st["ms2"][:, :], ssq[:, 1:2], 1.0 / D, EPS, ALU.mult, ALU.add).then_inc(ms_d, 1)
                    v.wait_ge(rt_d, 2 * t + 2)
                    did(v.reciprocal(st["rstd2"][:, :], st["rt2"][:, :]), x1s, 3 * t + 3)
                    if past(t, 2):
                        v.wait_ge(xn_st[b], 16 * i)
                        v.wait_ge(x_tp, 2 * t - 2)
                    v.tensor_scalar(xn[b][:, :], x1[b][:, :], st["rstd2"][:, 0:1], None, ALU.mult).then_inc(xn_d, 1)

                def merge(t, i, b):
                    v.wait_ge(s_mm, t + 1)
                    v.wait_ge(a_mm, t + 1)
                    v.wait_ge(g_in[b], 16 * i + 16)
                    if past(t, 1):
                        v.wait_ge(m_tp, 2 * t)
                    flat = [p_[:, :, :].rearrange("p a n -> p (a n)") for p_ in (psA, psS)]
                    v.tensor_tensor(mg[0][:, :], flat[0], gt[b][:, 0, :], ALU.mult).then_inc(mgs, 1)
                    v.tensor_tensor(mg[1][:, :], flat[1], gt[b][:, 1, :], ALU.mult).then_inc(mgs, 1)
                    v.wait_ge(mgs, 2 * t + 2)
                    v.tensor_tensor(mg[0][:, :], mg[0][:, :], mg[1][:, :], ALU.add).then_inc(m_d, 1)

                def body(s, i, b):
                    if real(s - 2):
                        residual(s - 2, i - 1, b)
                    if real(s):
                        gated(s, b)
                    if real(s - 2):
                        logits(s - 2)
                    if real(s + 1) and real(s):
                        combine(s + 1, i + b, 1 - b)
                    if real(s):
                        merge(s, i, b)

                v.wait_ge(w_in, 16 * 9)
                combine(0, 0, 0)
                steps(v, body)


def stage_route(nc, g, A, S):
    with Ctx(nc) as c:
        def sb(name, shape, dt=F32):
            return c.sb("r_" + name, shape, dt)

        lg = g["logits"]
        w8, w8i = sb("w8", [P, EPG]), sb("w8i", [P, EPG], I32)
        bi, bf = sb("bi", [P, NBLK], I32), sb("bf", [P, NBLK])
        tok = sb("tok", [P, NT], I32)
        tri, one = sb("tri", [P, P]), sb("one", [P, P])
        gm, gs, gate = (sb(n, [P, NT]) for n in ("gm", "gs", "gate"))
        gd, ohg, gt = (sb(n, [P, NT, NGR]) for n in ("gd", "ohg", "gt"))
        fm = sb("fm", [P, NT])
        full = sb("full", [P, NT, NGR, EPG])
        ein, e2, ohk, et = sb("ein", [P, NT, EPG]), sb("e2", [P, NT, EPG]), [sb(f"ohk{k}", [P, NT, EPG]) for k in range(2)], sb("et", [P, NT, EPG])
        v12 = [sb(f"v{k}", [P, NT]) for k in range(2)]
        dv, p1 = sb("dv", [P, NT]), sb("p1", [P, NT])
        OH = [sb(f"OH{k}", [P, NT, NGR, EPG]) for k in range(2)]
        oh = sb("OHs", [P, NT, NE])
        tot = sb("tot", [P, NT, NE])
        pre = sb("pre", [P, NT + 1, NE])
        rank = sb("rank", [P, NT, NE])
        nb, cum, st0 = (sb(n, [P, NE]) for n in ("nb", "cum", "st0"))
        cmp_ = sb("cmp", [P, NBLK, NE])
        be, nr, rn, par = (sb(n, [P, NBLK]) for n in ("be", "nr", "rn", "par"))
        hf, hu, e1 = (sb(n, [P, NBLK]) for n in ("hf", "hu", "e1"))
        cr = sb("cr", [P, NE, NBLK])
        npf, np2, nrk = (sb(n, [P, 1]) for n in ("npf", "np2", "nrk"))
        dest_f = sb("dest_f", [P, NT])
        zi = sb("zi", [P, NBLK + 1], I32)
        ps = [c.ps(f"ps_rank{n}", [P, 512]) for n in range(2)]
        io, tri0 = c.sem("r_iota"), c.sem("r_tri0")
        st_, ex, exd, mm = c.sem("r_step"), c.sem("r_exp_in"), c.sem("r_exp"), c.sem("rank_mm")
        ohd, z_st, sc, ready, tb = c.sem("r_oh"), c.sem("r_zero_st"), c.sem("r_scatter"), c.sem("r_dest"), c.sem("r_table")
        zd = c.sem("r_zero")
        rows = S["row_tok"]

        with nc.Block() as block:
            @block.gpsimd
            def _(pool):
                nc.gpsimd.iota(w8i[:, :], [[-1, EPG]], base=EPG, channel_multiplier=0).then_inc(io, 1)
                nc.gpsimd.iota(bi[:, :], [[1, NBLK]], base=0, channel_multiplier=0).then_inc(io, 1)
                nc.gpsimd.iota(tok[:, :], [[P, NT]], base=0, channel_multiplier=1).then_inc(io, 1)
                nc.gpsimd.memset(one[:, :], 1.0).then_inc(io, 1)
                nc.gpsimd.memset(tri[:, :], 1.0).then_inc(tri0, 1)
                pool.wait_ge(tri0, 1)
                nc.gpsimd.affine_select(out=tri[:, :], in_=tri[:, :], compare_op=ALU.is_gt, fill=0.0, base=0,
                                        pattern=[[1, P]], channel_multiplier=-1).then_inc(io, 1)
                pool.wait_ge(io, 5)
                pool.wait_ge(z_st, 16)
                pool.wait_ge(ready, 2)
                for k in range(2):
                    for t in range(NT):
                        pool.indirect_dma_start(rows, bass.IndirectOffsetOnAxis(g["dest"][:, k, t:t + 1], 0),
                                                tok[:, t:t + 1], None).then_inc(sc, 16)
                pool.wait_ge(sc, 16 * 2 * NT)

            @block.sync
            def _(sp):
                sp.wait_ge(zd, 1)
                sp.dma_start(rows.rearrange("(b p) a -> p (b a)", p=P), zi[:, :],
                             allow_slow_non_contiguous=True).then_inc(z_st, 16)
                sp.wait_ge(sc, 16 * 2 * NT)
                sp.dma_start(g["rowtok"][:, :], rows.rearrange("(b p) a -> p (b a)", p=P),
                             allow_slow_non_contiguous=True).then_inc(tb, 16)
                sp.wait_ge(tb, 16)

            @block.scalar
            def _(act):
                act.wait_ge(ex, 1)
                nc.scalar.activation(gd[:, :, :], gd[:, :, :], ACT.Exp).then_inc(exd, 1)
                act.wait_ge(ex, 2)
                nc.scalar.activation(dv[:, :], dv[:, :], ACT.Exp).then_inc(exd, 1)

            @block.tensor
            def _(pe):
                pe.wait_ge(io, 5)
                pe.wait_ge(ohd, 1)
                f = oh[:, :, :].rearrange("p t e -> p (t e)")
                nc.tensor.matmul(ps[0][:, :], tri[:, :], f, start=True, stop=True).then_inc(mm, 1)
                nc.tensor.matmul(ps[1][:, :], one[:, :], f, start=True, stop=True).then_inc(mm, 1)

            @block.vector
            def _(v):
                n_ = [0]

                def did(ins):
                    n_[0] += 1
                    ins.then_inc(st_, 1)
                    v.wait_ge(st_, n_[0])

                def tt(o, a, b, op):
                    did(v.tensor_tensor(o, a, b, op))

                def ts(o, a, s1, s2, op0, op1=None):
                    did(v.tensor_scalar(o, a, s1, s2, op0, op1) if op1 is not None else v.tensor_scalar(o, a, s1, None, op0))

                def floor(o, a, scale, off):
                    big = 1.5 * 2 ** 23
                    ts(o, a, scale, off, ALU.mult, ALU.add)
                    ts(o, o, big, None, ALU.add)
                    ts(o, o, big, None, ALU.subtract)

                def first_max(o, vals, top, tmp, k):
                    w = w8[:, EPG - k:].unsqueeze(1).to_broadcast([P, NT, k])
                    did(v.tensor_reduce(top, vals, AX_X, ALU.max))
                    tt(tmp, vals, top.unsqueeze(2).to_broadcast([P, NT, k]), ALU.is_equal)
                    tt(tmp, tmp, w, ALU.mult)
                    did(v.tensor_reduce(fm[:, :], tmp, AX_X, ALU.max))
                    tt(o, w, fm[:, :].unsqueeze(2).to_broadcast([P, NT, k]), ALU.is_equal)

                v.memset(zi[:, :], 0).then_inc(zd, 1)
                v.wait_ge(io, 5)
                did(v.tensor_copy(w8[:, :], w8i[:, :]))
                did(v.tensor_copy(bf[:, :], bi[:, :]))
                gl, el = lg[:, :, 0:NGR], lg[:, :, NGR:].rearrange("p t (a b) -> p t a b", b=EPG)
                first_max(ohg[:, :, :], gl, gm[:, :], gt[:, :, :], NGR)
                v.tensor_tensor(gd[:, :, :], gl, gm[:, :].unsqueeze(2).to_broadcast([P, NT, NGR]), ALU.subtract).then_inc(ex, 1)
                tt(full[:, :, :, :], el, ohg[:, :, :].unsqueeze(3).to_broadcast([P, NT, NGR, EPG]), ALU.mult)
                tt(ein[:, :, :], full[:, :, 0, :], full[:, :, 1, :], ALU.add)
                tt(et[:, :, :], full[:, :, 2, :], full[:, :, 3, :], ALU.add)
                tt(ein[:, :, :], ein[:, :, :], et[:, :, :], ALU.add)
                first_max(ohk[0][:, :, :], ein[:, :, :], v12[0][:, :], et[:, :, :], EPG)
                did(v.scalar_tensor_tensor(out=e2[:, :, :], in0=ohk[0][:, :, :], scalar=-3e38, in1=ein[:, :, :],
                                           op0=ALU.mult, op1=ALU.add))
                first_max(ohk[1][:, :, :], e2[:, :, :], v12[1][:, :], et[:, :, :], EPG)
                for k in range(2):
                    tt(OH[k][:, :, :, :], ohg[:, :, :].unsqueeze(3).to_broadcast([P, NT, NGR, EPG]),
                       ohk[k][:, :, :].unsqueeze(2).to_broadcast([P, NT, NGR, EPG]), ALU.mult)
                flat = [x[:, :, :, :].rearrange("p t a b -> p t (a b)") for x in OH]
                tt(oh[:, :, :], flat[0], flat[1], ALU.add)
                v.engine_nop().then_inc(ohd, 1)
                tt(dv[:, :], v12[1][:, :], v12[0][:, :], ALU.subtract)
                v.engine_nop().then_inc(ex, 1)
                v.wait_ge(exd, 1)
                did(v.tensor_reduce(gs[:, :], gd[:, :, :], AX_X, ALU.add))
                did(v.reciprocal(gate[:, :], gs[:, :]))
                v.wait_ge(exd, 2)
                ts(p1[:, :], dv[:, :], 1.0, None, ALU.add)
                did(v.reciprocal(p1[:, :], p1[:, :]))
                tt(g["wgt"][:, 0, :], p1[:, :], gate[:, :], ALU.mult)
                tt(g["wgt"][:, 1, :], g["wgt"][:, 0, :], dv[:, :], ALU.mult)
                v.wait_ge(mm, 2)
                did(v.tensor_copy(tot[:, :, :].rearrange("p t e -> p (t e)"), ps[1][:, :]))
                did(v.memset(pre[:, 0, :], 0.0))
                for t in range(NT):
                    tt(pre[:, t + 1, :], pre[:, t, :], tot[:, t, :], ALU.add)
                tt(rank[:, :, :].rearrange("p t e -> p (t e)"), ps[0][:, :], pre[:, 0:NT, :].rearrange("p t e -> p (t e)"), ALU.add)
                floor(nb[:, :], pre[:, NT, :], 1.0 / P, (P - 1) / P - 0.5 + 0.5 / P)
                did(v.tensor_tensor_scan(cum[:, :], one[:, 0:NE], nb[:, :], 0.0, ALU.mult, ALU.add))
                tt(st0[:, :], cum[:, :], nb[:, :], ALU.subtract)
                ts(st0[:, :], st0[:, :], float(P), None, ALU.mult)
                tt(rank[:, :, :], rank[:, :, :], st0[:, :].unsqueeze(1).to_broadcast([P, NT, NE]), ALU.add)
                for k in range(2):
                    tt(tot[:, :, :], flat[k], rank[:, :, :], ALU.mult)
                    did(v.tensor_reduce(dest_f[:, :], tot[:, :, :], AX_X, ALU.add))
                    v.tensor_copy(g["dest"][:, k, :], dest_f[:, :]).then_inc(ready, 1)
                    v.wait_ge(ready, k + 1)
                tt(cmp_[:, :, :], cum[:, :].unsqueeze(1).to_broadcast([P, NBLK, NE]),
                   bf[:, :].unsqueeze(2).to_broadcast([P, NBLK, NE]), ALU.is_le)
                did(v.tensor_reduce(be[:, :], cmp_[:, :, :], AX_X, ALU.add))
                ts(be[:, :], be[:, :], float(NE - 1), None, ALU.min)
                did(v.memset(nr[:, 0:1], 1.0))
                tt(nr[:, 1:], be[:, 1:], be[:, 0:NBLK - 1], ALU.not_equal)
                did(v.tensor_tensor_scan(rn[:, :], one[:, 0:NBLK], nr[:, :], 0.0, ALU.mult, ALU.add))
                floor(hf[:, :], rn[:, :], 0.5, -0.25)
                did(v.scalar_tensor_tensor(out=par[:, :], in0=hf[:, :], scalar=-2.0, in1=rn[:, :], op0=ALU.mult, op1=ALU.add))
                floor(npf[:, :], cum[:, NE - 1:NE], 0.5, 0.25)
                blk = g["blk"]

                def row(r, src):
                    did(v.tensor_copy(blk[0:1, r, 0:src.shape[1]], src[0:1, :]))

                def scaled(r, src, k, off):
                    ts(e1[:, :], src, k, off, ALU.mult, ALU.add)
                    row(r, e1[:, :])

                tt(hu[:, :], hf[:, :], par[:, :], ALU.add)
                row(OTHER, par[:, :])
                scaled(SIDE, par[:, :], -1.0, 1.0)
                scaled(N_SPLIT, rn[:, :], float(PIECES), 1.0 - PIECES)
                scaled(W2_A, hu[:, :], 16.0, 0.0)
                scaled(W2_B, hf[:, :], 16.0, 1.0)
                scaled(NEXT_A, hf[:, :], 32.0, 32.0)
                scaled(NEXT_B, hu[:, :], 32.0, 0.0)
                ts(np2[:, :], npf[:, :], 2.0, None, ALU.mult)
                tt(e1[:, :], bf[:, :], np2[:, :].to_broadcast([P, NBLK]), ALU.is_lt)
                tt(e1[:, :], e1[:, :], rn[:, :], ALU.mult)
                did(v.tensor_reduce(nrk[:, :], e1[:, :], AX_X, ALU.max))
                tt(e1[:, :], rn[:, :], nrk[:, :].to_broadcast([P, NBLK]), ALU.is_lt)
                tt(e1[:, :], e1[:, :], nr[:, :], ALU.mult)
                row(JOB, e1[:, :])
                ts(e1[:, :], rn[:, :], -1.0, None, ALU.add)
                of = [e1[:, :].unsqueeze(1).to_broadcast([P, NE, NBLK]), bf[:, 0:NE].unsqueeze(2).to_broadcast([P, NE, NBLK])]
                tt(cr[:, :, :], of[0], of[1], ALU.is_equal)
                tt(cr[:, :, :], cr[:, :, :], be[:, :].unsqueeze(1).to_broadcast([P, NE, NBLK]), ALU.mult)
                did(v.tensor_reduce(st0[:, :], cr[:, :, :], AX_X, ALU.max))
                row(R_EXPERT, st0[:, :])
                tt(cr[:, :, :], of[0], of[1], ALU.is_lt)
                did(v.tensor_reduce(st0[:, :], cr[:, :, :], AX_X, ALU.add))
                row(R_START, st0[:, :])
                row(META, npf[:, :])
                ts(npf[:, :], npf[:, :], -1.0, NBLK / 2, ALU.mult, ALU.add)
                did(v.tensor_copy(blk[0:1, META, 1:2], npf[0:1, :]))
                floor(nrk[:, :], nrk[:, :], 0.5, 0.25)
                did(v.tensor_copy(blk[0:1, META, 2:3], nrk[0:1, :]))


def stage_experts(nc, g, A, S):
    with Ctx(nc) as c:
        lo13, hi13 = (c.sb(f"w13_{n}", [P, 2, 2, KD, DE], FR) for n in ("lo", "hi"))
        w2 = c.sb("w2_sb", [P, 2, KE, D])
        idx = [c.sb(f"idx{b}", [P, 1], I32) for b in range(2)]
        tick, tick0 = c.sb("tick_x", [P, 1]), c.sem("tick_x0")
        xg = [c.sb(f"xg{b}", [P, D]) for b in range(2)]
        xf = c.sb("xgT_exact", [P, KD, P])
        xh, xl = (c.sb(f"xgT_{n}", [P, KD, P], FR) for n in ("hi", "lo"))
        ac = c.sb("act", [P, DE])
        aT = c.sb("actT", [P, KE, P])
        yo = [c.sb(f"yo{b}", [P, D]) for b in range(2)]
        zero = c.sb("zero_rows", [P, P])
        psT = [c.ps(f"ps_xT{h}", [P, 4, P]) for h in range(2)]
        psA = c.ps("ps_aT", [P, KE, P])
        psG, psU = c.ps("ps_g", [P, 512]), c.ps("ps_u", [P, 512])
        psY = c.ps("ps_y", [P, 2, 512])
        w13_in, w2_in = ([c.sem(f"{n}_in{b}") for b in range(2)] for n in ("w13", "w2"))
        hi_d, lo_d = c.sem("w13_hi_done"), c.sem("w13_lo_done")
        x_in = [c.sem(f"xg_in{b}") for b in range(2)]
        ix, x_tp, xf_d = c.sem("idx_done"), c.sem("xg_tp"), [c.sem(f"xgT_done{h}") for h in range(2)]
        xh_d, xl_d = c.sem("xh_done"), c.sem("xl_done")
        g_mm, u_mm, si_d, ac_d = c.sem("g_mm"), c.sem("u_mm"), c.sem("silu_done"), c.sem("act_done")
        a_tp, a_T, y_mm, y_d = c.sem("a_tp2"), c.sem("a_T2"), c.sem("y_mm"), c.sem("yo_done")
        y_st = [c.sem(f"yo_st{b}") for b in range(2)]
        pad_st = c.sem("pad_st")
        blk = g["blk"]
        yb = S["yb"].rearrange("(t p) n -> t p n", p=P)

        NPAIR = T // P

        def meta(eng, n, least, most):
            return eng.value_load(blk[0:1, META, n:n + 1], min_val=least, max_val=most)

        def entry(eng, r, n, least, most):
            return eng.value_load(blk[0:1, r, ds(n, 1)], min_val=least, max_val=most)

        def past(n, k):
            return not isinstance(n, int) or n >= k

        def pairs(eng, body):
            n_pairs = meta(eng, 0, NPAIR, NBLK // 2)
            for b in range(2):
                body(b, 0, b)
            with eng.Fori(1, n_pairs) as i:
                for b in range(2):
                    body(2 * i + b, i, b)
            return n_pairs

        def piece(w, side, j):
            k = KD * 2 // PIECES
            return w[:, ds(side, 1), j * 2 // PIECES, (j % (PIECES // 2)) * k:(j % (PIECES // 2) + 1) * k, :].rearrange(
                "p a k n -> p (a k) n")

        with nc.Block() as block:
            @block.sync
            def _(sp):
                n_rank_pairs, n_pairs = meta(sp, 2, 1, NE // 2), meta(sp, 0, NPAIR, NBLK // 2)

                def weights(r, b):
                    e = entry(sp, R_EXPERT, r, 0, NE - 1)
                    if past(r, 2):
                        start = entry(sp, R_START, r - 1, 1, NBLK)
                        sp.wait_ge(u_mm, start)
                    for m, name in enumerate(("w1", "w3")):
                        src = A[name][0].rearrange("e (k p) n -> e p k n", p=P)[ds(e, 1)].rearrange("a p k n -> (a p) k n")
                        sp.dma_start(lo13[:, b, m, :, :].bitcast(F32), src).then_inc(w13_in[b], 16)
                    if past(r, 2):
                        sp.wait_ge(y_mm, start)
                    src = A["w2"][0].rearrange("e (k p) n -> e p k n", p=P)[ds(e, 1)].rearrange("a p k n -> (a p) k n")
                    sp.dma_start(w2[:, b, :, :], src).then_inc(w2_in[b], 16)

                for b in range(2):
                    weights(b, b)
                sp.wait_ge(pad_st, 16)
                with sp.If(n_pairs < NBLK // 2):
                    with sp.Fori(n_pairs, NBLK // 2) as i:
                        for b in range(2):
                            sp.dma_start(yb[ds(2 * i + b, 1)].rearrange("a p (m n) -> (a p) m n", n=P),
                                         zero[:, :].unsqueeze(1).to_broadcast([P, D // P, P])).then_inc(pad_st, 16)
                with sp.If(n_rank_pairs > 1):
                    with sp.Fori(1, n_rank_pairs) as i:
                        for b in range(2):
                            weights(2 * i + b, b)

            @block.gpsimd
            def _(pool):
                nc.gpsimd.memset(tick[:, :], 0.0).then_inc(tick0, 1)
                pool.wait_ge(tick0, 1)

                def gather(n, b):
                    nc.gpsimd.tensor_copy(idx[b][:, :], g["rowtok"][:, ds(n, 1)]).then_inc(ix, 1)
                    pool.wait_ge(ix, n + 1)
                    nc.gpsimd.tensor_tensor(tick[:, :], tick[:, :], tick[:, :], ALU.add)
                    pool.indirect_dma_start(xg[b][:, :], None, S["xn2"],
                                            bass.IndirectOffsetOnAxis(idx[b][:, 0:1], 0)).then_inc(x_in[b], 16)

                def body(n, i, b):
                    if past(n, 1):
                        pool.wait_ge(x_tp, 2 * n)
                    gather(n + 1, 1 - b)

                gather(0, 0)
                pairs(pool, body)

            @block.tensor
            def _(pe):
                n_empty, n_rank_pairs = meta(pe, 1, 0, NBLK // 2), meta(pe, 2, 1, NE // 2)

                def turn(n, b, i):
                    pe.wait_ge(x_in[b], 16 * i + 16)
                    for h in range(2):
                        if past(n, 1):
                            pe.wait_ge(xf_d[h], n)
                        for k in range(4):
                            mm = nc.tensor.transpose(psT[h][:, k, :], xg[b][:, (4 * h + k) * P:(4 * h + k + 1) * P], g["ident"][:, :])
                        mm.then_inc(x_tp, 1)

                def body(n, i, b):
                    side = entry(pe, SIDE, n, 0, 1)
                    n_split = entry(pe, N_SPLIT, n, 1, PIECES * NE)
                    w2_a, w2_b = entry(pe, W2_A, n, 16, 16 * NE), entry(pe, W2_B, n, 1, 16 * NE + 1)
                    pe.wait_ge(xl_d, n + 1)
                    for m, (o, s) in enumerate(((psG, g_mm), (psU, u_mm))):
                        if past(n, 1):
                            pe.wait_ge(ac_d, n)
                        for k in range(KD):
                            if k % (KD * 2 // PIECES) == 0:
                                j = (m * KD + k) * PIECES // (2 * KD)
                                pe.wait_ge(lo_d, n_split + j if j else n_split)
                            for q, (xp, wp) in enumerate(((xh, hi13), (xl, hi13), (xh, lo13))):
                                mm = nc.tensor.matmul(o[:, :], xp[:, k, :],
                                                      wp[:, ds(side, 1), m, k, :].rearrange("p a n -> p (a n)"),
                                                      start=k == 0 and q == 0, stop=k == KD - 1 and q == 2)
                        mm.then_inc(s, 1)
                    turn(n + 1, 1 - b, i + b)
                    pe.wait_ge(ac_d, n + 1)
                    if past(n, 1):
                        pe.wait_ge(a_T, n)
                    for k in range(KE):
                        mm = nc.tensor.transpose(psA[:, k, :], ac[:, k * P:(k + 1) * P], g["ident"][:, :])
                    mm.then_inc(a_tp, 1)
                    pe.wait_ge(a_T, n + 1)
                    if past(n, 1):
                        pe.wait_ge(y_d, n)
                    pe.wait_ge(w2_in[0], w2_a)
                    pe.wait_ge(w2_in[1], w2_b)
                    for h in range(2):
                        for k in range(KE):
                            mm = nc.tensor.matmul(psY[:, h, :], aT[:, k, :],
                                                  w2[:, ds(side, 1), k, 512 * h:512 * h + 512].rearrange("p a n -> p (a n)"),
                                                  start=k == 0, stop=k == KE - 1)
                    mm.then_inc(y_mm, 1)

                turn(0, 0, 0)
                n_pairs = pairs(pe, body)
                for b in range(2):
                    pe.wait_ge(x_in[b], 16 * n_pairs + 16 * (1 - b))
                    pe.wait_ge(y_st[b], 16 * n_pairs)
                    pe.wait_ge(w13_in[b], 32 * n_rank_pairs)
                    pe.wait_ge(w2_in[b], 16 * n_rank_pairs + b)
                pe.wait_ge(pad_st, 32 * n_empty + 16)

            def leave(eng, op, h, n):
                eng.wait_ge(x_tp, 2 * n + h + 1)
                if past(n, 1):
                    eng.wait_ge(xl_d, n)
                for k in range(4 * h, 4 * h + 4):
                    e = op(xf[:, k, :], psT[h][:, k % 4, :], g["acol"][:, 1, k:k + 1], g["bcol"][:, 1, k:k + 1])
                e.then_inc(xf_d[h], 1)

            @block.scalar
            def _(act):
                def rows_hi(n):
                    leave(act, lambda o, a, s, t: nc.scalar.activation(o, a, ACT.Identity, bias=t, scale=s), 0, n)
                    for h in range(2):
                        act.wait_ge(xf_d[h], n + 1)
                    if past(n, 1):
                        act.wait_ge(u_mm, n)
                    nc.scalar.activation(xh[:, :, :], xf[:, :, :], ACT.Copy).then_inc(xh_d, 1)

                def split_hi(side):
                    for j in range(PIECES):
                        nc.scalar.activation(piece(hi13, side, j), piece(lo13, side, j).bitcast(F32), ACT.Copy).then_inc(hi_d, 1)

                def body(n, i, b):
                    job, other = entry(act, JOB, n, 0, 1), entry(act, OTHER, n, 0, 1)
                    next_a, next_b = (entry(act, r, n, 32, 32 * NE) for r in (NEXT_A, NEXT_B))
                    act.wait_ge(g_mm, n + 1)
                    if past(n, 1):
                        act.wait_ge(a_tp, n)
                    nc.scalar.activation(ac[:, :], psG[:, :], ACT.Silu).then_inc(si_d, 1)
                    rows_hi(n + 1)
                    with act.If(job > 0):
                        act.wait_ge(w13_in[0], next_a)
                        act.wait_ge(w13_in[1], next_b)
                        split_hi(other)
                    act.wait_ge(y_mm, n + 1)
                    if past(n, 2):
                        act.wait_ge(y_st[b], 16 * i)
                    nc.scalar.activation(yo[b][:, :], psY[:, :, :].rearrange("p a n -> p (a n)"), ACT.Copy).then_inc(y_d, 1)
                    act.wait_ge(y_d, n + 1)
                    act.dma_start(yb[ds(n, 1)].rearrange("a p n -> (a p) n"), yo[b][:, :]).then_inc(y_st[b], 16)

                act.wait_ge(w13_in[0], 32)
                split_hi(0)
                rows_hi(0)
                pairs(act, body)

            @block.vector
            def _(v):
                def rows_lo(n):
                    v.wait_ge(xh_d, n + 1)
                    v.tensor_tensor(xl[:, :, :], xf[:, :, :], xh[:, :, :], ALU.subtract).then_inc(xl_d, 1)

                def affine(o, a, s, t):
                    return v.tensor_scalar(o, a, s, t, ALU.mult, ALU.add)

                def split_lo(side, n_hi):
                    for j in range(PIECES):
                        v.wait_ge(hi_d, n_hi + j + 1)
                        v.tensor_tensor(piece(lo13, side, j), piece(lo13, side, j).bitcast(F32), piece(hi13, side, j),
                                        ALU.subtract).then_inc(lo_d, 1)

                def body(n, i, b):
                    job, other = entry(v, JOB, n, 0, 1), entry(v, OTHER, n, 0, 1)
                    n_hi = entry(v, N_SPLIT, n, 1, PIECES * NE)
                    v.wait_ge(si_d, n + 1)
                    v.wait_ge(u_mm, n + 1)
                    v.tensor_tensor(ac[:, :], ac[:, :], psU[:, :], ALU.mult).then_inc(ac_d, 1)
                    leave(v, affine, 1, n + 1)
                    v.wait_ge(a_tp, n + 1)
                    if past(n, 1):
                        v.wait_ge(y_mm, n)
                    v.tensor_copy(aT[:, :, :], psA[:, :, :]).then_inc(a_T, 1)
                    rows_lo(n + 1)
                    with v.If(job > 0):
                        split_lo(other, n_hi + PIECES - 1)

                v.memset(zero[:, :], 0.0).then_inc(pad_st, 16)
                v.engine_nop().then_inc(w2_in[1], 1)
                leave(v, affine, 1, 0)
                rows_lo(0)
                split_lo(0, 0)
                pairs(v, body)


def stage_output(nc, g, A, S, out):
    with Ctx(nc) as c:
        idx = [[c.sb(f"di{b}{k}", [P, 1], I32) for k in range(2)] for b in range(2)]
        yr = [[c.sb(f"yr{b}{k}", [P, D]) for k in range(2)] for b in range(2)]
        x1 = [c.sb(f"x1o{b}", [P, D]) for b in range(2)]
        y = [c.sb(f"ysum{b}", [P, D]) for b in range(2)]
        ob = [c.sb(f"ob{b}", [P, D]) for b in range(2)]
        junk = [c.sb(f"junk_o{b}", [P, D]) for b in range(2)]
        ssq, ms, rt, rstd = ([c.sb(f"{n}{b}", [P, 1]) for b in range(2)] for n in ("o_ss", "o_ms", "o_rt", "o_rstd"))
        ix = c.sem("di_done")
        tick, tick0 = c.sb("tick_o", [P, 1]), c.sem("tick_o0")
        y_in = [c.sem(f"yr_in{b}") for b in range(2)]
        x_in = [c.sem(f"x1o_in{b}") for b in range(2)]
        ys, y_d, sq, ms_d, rt_d, os_, o_d = (c.sem(n) for n in ("y_scaled", "y_sum", "o_sq", "o_ms_d", "o_rt_d", "o_step", "o_done"))
        o_st = [c.sem(f"out_st{b}") for b in range(2)]

        def tile(dram, t):
            return dram.rearrange("(t p) n -> t p n", p=P)[ds(t, 1)].rearrange("a p n -> (a p) n")

        with nc.Block() as block:
            @block.gpsimd
            def _(pool):
                nc.gpsimd.memset(tick[:, :], 0.0).then_inc(tick0, 1)
                pool.wait_ge(tick0, 1)

                def pair(i):
                    for b in range(2):
                        t = 2 * i + b
                        for k in range(2):
                            if not isinstance(i, int) and k == 0:
                                pool.wait_ge(y_d, t - 1)
                            nc.gpsimd.tensor_copy(idx[b][k][:, :], g["dest"][:, k, ds(t, 1)]).then_inc(ix, 1)
                            pool.wait_ge(ix, 2 * t + k + 1)
                            nc.gpsimd.tensor_tensor(tick[:, :], tick[:, :], tick[:, :], ALU.add)
                            pool.indirect_dma_start(yr[b][k][:, :], None, S["yb"],
                                                    bass.IndirectOffsetOnAxis(idx[b][k][:, 0:1], 0)).then_inc(y_in[b], 16)

                pair(0)
                with pool.Fori(1, NT // 2) as i:
                    pair(i)

            @block.sync
            def _(sp):
                for b in range(2):
                    sp.dma_start(x1[b][:, :], tile(S["x1"], b)).then_inc(x_in[b], 16)

                def store(t, b):
                    sp.wait_ge(o_d, t + 1)
                    sp.dma_start(tile(out[0], t), ob[b][:, :]).then_inc(o_st[b], 16)
                with sp.Fori(0, NT // 2 - 1) as i:
                    for b in range(2):
                        store(2 * i + b, b)
                        sp.dma_start(x1[b][:, :], tile(S["x1"], 2 * i + b + 2)).then_inc(x_in[b], 16)
                for b in range(2):
                    store(NT - 2 + b, b)
                for b in range(2):
                    sp.wait_ge(o_st[b], 16 * NT // 2)

            @block.scalar
            def _(act):
                with act.Fori(0, NT // 2) as i:
                    for b in range(2):
                        t = 2 * i + b
                        act.wait_ge(y_d, t + 1)
                        nc.scalar.activation(junk[b][:, :], y[b][:, :], ACT.Square, accum_out=ssq[b][:, :]).then_inc(sq, 1)
                        act.wait_ge(ms_d, t + 1)
                        nc.scalar.activation(rt[b][:, :], ms[b][:, :], ACT.Sqrt).then_inc(rt_d, 1)

            @block.vector
            def _(v):
                def head(t, i, b):
                    v.wait_ge(y_in[b], 32 * i + 32)
                    v.tensor_scalar(y[b][:, :], yr[b][0][:, :], g["wgt"][:, 0, ds(t, 1)], None, ALU.mult).then_inc(ys, 1)
                    v.wait_ge(ys, t + 1)
                    v.scalar_tensor_tensor(out=y[b][:, :], in0=yr[b][1][:, :], scalar=g["wgt"][:, 1, ds(t, 1)], in1=y[b][:, :],
                                           op0=ALU.mult, op1=ALU.add).then_inc(y_d, 1)

                def tail(t, i, b):
                    v.wait_ge(sq, t + 1)
                    v.tensor_scalar(ms[b][:, :], ssq[b][:, :], 1.0 / D, EPS, ALU.mult, ALU.add).then_inc(ms_d, 1)
                    v.wait_ge(rt_d, t + 1)
                    v.reciprocal(rstd[b][:, :], rt[b][:, :]).then_inc(os_, 1)
                    v.wait_ge(os_, 2 * t + 1)
                    if not (isinstance(t, int) and t < 2):
                        v.wait_ge(o_st[b], 16 * i)
                    v.scalar_tensor_tensor(out=ob[b][:, :], in0=y[b][:, :], scalar=rstd[b][:, 0:1], in1=g["grow"][:, 1, :],
                                           op0=ALU.mult, op1=ALU.mult).then_inc(os_, 1)
                    v.wait_ge(os_, 2 * t + 2)
                    v.wait_ge(x_in[b], 16 * i + 16)
                    v.tensor_tensor(ob[b][:, :], ob[b][:, :], x1[b][:, :], ALU.add).then_inc(o_d, 1)

                head(0, 0, 0)
                head(1, 0, 1)
                tail(0, 0, 0)
                head(2, 1, 0)
                tail(1, 0, 1)
                with v.Fori(1, NT // 2 - 1) as i:
                    head(2 * i + 1, i, 1)
                    tail(2 * i, i, 0)
                    head(2 * i + 2, i + 1, 0)
                    tail(2 * i + 1, i, 1)
                i = NT // 2 - 1
                head(NT - 1, i, 1)
                tail(NT - 2, i, 0)
                tail(NT - 1, i, 1)


def program(nc, A, out, scratch_kind="Internal"):
    def dram(name, shape, dt=F32):
        return nc.dram_tensor(name, shape, dt, kind=scratch_kind).ap()

    S = {
        "qkvu": dram("s_qkvu", (T, QKVU)),
        "gates": dram("s_gates", (T, 2 * D)),
        "rec": dram("s_rec", (NG_S, P, REC)),
        "kpad": dram("s_kpad", (NG_S, CH_S, 512)),
        "row_tok": dram("s_row_tok", (CAP + P, 1), I32),
        "rot": dram("s_rot", (2, P, NG_S, NC)),
        "rho": dram("s_rho", (P, NG_S)),
        "yb": dram("s_yb", (CAP, D)),
        "x1": dram("s_x1", (T, D)),
        "xn2": dram("s_xn2", (T, D)),
        "y": dram("s_y", (T, SW)),
        "bias_rows": dram("s_bias_rows", (NH, len(DILS), 3 * P - 1)),
        "bias_copies": dram("s_bias_copies", (P, NH * len(DILS) * (3 * P - 1))),
        "o": [dram(f"s_o{p}", (T, AW + 2 * NH)) for p in range(len(DILS))],
    }
    with Ctx(nc) as c:
        g = {
            "ident": c.sb("ident", [P, P]),
            "acol": c.sb("acol", [P, 2, KD]),
            "bcol": c.sb("bcol", [P, 2, KD]),
            "grow": c.sb("grow", [P, 2, D]),
            "rstd": c.sb("rstd", [P, NT]),
            "dest": c.sb("dest", [P, 2, NT], I32),
            "wgt": c.sb("wgt", [P, 2, NT]),
            "rowtok": c.sb("rowtok", [P, NBLK + 1], I32),
            "blk": c.sb("blk", [1, META + 1, NBLK], I32),
        }
        stage_modulation(nc, g, A, S)
        stage_projection(nc, g, A, S)
        with Ctx(nc) as ca:
            ga = {**g, "bias": ca.sb("bias", [P, len(DILS), NH, 2 * P]), "bias_in": ca.sem("bias_in")}
            stage_ssm(nc, ga, A, S)
            stage_attention(nc, ga, A, S)
        with Ctx(nc) as cr:
            gr = {**g, "logits": cr.sb("logits", [P, NT, NR])}
            stage_merge(nc, gr, A, S)
            stage_route(nc, gr, A, S)
        stage_experts(nc, g, A, S)
        stage_output(nc, g, A, S, out)


_INS = ['x', 'c', 'w_mod', 'b_mod', 'g_pre_mix', 'g_post_mix', 'g_pre_ffn', 'g_post_ffn', 'w_in', 'rel_bias', 'a_re', 'a_im', 'log_dt', 'ssm_b_re', 'ssm_b_im', 'ssm_c_re', 'ssm_c_im', 'd_skip', 'w_glu', 'b_glu', 'w_branch_attn', 'w_branch_ssm', 'w_out', 'w_router_group', 'b_router_group', 'w_router_expert', 'b_router_expert', 'w1', 'w3', 'w2']


def kernel(**inputs):
    import numpy as _np
    import concourse.bacc as _bacc
    from concourse import mybir as _mybir
    from concourse.bass_utils import run_bass_kernel_spmd as _run

    nc = _bacc.Bacc("TRN2", target_bir_lowering=False, num_devices=1)
    given = {name: _np.ascontiguousarray(inputs[name]) for name in _INS}
    given["bucket_hot"] = bucket_one_hot()
    arrays, A = {}, {}
    for name, a in given.items():
        arrays[f"in_{name}_dram"] = a
        A[name] = nc.dram_tensor(f"in_{name}_dram", a.shape, _mybir.dt.from_np(a.dtype), kind="ExternalInput").ap()
    out = nc.dram_tensor("out_0_dram", (1, T, D), _mybir.dt.float32, kind="ExternalOutput").ap()
    program(nc, A, out)
    r = _run(nc, [arrays], core_ids=[0])
    return r.results[0]["out_0_dram"]
```
